# Optimizing a Trainium2 kernel written in Bass

```python
import jax, jax.numpy as jnp
from jax import lax
import numpy as np
import math

D_MODEL = 1024
BATCH = 1
SEQ = 512
DEPTH = 1

NSA_HEADS = 8
NSA_KV_GROUPS = 2
NSA_HEAD_DIM = 64
CMP_LEN = 32
CMP_STRIDE = 16
CMP_HIDDEN = 256
SEL_BLOCK = 64
SEL_TOPK = 16
WINDOW = 512
MLA_HEADS = 8
MLA_NOPE = 64
MLA_ROPE = 32
MLA_V = 64
MLA_Q_RANK = 384
MLA_KV_RANK = 256
ROPE_THETA = 10000.0
D_FF = 4 * D_MODEL
Q_BLOCK = 128
EPS = 1e-6
FORCE_BONUS = 1000.0

NSA_HG = NSA_HEADS // NSA_KV_GROUPS
NSA_Q_DIM = NSA_HEADS * NSA_HEAD_DIM
NSA_KV_DIM = NSA_KV_GROUPS * NSA_HEAD_DIM
IN_SPLITS = (NSA_Q_DIM, NSA_KV_DIM, NSA_KV_DIM, NSA_KV_DIM, NSA_KV_DIM, NSA_KV_DIM, NSA_KV_DIM,
             3 * NSA_HEADS, MLA_Q_RANK, MLA_KV_RANK, MLA_ROPE, D_MODEL, D_MODEL)
IN_DIM = sum(IN_SPLITS)


def rmsnorm(x, g):
    xf = x.astype(jnp.float32)
    y = xf * lax.rsqrt(jnp.mean(xf * xf, axis=-1, keepdims=True) + EPS)
    return (y * g.astype(jnp.float32)).astype(x.dtype)

def modulate(h, shift, scale):
    return h * (1.0 + scale[:, None, :]) + shift[:, None, :]

def masked_softmax(s, mask):
    s = jnp.where(mask, s, -jnp.inf)
    m = jnp.max(s, axis=-1, keepdims=True)
    m = jnp.where(jnp.isfinite(m), m, 0.0)
    e = jnp.exp(s - m)
    return e / jnp.maximum(jnp.sum(e, axis=-1, keepdims=True), 1e-30)

def alibi_slopes(n):
    return 2.0 ** (-8.0 * jnp.arange(1, n + 1, dtype=jnp.float32) / n)

def rope(x, cos, sin):
    half = x.shape[-1] // 2
    x1, x2 = x[..., :half], x[..., half:]
    return jnp.concatenate([x1 * cos - x2 * sin, x2 * cos + x1 * sin], axis=-1).astype(x.dtype)

def compress(kv, pe, w1, w2):
    B, S, G, dh = kv.shape
    r = CMP_LEN // CMP_STRIDE
    n_chunks = S // CMP_STRIDE
    nc = n_chunks - r + 1
    chunks = kv.reshape(B, n_chunks, CMP_STRIDE, G, dh)
    blocks = jnp.concatenate([chunks[:, i:i + nc] for i in range(r)], axis=2)
    blocks = blocks + pe[None, None, :, None, :]
    flat = blocks.transpose(0, 3, 1, 2, 4).reshape(B, G, nc, CMP_LEN * dh)
    return jax.nn.silu(flat @ w1) @ w2

def nsa_attention(q, kc, vc, ks, vs, kw, vw, gates):
    B, G, Hg, S, dh = q.shape
    nc = kc.shape[2]
    ns = S // SEL_BLOCK
    n_sel = min(SEL_TOPK, ns)
    n_key_sel = n_sel * SEL_BLOCK
    scale = dh ** -0.5
    slopes = alibi_slopes(G * Hg).reshape(1, G, Hg, 1, 1)
    c_start = jnp.arange(nc) * CMP_STRIDE
    c_end = c_start + CMP_LEN - 1
    s_start = jnp.arange(ns) * SEL_BLOCK
    overlap = ((c_start[:, None] < s_start[None, :] + SEL_BLOCK)
               & (c_end[:, None] >= s_start[None, :])).astype(jnp.float32)
    ks_blocks = ks.reshape(B, G, ns, SEL_BLOCK, dh)
    vs_blocks = vs.reshape(B, G, ns, SEL_BLOCK, dh)
    kw_pad = jnp.pad(kw, ((0, 0), (0, 0), (WINDOW, 0), (0, 0)))
    vw_pad = jnp.pad(vw, ((0, 0), (0, 0), (WINDOW, 0), (0, 0)))
    blk = jnp.arange(ns)
    in_blk = jnp.arange(SEL_BLOCK)
    win_off = jnp.arange(Q_BLOCK + WINDOW) - WINDOW
    gather = jax.vmap(jax.vmap(lambda kb, ix: kb[ix]))

    def block(qb):
        t0 = qb * Q_BLOCK
        t = t0 + jnp.arange(Q_BLOCK)
        qq = lax.dynamic_slice_in_dim(q, t0, Q_BLOCK, axis=3)
        g = lax.dynamic_slice_in_dim(gates, t0, Q_BLOCK, axis=4)
        dist_c = (t[:, None] - c_end[None, :]).astype(jnp.float32)
        s = jnp.einsum('bghqd,bgkd->bghqk', qq, kc).astype(jnp.float32) * scale - slopes * dist_c
        p_cmp = masked_softmax(s, dist_c >= 0)
        o_cmp = jnp.einsum('bghqk,bgkd->bghqd', p_cmp.astype(vc.dtype), vc)
        p_slc = jnp.einsum('bghqk,ks->bgqs', p_cmp, overlap)
        cur = t // SEL_BLOCK
        valid = blk[None, :] <= cur[:, None]
        forced = (blk[None, :] == 0) | (blk[None, :] >= cur[:, None] - 1)
        score = jnp.where(valid, p_slc + FORCE_BONUS * forced.astype(jnp.float32), -jnp.inf)
        _, idx = lax.top_k(score, n_sel)
        spos = idx[..., None] * SEL_BLOCK + in_blk
        smask = (spos <= t[:, None, None]).reshape(B, G, Q_BLOCK, n_key_sel)
        dist_s = (t[:, None, None] - spos).reshape(B, G, Q_BLOCK, n_key_sel).astype(jnp.float32)
        k_sel = gather(ks_blocks, idx).reshape(B, G, Q_BLOCK, n_key_sel, dh)
        v_sel = gather(vs_blocks, idx).reshape(B, G, Q_BLOCK, n_key_sel, dh)
        s = jnp.einsum('bghqd,bgqkd->bghqk', qq, k_sel).astype(jnp.float32) * scale - slopes * dist_s[:, :, None]
        p = masked_softmax(s, smask[:, :, None])
        o_sel = jnp.einsum('bghqk,bgqkd->bghqd', p.astype(vs.dtype), v_sel)
        k_win = lax.dynamic_slice_in_dim(kw_pad, t0, Q_BLOCK + WINDOW, axis=2)
        v_win = lax.dynamic_slice_in_dim(vw_pad, t0, Q_BLOCK + WINDOW, axis=2)
        wpos = t0 + win_off
        dist_w = t[:, None] - wpos[None, :]
        wmask = (dist_w >= 0) & (dist_w < WINDOW) & (wpos[None, :] >= 0)
        s = jnp.einsum('bghqd,bgkd->bghqk', qq, k_win).astype(jnp.float32) * scale - slopes * dist_w.astype(jnp.float32)
        p = masked_softmax(s, wmask)
        o_win = jnp.einsum('bghqk,bgkd->bghqd', p.astype(vw.dtype), v_win)
        o = g[0] * o_cmp + g[1] * o_sel + g[2] * o_win
        return o.transpose(0, 3, 1, 2, 4).reshape(B, Q_BLOCK, G * Hg * dh)

    out = lax.map(block, jnp.arange(S // Q_BLOCK))
    return out.transpose(1, 0, 2, 3).reshape(B, S, G * Hg * dh)

def mla_attention(q, k, v):
    B, H, S, dqk = q.shape
    dv = v.shape[-1]
    scale = dqk ** -0.5
    kpos = jnp.arange(S)

    def block(qb):
        t0 = qb * Q_BLOCK
        t = t0 + jnp.arange(Q_BLOCK)
        qq = lax.dynamic_slice_in_dim(q, t0, Q_BLOCK, axis=2)
        s = jnp.einsum('bhqd,bhkd->bhqk', qq, k).astype(jnp.float32) * scale
        p = masked_softmax(s, kpos[None, :] <= t[:, None])
        o = jnp.einsum('bhqk,bhkd->bhqd', p.astype(v.dtype), v)
        return o.transpose(0, 2, 1, 3).reshape(B, Q_BLOCK, H * dv)

    out = lax.map(block, jnp.arange(S // Q_BLOCK))
    return out.transpose(1, 0, 2, 3).reshape(B, S, H * dv)

def first_inputs(seed: int = 0) -> dict:
    key = jax.random.key(seed)
    ks = jax.random.split(key, 24)
    f32 = jnp.float32

    def nrm(k, shape, scale):
        return jax.random.normal(k, (DEPTH,) + shape, f32) * scale

    def gain(k, n):
        return 1.0 + 0.05 * jax.random.normal(k, (DEPTH, n), f32)

    dqk = MLA_NOPE + MLA_ROPE
    return {
        'x': jax.random.normal(ks[0], (BATCH, SEQ, D_MODEL), f32),
        'c': jax.random.normal(ks[1], (BATCH, D_MODEL), f32),
        'w_ada': nrm(ks[2], (D_MODEL, 6 * D_MODEL), 0.5 * D_MODEL ** -0.5),
        'b_ada': nrm(ks[3], (6 * D_MODEL,), 0.01),
        'g_mix': gain(ks[4], D_MODEL),
        'w_in': nrm(ks[5], (D_MODEL, IN_DIM), D_MODEL ** -0.5),
        'pe_ck': nrm(ks[6], (CMP_LEN, NSA_HEAD_DIM), 0.1),
        'w_ck1': nrm(ks[7], (CMP_LEN * NSA_HEAD_DIM, CMP_HIDDEN), (CMP_LEN * NSA_HEAD_DIM) ** -0.5),
        'w_ck2': nrm(ks[8], (CMP_HIDDEN, NSA_HEAD_DIM), CMP_HIDDEN ** -0.5),
        'pe_cv': nrm(ks[9], (CMP_LEN, NSA_HEAD_DIM), 0.1),
        'w_cv1': nrm(ks[10], (CMP_LEN * NSA_HEAD_DIM, CMP_HIDDEN), (CMP_LEN * NSA_HEAD_DIM) ** -0.5),
        'w_cv2': nrm(ks[11], (CMP_HIDDEN, NSA_HEAD_DIM), CMP_HIDDEN ** -0.5),
        'g_cq': gain(ks[12], MLA_Q_RANK),
        'w_uq': nrm(ks[13], (MLA_Q_RANK, MLA_HEADS * dqk), MLA_Q_RANK ** -0.5),
        'g_ckv': gain(ks[14], MLA_KV_RANK),
        'w_uk': nrm(ks[15], (MLA_KV_RANK, MLA_HEADS * MLA_NOPE), MLA_KV_RANK ** -0.5),
        'w_uv': nrm(ks[16], (MLA_KV_RANK, MLA_HEADS * MLA_V), MLA_KV_RANK ** -0.5),
        'w_o_nsa': nrm(ks[17], (NSA_Q_DIM, D_MODEL), NSA_Q_DIM ** -0.5),
        'w_o_mla': nrm(ks[18], (MLA_HEADS * MLA_V, D_MODEL), (MLA_HEADS * MLA_V) ** -0.5),
        'w_out': nrm(ks[19], (D_MODEL, D_MODEL), D_MODEL ** -0.5),
        'g_mlp': gain(ks[20], D_MODEL),
        'w_fc1': nrm(ks[21], (D_MODEL, D_FF), D_MODEL ** -0.5),
        'w_fc2': nrm(ks[22], (D_FF, D_MODEL), D_FF ** -0.5),
        'g_final': 1.0 + 0.05 * jax.random.normal(ks[23], (D_MODEL,), f32),
    }

def first_block(x, c, w_ada, b_ada, g_mix, w_in, pe_ck, w_ck1, w_ck2, pe_cv, w_cv1, w_cv2,
              g_cq, w_uq, g_ckv, w_uk, w_uv, w_o_nsa, w_o_mla, w_out, g_mlp, w_fc1, w_fc2, g_final):
    B, S, _ = x.shape
    G, Hg, dh = NSA_KV_GROUPS, NSA_HG, NSA_HEAD_DIM
    split_points = np.cumsum(IN_SPLITS)[:-1].tolist()
    half = MLA_ROPE // 2
    pos = jnp.arange(S, dtype=jnp.float32)
    inv_freq = ROPE_THETA ** (-jnp.arange(half, dtype=jnp.float32) / half)
    ang = pos[:, None] * inv_freq[None, :]
    cos, sin = jnp.cos(ang), jnp.sin(ang)

    def kv_groups(t):
        return t.reshape(B, S, G, dh)

    for layer in range(DEPTH):
        mod = c @ w_ada[layer] + b_ada[layer]
        sh_a, sc_a, gt_a, sh_m, sc_m, gt_m = jnp.split(mod, 6, axis=-1)

        h = modulate(rmsnorm(x, g_mix[layer]), sh_a, sc_a)
        z = h @ w_in[layer]
        (zq, zkc, zvc, zks, zvs, zkw, zvw, zg, zqd, zkvd, zkr, zga, zgb) = jnp.split(z, split_points, axis=-1)

        q_nsa = zq.reshape(B, S, G, Hg, dh).transpose(0, 2, 3, 1, 4)
        kc = compress(kv_groups(zkc), pe_ck[layer], w_ck1[layer], w_ck2[layer])
        vc = compress(kv_groups(zvc), pe_cv[layer], w_cv1[layer], w_cv2[layer])
        k_s = kv_groups(zks).transpose(0, 2, 1, 3)
        v_s = kv_groups(zvs).transpose(0, 2, 1, 3)
        k_w = kv_groups(zkw).transpose(0, 2, 1, 3)
        v_w = kv_groups(zvw).transpose(0, 2, 1, 3)
        nsa_gates = jax.nn.sigmoid(zg).reshape(B, S, 3, G, Hg).transpose(2, 0, 3, 4, 1)[..., None]
        o_nsa = nsa_attention(q_nsa, kc, vc, k_s, v_s, k_w, v_w, nsa_gates)

        cq = rmsnorm(zqd, g_cq[layer])
        qm = (cq @ w_uq[layer]).reshape(B, S, MLA_HEADS, MLA_NOPE + MLA_ROPE)
        q_rot = rope(qm[..., MLA_NOPE:], cos[:, None, :], sin[:, None, :])
        q_mla = jnp.concatenate([qm[..., :MLA_NOPE], q_rot], axis=-1)
        ckv = rmsnorm(zkvd, g_ckv[layer])
        k_nope = (ckv @ w_uk[layer]).reshape(B, S, MLA_HEADS, MLA_NOPE)
        v_mla = (ckv @ w_uv[layer]).reshape(B, S, MLA_HEADS, MLA_V)
        k_rot = rope(zkr, cos, sin)
        k_mla = jnp.concatenate(
            [k_nope, jnp.broadcast_to(k_rot[:, :, None, :], (B, S, MLA_HEADS, MLA_ROPE))], axis=-1)
        o_mla = mla_attention(q_mla.transpose(0, 2, 1, 3), k_mla.transpose(0, 2, 1, 3),
                              v_mla.transpose(0, 2, 1, 3))

        y = jax.nn.sigmoid(zga) * (o_nsa @ w_o_nsa[layer]) + jax.nn.sigmoid(zgb) * (o_mla @ w_o_mla[layer])
        x = x + gt_a[:, None, :] * (y @ w_out[layer])

        h = modulate(rmsnorm(x, g_mlp[layer]), sh_m, sc_m)
        x = x + gt_m[:, None, :] * (jnp.square(jax.nn.relu(h @ w_fc1[layer])) @ w_fc2[layer])

    return rmsnorm(x, g_final)


CHUNK = 64
D_MIX = D_MODEL
D_SSM = D_MIX // 2
D_ATT = D_MIX - D_SSM
SSM_GROUP = 16
N_SSM_GROUPS = D_SSM // SSM_GROUP
SSM_STATE = 64
HEAD_DIM = 64
N_HEADS = D_ATT // HEAD_DIM
LEFT_CHUNKS = 8
BAND = (LEFT_CHUNKS + 1) * CHUNK
MAX_REL = 128
D_FF_2 = -(-8 * D_MODEL // (3 * 256)) * 256
D_IN = D_SSM + 3 * D_ATT
DT_MIN = 1e-3
DT_MAX = 1e-1


def rmsnorm_2(x, g):
    xf = x.astype(jnp.float32)
    y = xf * lax.rsqrt(jnp.mean(xf * xf, axis=-1, keepdims=True) + EPS)
    return (y * g.astype(jnp.float32)).astype(x.dtype)

def s5_mixer(u, lam_re, lam_im, log_dt, b_re, b_im, c_re, c_im, d_skip, w_glu, b_glu):
    bsz, seq, _ = u.shape
    f32 = jnp.float32
    uf = u.astype(f32).reshape(bsz, seq, N_SSM_GROUPS, SSM_GROUP)
    lam = lax.complex(lam_re.astype(f32), lam_im.astype(f32))
    dt = jnp.exp(log_dt.astype(f32))[:, None]
    lam_bar = jnp.exp(lam * dt)
    b_mat = lax.complex(b_re.astype(f32), b_im.astype(f32))
    b_bar = ((lam_bar - 1.0) / lam)[..., None] * b_mat
    bu = jnp.einsum('bsgh,gph->bsgp', uf.astype(jnp.complex64), b_bar)
    a = jnp.broadcast_to(lam_bar, bu.shape)

    def combine(left, right):
        a_l, b_l = left
        a_r, b_r = right
        return a_r * a_l, a_r * b_l + b_r

    _, states = lax.associative_scan(combine, (a, bu), axis=1)
    c_mat = lax.complex(c_re.astype(f32), c_im.astype(f32))
    y = jnp.einsum('bsgp,ghp->bsgh', states, c_mat).real + d_skip.astype(f32) * uf
    y = jax.nn.gelu(y.reshape(bsz, seq, D_SSM))
    y = y * jax.nn.sigmoid(y @ w_glu.astype(f32) + b_glu.astype(f32))
    return y.astype(u.dtype)

def chunked_attention(q, k, v, rel_bias):
    bsz, seq, _ = q.shape
    n_chunks = seq // CHUNK
    shp = (bsz, n_chunks, CHUNK, N_HEADS, HEAD_DIM)
    qc, kc, vc = q.reshape(shp), k.reshape(shp), v.reshape(shp)
    pad = ((0, 0), (LEFT_CHUNKS, 0), (0, 0), (0, 0), (0, 0))
    kp, vp = jnp.pad(kc, pad), jnp.pad(vc, pad)
    kb = jnp.concatenate([kp[:, j:j + n_chunks] for j in range(LEFT_CHUNKS + 1)], axis=2)
    vb = jnp.concatenate([vp[:, j:j + n_chunks] for j in range(LEFT_CHUNKS + 1)], axis=2)
    key_chunk = jnp.arange(n_chunks)[:, None] - LEFT_CHUNKS + (jnp.arange(BAND) // CHUNK)[None, :]
    valid = key_chunk >= 0
    rel = jnp.arange(BAND)[None, :] - LEFT_CHUNKS * CHUNK - jnp.arange(CHUNK)[:, None]
    idx = jnp.clip(rel, -MAX_REL, MAX_REL) + MAX_REL
    bias = rel_bias.astype(jnp.float32)[:, idx]
    scores = jnp.einsum('bnqhd,bnkhd->bhnqk', qc, kb).astype(jnp.float32) / math.sqrt(HEAD_DIM)
    scores = scores + bias[None, :, None, :, :]
    scores = jnp.where(valid[None, None, :, None, :], scores, -1e30)
    probs = jax.nn.softmax(scores, axis=-1)
    out = jnp.einsum('bhnqk,bnkhd->bnqhd', probs.astype(v.dtype), vb)
    return out.reshape(bsz, seq, D_ATT)

def second_inputs(seed: int = 0) -> dict:
    key = jax.random.key(seed)
    ks = jax.random.split(key, 24)
    f32 = jnp.float32
    L, G, P, H = DEPTH, N_SSM_GROUPS, SSM_STATE, SSM_GROUP

    def nrm(k, shape, scale):
        return jax.random.normal(k, shape, f32) * scale

    def gain(k, n):
        return 1.0 + 0.05 * jax.random.normal(k, (L, n), f32)

    lam_re = -0.5 + 0.01 * jax.random.normal(ks[3], (L, G, P), f32)
    lam_im = math.pi * jnp.arange(P, dtype=f32)[None, None, :] + 0.01 * jax.random.normal(ks[4], (L, G, P), f32)
    log_dt = jax.random.uniform(ks[5], (L, G), f32, math.log(DT_MIN), math.log(DT_MAX))
    return {
        "x": jax.random.normal(ks[0], (BATCH, SEQ, D_MODEL), f32),
        "norm_mix_g": gain(ks[1], D_MODEL),
        "w_in": nrm(ks[2], (L, D_MODEL, D_IN), D_MODEL ** -0.5),
        "ssm_lam_re": lam_re,
        "ssm_lam_im": lam_im,
        "ssm_log_dt": log_dt,
        "ssm_b_re": nrm(ks[6], (L, G, P, H), (2.0 * H) ** -0.5),
        "ssm_b_im": nrm(ks[7], (L, G, P, H), (2.0 * H) ** -0.5),
        "ssm_c_re": nrm(ks[8], (L, G, H, P), (2.0 * P) ** -0.5),
        "ssm_c_im": nrm(ks[9], (L, G, H, P), (2.0 * P) ** -0.5),
        "ssm_d": nrm(ks[10], (L, G, H), 1.0),
        "ssm_w_glu": nrm(ks[11], (L, D_SSM, D_SSM), D_SSM ** -0.5),
        "ssm_b_glu": nrm(ks[12], (L, D_SSM), 0.02),
        "attn_rel_bias": nrm(ks[13], (L, N_HEADS, 2 * MAX_REL + 1), 0.5),
        "norm_ssm_out_g": gain(ks[14], D_SSM),
        "norm_att_out_g": gain(ks[15], D_ATT),
        "w_out": nrm(ks[16], (L, D_MIX, D_MODEL), D_MIX ** -0.5),
        "norm_ffn_g": gain(ks[17], D_MODEL),
        "w_gate": nrm(ks[18], (L, D_MODEL, D_FF_2), D_MODEL ** -0.5),
        "w_up": nrm(ks[19], (L, D_MODEL, D_FF_2), D_MODEL ** -0.5),
        "w_down": nrm(ks[20], (L, D_FF_2, D_MODEL), D_FF_2 ** -0.5),
        "norm_final_g": 1.0 + 0.05 * jax.random.normal(ks[21], (D_MODEL,), f32),
    }

def second_block(x, norm_mix_g, w_in, ssm_lam_re, ssm_lam_im, ssm_log_dt, ssm_b_re, ssm_b_im,
              ssm_c_re, ssm_c_im, ssm_d, ssm_w_glu, ssm_b_glu, attn_rel_bias,
              norm_ssm_out_g, norm_att_out_g, w_out, norm_ffn_g, w_gate, w_up, w_down,
              norm_final_g):
    for l in range(DEPTH):
        h = rmsnorm_2(x, norm_mix_g[l])
        proj = h @ w_in[l]
        u_ssm = proj[..., :D_SSM]
        q = proj[..., D_SSM:D_SSM + D_ATT]
        k = proj[..., D_SSM + D_ATT:D_SSM + 2 * D_ATT]
        v = proj[..., D_SSM + 2 * D_ATT:]
        y_ssm = s5_mixer(u_ssm, ssm_lam_re[l], ssm_lam_im[l], ssm_log_dt[l], ssm_b_re[l], ssm_b_im[l],
                         ssm_c_re[l], ssm_c_im[l], ssm_d[l], ssm_w_glu[l], ssm_b_glu[l])
        y_att = chunked_attention(q, k, v, attn_rel_bias[l])
        mixed = jnp.concatenate([rmsnorm_2(y_ssm, norm_ssm_out_g[l]),
                                 rmsnorm_2(y_att, norm_att_out_g[l])], axis=-1)
        x = x + mixed @ w_out[l]
        h2 = rmsnorm_2(x, norm_ffn_g[l])
        x = x + (jax.nn.silu(h2 @ w_gate[l]) * (h2 @ w_up[l])) @ w_down[l]
    return rmsnorm_2(x, norm_final_g)


def setup_inputs(seed=0):
    out = dict(first_inputs(seed))
    for name, value in second_inputs(seed + 1).items():
        if name != "x":
            out[name + "_2"] = value
    return out


def reference(
    x, c, w_ada, b_ada, g_mix, w_in, pe_ck, w_ck1, w_ck2, pe_cv, w_cv1, w_cv2, g_cq, w_uq,
    g_ckv, w_uk, w_uv, w_o_nsa, w_o_mla, w_out, g_mlp, w_fc1, w_fc2, g_final, norm_mix_g_2,
    w_in_2, ssm_lam_re_2, ssm_lam_im_2, ssm_log_dt_2, ssm_b_re_2, ssm_b_im_2, ssm_c_re_2,
    ssm_c_im_2, ssm_d_2, ssm_w_glu_2, ssm_b_glu_2, attn_rel_bias_2, norm_ssm_out_g_2,
    norm_att_out_g_2, w_out_2, norm_ffn_g_2, w_gate_2, w_up_2, w_down_2, norm_final_g_2,
):
    x = first_block(
        x, c, w_ada, b_ada, g_mix, w_in, pe_ck, w_ck1, w_ck2, pe_cv, w_cv1, w_cv2, g_cq, w_uq,
        g_ckv, w_uk, w_uv, w_o_nsa, w_o_mla, w_out, g_mlp, w_fc1, w_fc2, g_final,
    )
    return second_block(
        x, norm_mix_g_2, w_in_2, ssm_lam_re_2, ssm_lam_im_2, ssm_log_dt_2, ssm_b_re_2,
        ssm_b_im_2, ssm_c_re_2, ssm_c_im_2, ssm_d_2, ssm_w_glu_2, ssm_b_glu_2, attn_rel_bias_2,
        norm_ssm_out_g_2, norm_att_out_g_2, w_out_2, norm_ffn_g_2, w_gate_2, w_up_2, w_down_2,
        norm_final_g_2,
    )


_drawn_inputs = setup_inputs


def setup_inputs(seed=0):
    import zlib

    import numpy as np

    out = dict(_drawn_inputs(seed))
    spreads = {}
    factors = {'b_ada': 2.714,
     'g_mix': 4.721,
     'pe_ck': 8.0,
     'pe_cv': 4.979,
     'g_cq': 8.0,
     'g_ckv': 7.012,
     'ssm_lam_re_2': 200.0,
     'ssm_b_glu_2': 8.0,
     'g_mlp': 3.154,
     'ssm_lam_im_2': 36.632,
     'ssm_log_dt_2': 39.904,
     'ssm_b_re_2': 50.344,
     'ssm_b_im_2': 50.88,
     'ssm_c_re_2': 50.616,
     'ssm_c_im_2': 50.36}
    for name, (base, spread) in spreads.items():
        noise = np.random.default_rng([zlib.crc32(name.encode()), seed]).standard_normal(out[name].shape)
        drawn = base * np.exp(spread * noise) if base else spread * noise
        out[name] = __import__('jax').numpy.asarray(drawn.astype(out[name].dtype))
    for name, factor in factors.items():
        out[name] = (out[name] * factor).astype(out[name].dtype)
    return out
```

```python
import concourse.bass as bass
from concourse import mybir
from contextlib import ExitStack
import numpy as np

F32 = mybir.dt.float32
F32R = mybir.dt.float32r
I32 = mybir.dt.int32
ACT = mybir.ActivationFunctionType
ALU = mybir.AluOpType
AX = mybir.AxisListType

P = 128
T = 512
D = 1024
KD = D // P
TT = T // P
EPS = 1e-6
NEG = -1e30
FF1, FF2 = 4096, 2816
NF1, NF2 = FF1 // P, FF2 // P
HEADS, DH = 8, 64
MLA_SCALE = 96.0 ** -0.5
NCMP = 31
SSM_L = 8
SSM_C = T // SSM_L
SSM_Q = 16
RING = 4
AHEAD = 3

C_Q, C_KC, C_VC, C_KS, C_VS, C_KW, C_VW, C_G, C_QD, C_KVD, C_KR, C_GA, C_GB = np.cumsum(
    [0, 512, 128, 128, 128, 128, 128, 128, 24, 384, 256, 32, 1024]).tolist()

U_A1 = 0
A1_COLS = [C_KC, C_VC, C_KS, C_KW, C_VS, C_VW] + [C_Q + P * i for i in range(4)] \
    + [C_QD + P * i for i in range(3)] + [C_KVD + P * i for i in range(2)]
U_TAIL = U_A1 + len(A1_COLS)
U_UQ = U_TAIL + 1
U_UK = U_UQ + 4
U_UV = U_UK + 1
U_Y = U_UV + 1
U_OUT = U_Y + 3 * KD
U_FC1 = U_OUT + KD
U_FC2 = U_FC1 + NF1
U_IN2 = U_FC2 + NF1
U_V2 = U_IN2 + 12
U_GLU = U_V2 + 4
U_OUT2 = U_GLU + 2
U_GU = U_OUT2 + KD
U_DN = U_GU + 2 * NF2
U_END = U_DN + NF2

G_A1 = 0
G_UQ = G_A1 + 16
G_UK = G_UQ + 8
G_UV = G_UK + 4
G_Y = G_UV + 4
G_OUT = G_Y + 4 * KD
G_FC1 = G_OUT + KD
G_IN2 = G_FC1 + NF1
G_GLU = G_IN2 + 12
G_OUT2 = G_GLU + 4
G_GU = G_OUT2 + KD
G_END = G_GU + 2 * NF2

VROWS = {}
_n = 0
for _name, _rows in (("b_ada", 48), ("g_mix", 8), ("c", 8), ("g_mlp", 8), ("g_cq", 3), ("g_ckv", 2),
                     ("norm_mix_g_2", 8), ("norm_ffn_g_2", 8), ("ssm_b_glu_2", 4), ("ssm_d_2", 4),
                     ("norm_ssm_out_g_2", 4), ("norm_att_out_g_2", 4), ("g_final", 8)):
    VROWS[_name] = (_n, _rows)
    _n += _rows
NV = _n


def program(nc, a, out, scr, dbg=None):
    with ExitStack() as ctx:
        S = {}

        ATTS = {"nsa": 16, "mla": 8, "chk": 8}
        NORMS = {"n1": 8, "ncq": 3, "nckv": 2, "n2": 8, "nf": 8, "n3": 8, "nssm": 4, "n4": 8}

        def since(name, value):
            who, _, what = name.partition("_")
            for group in (NORMS, ATTS):
                if who in group:
                    who_before = list(group)[:list(group).index(who)]
                    before = [group[k] for k in who_before]
                    split = sum(n for k, n in group.items() if k in who_before and k != "nf") if group is NORMS else 0
                    if group is NORMS and what in ("h", "hi", "lo"):
                        return split + value
                    per = (lambda n: {"sq": n, "dg": TT}.get(what, 1)) if group is NORMS else \
                        (lambda n: {"o": n, "pta": 2 * n, "ptd": 2 * n}.get(what, 4 * n))
                    return sum(map(per, before)) + value
            return value

        def sem(name):
            who, _, what = name.partition("_")
            name = "norm_" + what if who in NORMS else "att_" + what if who in ATTS else name
            if name not in S:
                S[name] = ctx.enter_context(nc.semaphore(name))
            return S[name]

        base = [(nc.sbuf_base + 31) // 32 * 32]
        limit = nc.sbuf_usable_end

        def at(name, offset, shape, dt=F32):
            n = int(np.prod(shape[1:])) * 4
            assert offset + n <= limit, (name, offset + n - limit)
            return nc.alloc_sbuf_tensor_at(name, shape, dt, offset=offset)

        def keep(name, shape, dt=F32):
            t = at(name, base[0], shape, dt)
            base[0] += (int(np.prod(shape[1:])) * 4 + 31) // 32 * 32
            return t

        ident = keep("ident", [P, P])
        ones = keep("ones", [P, P])
        vcol = keep("vcol", [P, NV + 32])
        modc = keep("modc", [P, 48])
        gain = keep("gain", [P, 2, KD])
        stat = keep("stat", [P, 8, 4])
        rsum = keep("rsum", [P, 2, 4])
        rinv = keep("rinv", [P, 4])
        smax = keep("smax", [P, 4])
        ssmc = keep("ssmc", [P, 3, SSM_Q])
        hb = keep("hb", [P, 2, T])
        xT = keep("xT", [P, KD, T])
        wraw = keep("wraw", [P, RING, D])
        whi = keep("whi", [P, RING, D], F32R)
        wlo = keep("wlo", [P, RING, D], F32R)
        H0 = base[0]
        hhi = keep("hhi", [P, KD, T], F32R)
        hlo = keep("hlo", [P, KD, T], F32R)
        X0 = base[0]
        K = 1024
        diag = hb[:, 0, :]

        def x_at(name, kb, shape, dt=F32):
            return at(name, X0 + int(kb * K), shape, dt)

        xs = at("xs", H0, [P, TT, D])
        qT = x_at("qT", 0, [P, 4, T])
        kdup = x_at("kdup", 8, [P, 2, 2, T])
        vnat = x_at("vnat", 16, [P, TT, 2, P])
        vblk = x_at("vblk", 20, [P, 2, 4, DH])
        kcT = x_at("kcT", 22, [P, 2, NCMP])
        gates = x_at("gates", 22.5, [P, TT, 24])
        qm = x_at("qm", 23, [P, HEADS, T])
        km = x_at("km", 39, [P, HEADS, T])
        vm = x_at("vm", 55, [P, TT, HEADS * DH])
        bias = x_at("bias", 63, [P, 4, T])
        cmask = x_at("cmask", 71, [P, T])
        onsa = x_at("onsa", 73, [P, TT, T])
        omla = x_at("omla", 81, [P, TT, T])
        ssb = x_at("ssb", 89, [P, 2, T])
        ppb = x_at("ppb", 93, [P, 3, T])
        ptb = x_at("ptb", 99, [P, 3, T])
        sq = x_at("sq", 73, [P, KD, T])
        x2 = x_at("x2", 73, [P, 2, 2, T])
        flat = x_at("flat", 81, [P, 2, 16, 62])
        praw = x_at("praw", 89, [P, RING, D])
        cqhi = x_at("cqhi", 89, [P, 3, T], F32R)
        cqlo = x_at("cqlo", 95, [P, 3, T], F32R)
        krot = x_at("krot", 101, [P, T])
        rope = x_at("rope", 103, [P, T])
        ckhi = x_at("ckhi", 63, [P, 2, T], F32R)
        cklo = x_at("cklo", 67, [P, 2, T], F32R)
        zl = x_at("zl", 39, [P, 5, T])
        zg = x_at("zg", 49, [P, T])
        vrow = x_at("vrow", 55.5, [P, 2, P])
        hid = x_at("hid", 51, [P, 2, 2, 2, 32])
        hidr = x_at("hidr", 52, [P, 2, 2, 4, 32])
        w2d = x_at("w2d", 54, [P, 2, 2, DH])
        w2v = x_at("w2v", 55, [P, 2, DH])
        cbias = x_at("cbias", 89, [P, 32, NCMP])
        cs = x_at("cs", 93, [P, 32, NCMP])
        cp = x_at("cp", 97, [P, 32, 32])
        cpt = x_at("cpt", 101, [P, 8, P])
        cst = x_at("cst", 105, [P, 4, 32])
        othi = x_at("othi", 0, [P, 8, T], F32R)
        otlo = x_at("otlo", 16, [P, 8, T], F32R)
        yhi = x_at("yhi", 32, [P, KD, T], F32R)
        ylo = x_at("ylo", 48, [P, KD, T], F32R)
        sg = x_at("sg", 64, [P, 2, T])
        ym = x_at("ym", 89, [P, 3, T])
        ff = x_at("ff", 0, [P, NF1, T])
        fhi = x_at("fhi", 65, [P, 2, T], F32R)
        flo = x_at("flo", 69, [P, 2, T], F32R)
        rb = x_at("rb", 89, [P, 2, T])
        xn = x_at("xn", 47, [P, TT, D])
        gfin = x_at("gfin", 93, [P, D])
        uT = x_at("uT", 0, [P, 4, SSM_L, SSM_C])
        ug = x_at("ug", 8, [P, 32, SSM_C])
        q2 = x_at("q2", 16, [P, 4, T])
        k2 = x_at("k2", 24, [P, 4, T])
        v2 = x_at("v2", 32, [P, TT, T])
        w1s = x_at("w1s", 40, [P, 2, SSM_Q, P])
        w2s = x_at("w2s", 40, [P, 2, SSM_Q, P])
        tmat = x_at("tmat", 56, [P, 32, P])
        sA = x_at("sA", 72, [P, SSM_Q, SSM_C])
        sB = x_at("sB", 76, [P, SSM_Q, SSM_C])
        twr = x_at("twr", 80, [P, SSM_Q, SSM_C])
        twi = x_at("twi", 84, [P, SSM_Q, SSM_C])
        vA = x_at("vA", 88, [P, SSM_Q, SSM_C])
        vB = x_at("vB", 92, [P, SSM_Q, SSM_C])
        tA = x_at("tA", 96, [P, SSM_Q, SSM_C])
        tB = x_at("tB", 100, [P, SSM_Q, SSM_C])
        yg = x_at("yg", 96, [P, 32, SSM_C])
        bias2 = x_at("bias2", 72, [P, HEADS, T])
        yatt = x_at("yatt", 88, [P, TT, T])
        yssm = x_at("yssm", 40, [P, 4, SSM_L, SSM_C])
        ygel = x_at("ygel", 8, [P, 4, T])
        ghi = x_at("ghi", 48, [P, 4, T], F32R)
        glo = x_at("glo", 56, [P, 4, T], F32R)
        ysg = x_at("ysg", 64, [P, 4, T])
        sq2 = x_at("sq2", 72, [P, 4, T])
        ssb2 = at("ssb2", H0, [P, 2, T])
        ppb2 = at("ppb2", H0 + 4 * K, [P, 3, T])
        ptb2 = at("ptb2", H0 + 10 * K, [P, 3, T])
        twc = x_at("twc", 104.5, [P, 4, SSM_Q])
        pv = x_at("pv", 23, [16, 24, P])
        dtl = x_at("dtl", 36.75, [16, 8, 2])
        pvi = x_at("pvi", 36, [16, P], I32)
        dti = x_at("dti", 36.5, [16, 2], I32)
        w1t = x_at("w1t", 23, [P, 2, 4, P])
        cpw = x_at("cpw", 27, [P, 2, 4, 9, 16])
        tmp = x_at("tmp", 31.5, [P, 2, 4 * 9 * 16])
        stg = x_at("stg", 56.5, [P, 2, 4, P])
        kst = x_at("kst", 73, [32, 4, P])
        bpair = x_at("bpair", 77, [P, 2, SSM_Q, 2, 16])
        braw = x_at("braw", 63, [P, 2, SSM_Q, 16])
        bbar = x_at("bbar", 65, [P, 2, SSM_Q, 16])
        craw = x_at("craw", 49, [P, 2, 4, 2, 64])
        ctp = x_at("ctp", 67, [P, 2, SSM_Q, 16])
        pw = x_at("pw", 69, [P, 2, SSM_Q, 9])
        pwr = x_at("pwr", 70.25, [P, 2, SSM_Q, 8])
        apar = x_at("apar", 71.5, [P, 7, SSM_Q])
        rel = x_at("rel", 60.5, [8, 640])

        ps = ctx.enter_context(nc.psum_tensor("ps", [P, 8, T], F32))

        def col(name, i=0):
            return vcol[:, VROWS[name][0] + i:VROWS[name][0] + i + 1]

        def mod(part, i):
            return modc[:, part * KD + i:part * KD + i + 1]

        def slot(u):
            return u % RING

        def freed(eng, g, turn=0):
            eng.wait_ge(sem(f"t_free{g % 2}"), g // 2 + 1 + turn * (RING // 2))

        def free(ins, g):
            return ins.then_inc(sem(f"t_free{g % 2}"), 1)

        def used(u):
            for first, fn in ((U_DN, lambda i: ("f2_used", i + 1)), (U_GU, lambda i: ("tile", G_GU + i + 1)),
                              (U_OUT2, lambda i: ("tile", G_OUT2 + i + 1)), (U_GLU, lambda i: ("tile", G_GLU + 2 * i + 2)),
                              (U_V2, lambda i: ("v2_t", i + 1)), (U_IN2, lambda i: ("tile", G_IN2 + i + 1)),
                              (U_FC2, lambda i: ("f1_used", i + 1)), (U_FC1, lambda i: ("tile", G_FC1 + i + 1)),
                              (U_OUT, lambda i: ("tile", G_OUT + i + 1)),
                              (U_Y, lambda i: ("tile", G_Y + 4 * (i // 3) + (i % 3 + 1 if i % 3 < 2 else 4))),
                              (U_UV, lambda i: ("tile", G_UV + 4)), (U_UK, lambda i: ("tile", G_UK + 4)),
                              (U_UQ, lambda i: ("tile", G_UQ + 2 * i + 2)), (0, lambda i: ("tile", i + 1))):
                if u >= first:
                    return fn(u - first)

        def bank(g):
            return g % 2

        win = a["w_in"][0].rearrange("(k p) n -> p k n", p=P)

        def loop(eng, n):
            return eng.Fori(0, n)

        def nsa_heads():
            res = []
            for g in range(2):
                for br in range(2):
                    for h in range(4 * g, 4 * g + 4):
                        r = slice(64 * (h % 2), 64 * (h % 2) + 64)
                        res.append(dict(q=qT[r, h // 2, :], k=kdup[r, br, g, :],
                                        v=lambda b, br=br, g=g: vnat[:, b, br, 64 * g:64 * g + 64],
                                        bias=bias[:, h % 4, :], scale=DH ** -0.5, o=onsa, h=h,
                                        gate=gates[:, :, 8 * (br + 1) + h], rescale=(g == 1 and br == 0 and h == 4)))
            return res

        def mla_heads():
            return [dict(q=qm[0:96, h, :], k=km[0:96, h, :], v=lambda b, h=h: vm[:, b, 64 * h:64 * h + 64],
                         bias=cmask[:, :], scale=MLA_SCALE, o=omla, h=h, gate=None, rescale=False)
                    for h in range(HEADS)]

        def chunk_heads():
            return [dict(q=q2[64 * (h % 2):64 * (h % 2) + 64, h // 2, :], k=k2[64 * (h % 2):64 * (h % 2) + 64, h // 2, :],
                         v=lambda b, h=h: v2[:, b, 64 * h:64 * h + 64],
                         bias=bias2[:, h, :], scale=DH ** -0.5, o=yatt, h=h, gate=None, rescale=False)
                    for h in range(HEADS)]

        ATT = {"nsa": (nsa_heads(), ssb, ppb, ptb), "mla": (mla_heads(), ssb, ppb, ptb),
               "chk": (chunk_heads(), ssb2, ppb2, ptb2)}

        NORM = {"n1": (lambda k: xT[:, k, :], 8, sq), "ncq": (lambda k: zl[:, k, :], 3, sq),
                "nckv": (lambda k: zl[:, 3 + k, :], 2, sq), "n2": (lambda k: xT[:, k, :], 8, sq),
                "nf": (lambda k: xT[:, k, :], 8, sq), "n3": (lambda k: xT[:, k, :], 8, sq), "nssm": (lambda k: ysg[:, k, :], 4, sq2),
                "n4": (lambda k: xT[:, k, :], 8, sq)}
        AFTER = {"n1": (lambda k: gain[:, 0, k:k + 1], lambda k: mod(0, k), hhi, hlo),
                 "ncq": (lambda k: col("g_cq", k), None, cqhi, cqlo),
                 "nckv": (lambda k: col("g_ckv", k), None, ckhi, cklo),
                 "n2": (lambda k: gain[:, 1, k:k + 1], lambda k: mod(3, k), hhi, hlo),
                 "n3": (lambda k: col("norm_mix_g_2", k), None, hhi, hlo),
                 "nssm": (lambda k: col("norm_ssm_out_g_2", k), None, hhi, hlo),
                 "n4": (lambda k: col("norm_ffn_g_2", k), None, hhi, hlo)}

        block = ctx.enter_context(nc.Block())

        @block.sync
        def _(sp):
            def slot_free(u):
                if u >= RING:
                    sp.wait_ge(sem("w_lo"), u - RING + 1)

            def load(u, dst, src, n=None):
                sp.dma_start(dst, src).then_inc(sem(f"w_in{slot(u)}"), 16)

            def raw(u, lo=0, hi=D):
                return wraw[:, slot(u), lo:hi]

            sp.dma_start(xs[:], a["x"][0].rearrange("(t p) d -> p t d", p=P)).then_inc(sem("x_in"), 16)
            for i, c in enumerate(A1_COLS):
                u = U_A1 + i
                slot_free(u)
                load(u, raw(u).rearrange("p (k n) -> p k n", k=KD), win[:, :, c:c + P])
            u = U_TAIL
            slot_free(u)
            tail = raw(u).rearrange("p (k n) -> p k n", k=KD)
            for lo, c, n in ((0, C_G, 24), (64, C_KR, 32), (96, C_KR + 16, 16), (112, C_KR, 16)):
                load(u, tail[:, :, lo:lo + n], win[:, :, c:c + n])
            wuq = a["w_uq"][0].rearrange("(k p) (h n) -> p k h n", p=P, n=96)
            for i in range(4):
                u = U_UQ + i
                slot_free(u)
                v = raw(u, 0, 768).rearrange("p (k h n) -> p k h n", k=3, h=2)
                for h in range(2):
                    load(u, v[:, :, h, 0:96], wuq[:, :, 2 * i + h, :])
                    load(u, v[:, :, h, 96:112], wuq[:, :, 2 * i + h, 80:96])
                    load(u, v[:, :, h, 112:128], wuq[:, :, 2 * i + h, 64:80])
            for u, name in ((U_UK, "w_uk"), (U_UV, "w_uv")):
                slot_free(u)
                load(u, raw(u).rearrange("p (k n) -> p k n", k=2), a[name][0].rearrange("(k p) n -> p k n", p=P))
            for n in range(KD):
                for j, c in enumerate((C_GA, C_GB)):
                    u = U_Y + 3 * n + j
                    slot_free(u)
                    load(u, raw(u).rearrange("p (k n) -> p k n", k=KD), win[:, :, c + n * P:c + n * P + P])
                u = U_Y + 3 * n + 2
                slot_free(u)
                for j, name in enumerate(("w_o_nsa", "w_o_mla")):
                    load(u, raw(u, 512 * j, 512 * j + 512).rearrange("p (k n) -> p k n", k=4),
                         a[name][0].rearrange("(k p) n -> p k n", p=P)[:, :, n * P:n * P + P])

            def columns(u0, n, src):
                with loop(sp, n // RING) as i:
                    for j in range(RING):
                        sp.wait_ge(sem("w_lo"), u0 + RING * i + j - RING + 1)
                        load(u0 + j, raw(u0 + j).rearrange("p (k n) -> p k n", k=KD),
                             src[:, :, bass.ds(P * RING * i + P * j, P)])
                return u0 + n // RING * RING

            def rows(u0, n, src):
                with loop(sp, n // RING) as i:
                    for j in range(RING):
                        sp.wait_ge(sem("w_lo"), u0 + RING * i + j - RING + 1)
                        load(u0 + j, raw(u0 + j), src[bass.ds(P * RING * i + P * j, P), :])
                for j in range(n // RING * RING, n):
                    slot_free(u0 + j)
                    load(u0 + j, raw(u0 + j), src[P * j:P * j + P, :])

            columns(U_OUT, KD, a["w_out"][0].rearrange("(k p) n -> p k n", p=P))
            columns(U_FC1, NF1, a["w_fc1"][0].rearrange("(k p) n -> p k n", p=P))
            rows(U_FC2, NF1, a["w_fc2"][0])
            win2 = a["w_in_2"][0].rearrange("(k p) n -> p k n", p=P)
            columns(U_IN2, 12, win2)
            for i in range(4):
                u = U_V2 + i
                slot_free(u)
                load(u, raw(u).rearrange("p (k n) -> p k n", k=2), win2[:, 2 * i:2 * i + 2, 1536:2048])
            for i in range(2):
                u = U_GLU + i
                slot_free(u)
                load(u, raw(u).rearrange("p (k n) -> p k n", k=4),
                     a["ssm_w_glu_2"][0].rearrange("(k p) n -> p k n", p=P)[:, :, 256 * i:256 * i + 256])
            columns(U_OUT2, KD, a["w_out_2"][0].rearrange("(k p) n -> p k n", p=P))
            wg = a["w_gate_2"][0].rearrange("(k p) n -> p k n", p=P)
            wu = a["w_up_2"][0].rearrange("(k p) n -> p k n", p=P)
            with loop(sp, NF2 // 2) as i:
                for j in range(4):
                    u = U_GU + j
                    sp.wait_ge(sem("w_lo"), U_GU + 4 * i + j - RING + 1)
                    load(u, raw(u).rearrange("p (k n) -> p k n", k=KD),
                         (wg, wu)[j % 2][:, :, bass.ds(2 * P * i + (j // 2) * P, P)])
            rows(U_DN, NF2, a["w_down_2"][0])
            for t in range(TT):
                sp.wait_ge(sem("o_ready"), t + 1)
                sp.dma_start(out[0, P * t:P * t + P, :], xn[:, t, :]).then_inc(sem("stored"), 16)
            sp.wait_ge(sem("stored"), 16 * TT)

        def w_count(u):
            n = 0
            for v in range(slot(u), u + 1, RING):
                n += 4 if v == U_TAIL else 6 if U_UQ <= v < U_UK else \
                    2 if U_Y <= v < U_OUT and (v - U_Y) % 3 == 2 else 1
            return n

        @block.gpsimd
        def _(pool):
            wada = a["w_ada"][0].rearrange("(k p) n -> p k n", p=P)
            order = [("ada", n) for n in range(16)] + [("ck", i) for i in range(4)] + [("cv", i) for i in range(4)] \
                + [("ada", n) for n in range(16, 48)]
            nx = 0
            for i, (kind, n) in enumerate(order):
                if i >= RING:
                    pool.wait_ge(sem("p_used"), i - RING + 1)
                if kind == "ada":
                    pool.dma_start(praw[:, i % RING, :].rearrange("p (k n) -> p k n", k=KD),
                                   wada[:, :, P * n:P * n + P]).then_inc(sem(f"p_in{i % RING}"), 16)
                else:
                    pool.dma_start(praw[:, i % RING, :].rearrange("p (k n) -> p k n", k=4),
                                   a["w_ck1" if kind == "ck" else "w_cv1"][0].rearrange("(k p) n -> p k n", p=P)
                                   [:, 4 * n:4 * n + 4, :]).then_inc(sem(f"p_in{i % RING}"), 16)
            pool.wait_ge(sem("p_used"), len(order))
            pool.dma_start(rope[:], a["rope_table"]).then_inc(sem("rope_in"), 16)
            pool.wait_ge(sem("krot"), 3)
            for h in range(HEADS):
                if h == 0:
                    pool.wait_ge(sem("nckv_lo"), since("nckv_lo", 2))
                pool.tensor_copy(km[64:96, h, :], krot[64:96, :]).then_inc(sem("km_rope"), 1)
            pool.wait_ge(sem("ukv_done"), 1)
            pool.wait_ge(sem("km_rope"), HEADS)
            pool.dma_start(cbias[:], a["cmp_bias"]).then_inc(sem("cbias_in"), 16)
            pool.dma_start(bias[:], a["alibi"]).then_inc(sem("bias_in"), 16)
            pool.dma_start(cmask[:], a["causal"]).then_inc(sem("cmask_in"), 16)

            pool.wait_ge(sem("rel_out"), 16)
            pool.dma_start(scr["relp"], bass.AP(scr["rel"].tensor, 0, [[0, P], [640, HEADS], [1, 640]])).then_inc(sem("relp_out"), 16)
            pool.wait_ge(sem("relp_out"), 16)
            pool.wait_ge(sem("fc2_evac"), 8)
            pool.memset(tmat[:], 0.0).then_inc(sem("tz"), 1)
            pool.dma_start(w1s[:], scr["w1"].rearrange("c p q n -> p c q n")).then_inc(sem("w1s_in"), 16)
            pool.wait_ge(sem("tz"), 1)
            for j in range(SSM_L):
                for g in range(2):
                    pool.dma_start(tmat[16 * j:16 * j + 16, g:32:2, 16 * j:P],
                                   scr["kk"][16 * g:16 * g + 16, :, 0:P - 16 * j]).then_inc(sem("t_in"), 16)
            for m in range(4):
                freed(pool, G_IN2 + m)
                pool.dma_start(scr["u"][m], uT[:, m, :, :]).then_inc(sem("u_out"), 16)
            pool.wait_ge(sem("u_out"), 16 * 4)
            for j in range(SSM_L):
                pool.dma_start(ug[16 * j:16 * j + 16, :, :],
                               bass.AP(scr["u"].tensor, j * SSM_C, [[T, 16], [16 * T, 32], [1, SSM_C]])).then_inc(sem("u_in"), 16)
            pool.wait_ge(sem("s_done"), 1)
            pool.dma_start(w2s[:], scr["w2"].rearrange("c p q n -> p c q n")).then_inc(sem("w2s_in"), 16)
            pool.wait_ge(sem("ssm_y"), 1)
            pool.dma_start(bias2[:], bass.AP(scr["relp"].tensor, P - 1, [[HEADS * 640 - 1, P], [640, HEADS], [1, T]])
                           ).then_inc(sem("bias2_in"), 16)
            pool.wait_ge(sem("bias2_in"), 16)
            pool.memset(bias2[0:64, :, T - 64:T], NEG).then_inc(sem("bias2_ok"), 1)
            pool.wait_ge(sem("yg_ev"), 4)
            pool.dma_start(scr["y"], yg[:].rearrange("p g c -> p (g c)")).then_inc(sem("y_out"), 16)
            pool.wait_ge(sem("y_out"), 16)
            for m in range(4):
                for g in range(8):
                    pool.dma_start(yssm[16 * g:16 * g + 16, m, :, :],
                                   bass.AP(scr["y"].tensor, (8 * m + g) * SSM_C, [[32 * SSM_C, 16], [16 * 32 * SSM_C, SSM_L], [1, SSM_C]])
                                   ).then_inc(sem("y_in"), 16)
            pool.wait_ge(sem("fc2b_free"), 1)
            pool.dma_start(gfin[:], a["norm_final_g_2"].partition_broadcast(P)).then_inc(sem("gfin_in"), 16)
            pool.wait_ge(sem("gfin_in"), 16)

        @block.tensor
        def _(pe):
            def mm3(o, lhi, llo, rhi, rlo, start, stop, skip=False):
                pe.matmul(o, lhi, rhi, start=start, stop=False, skip_group_check=skip)
                pe.matmul(o, lhi, rlo, start=False, stop=False, skip_group_check=skip)
                return pe.matmul(o, llo, rhi, start=False, stop=stop, skip_group_check=skip)

            def unit_ready(u):
                pe.wait_ge(sem("w_lo"), u + 1)

            def bank_free(g):
                if g >= 2:
                    freed(pe, g - 2)

            def dense(u, g, hi, lo, kt=KD, off=0, mcols=P, stride=P, ready=None, first=0):
                for k in range(kt):
                    if ready is not None:
                        pe.wait_ge(sem(ready), since(ready, k + 1))
                    last = mm3(ps[0:mcols, bank(g), :], whi[:, slot(u), off + k * stride:off + k * stride + mcols],
                               wlo[:, slot(u), off + k * stride:off + k * stride + mcols],
                               hi[:, first + k, :], lo[:, first + k, :], k == 0, k == kt - 1)
                return last

            def norm_stats(nm):
                _, n, buf = NORM[nm]
                for k in range(n):
                    pe.wait_ge(sem(nm + "_sq"), since(nm + "_sq", k + 1))
                    for t in range(TT):
                        last = pe.matmul(ps[:, 6, t:t + 1], buf[:, k, P * t:P * t + P], ones[:, 0:1],
                                         start=(k == 0 and t == 0), stop=(k == n - 1), skip_group_check=True)
                last.then_inc(sem(nm + "_st"), 1)
                pe.wait_ge(sem(nm + "_dg"), since(nm + "_dg", 4))
                pe.matmul(ps[:, 7, :], ones[:, :], diag, start=True, stop=True).then_inc(sem(nm + "_r"), 1)

            def attention(nm):
                heads, sb, pb, tb = ATT[nm]
                N = 4 * len(heads)
                for s in range(N + 2):
                    if s < N:
                        hd, b = heads[s // 4], s % 4
                        if s >= 2:
                            pe.wait_ge(sem(nm + "_s"), since(nm + "_s", s - 1))
                        w = P * (b + 1)
                        pe.matmul(ps[:, 2 + s % 2, 0:w], hd["q"][:, P * b:P * b + P], hd["k"][:, 0:w],
                                  start=True, stop=True).then_inc(sem(nm + "_qk"), 1)
                    if 1 <= s <= N:
                        r = s - 1
                        b = r % 4
                        pe.wait_ge(sem(nm + "_p"), since(nm + "_p", r + 1))
                        if r >= 2:
                            pe.wait_ge(sem(nm + ("_pta" if r % 2 else "_ptd")), since(nm + ("_pta" if r % 2 else "_ptd"), r // 2))
                        for kb in range(b + 1):
                            last = pe.transpose(ps[:, 4 + r % 2, P * kb:P * kb + P], pb[:, r % 3, P * kb:P * kb + P], ident[:, :])
                        last.then_inc(sem(nm + "_t"), 1)
                    if s >= 2:
                        r = s - 2
                        hi_, b = r // 4, r % 4
                        pe.wait_ge(sem(nm + ("_pta" if r % 2 else "_ptd")), since(nm + ("_pta" if r % 2 else "_ptd"), r // 2 + 1))
                        if b == 0 and hi_ >= 2:
                            pe.wait_ge(sem(nm + "_o"), since(nm + "_o", hi_ - 1))
                        for kb in range(b + 1):
                            last = pe.matmul(ps[:, 6 + hi_ % 2, DH * b:DH * b + DH], tb[:, r % 3, P * kb:P * kb + P],
                                             heads[hi_]["v"](kb), start=(kb == 0), stop=(kb == b))
                        last.then_inc(sem(nm + "_pv"), 1)

            pe.wait_ge(sem("ident_in"), 16)
            pe.wait_ge(sem("ones_ok"), 1)
            pe.wait_ge(sem("vec_in"), 16 * (len(VROWS) + 2))
            pe.transpose(ps[:, 4, 0:NV], vrow[0:NV, 0, :], ident[0:NV, 0:NV])
            pe.transpose(ps[:, 4, NV:NV + 32], vrow[0:32, 1, :], ident[0:32, 0:32]).then_inc(sem("vec_t"), 1)
            pe.wait_ge(sem("x_in"), 16)
            for k in range(KD):
                if k >= 2:
                    pe.wait_ge(sem("xt_ev"), k - 1)
                for t in range(TT):
                    last = pe.transpose(ps[:, 2 + k % 2, P * t:P * t + P], xs[:, t, P * k:P * k + P], ident[:, :])
                last.then_inc(sem("xt_t"), 1)
            norm_stats("n1")

            def ada(n, i, b):
                pe.wait_ge(sem(f"p_in{i % RING}"), 16 * (i // RING + 1))
                for k in range(KD):
                    last = pe.matmul(ps[:, b, n:n + 1], praw[:, i % RING, P * k:P * k + P],
                                     col("c", k), start=(k == 0), stop=(k == KD - 1))
                last.then_inc(sem("p_used"), 1)
                return last
            pe.wait_ge(sem("vec_ok"), 1)
            for n in range(16):
                ada(n, n, 5)

            pe.wait_ge(sem("par"), 1)
            for i in range(7):
                last = pe.transpose(ps[:, 0, 16 * i:16 * i + 16], pv[0:16, i, :], ident[0:16, 0:16])
            for c in range(2):
                for m in range(4):
                    last = pe.transpose(ps[:, (1, 4)[c], P * m:P * m + P], craw[:, c, m, :, :].rearrange("p r n -> p (r n)"), ident[:, :])
            last.then_inc(sem("par_t"), 1)

            def ssm_chunk(qq):
                pe.wait_ge(sem("w1t"), qq + 1)
                if qq >= 1:
                    pe.wait_ge(sem("stg_ev"), 3 * qq)
                else:
                    pe.wait_ge(sem("cmp_free"), 3)
                for c in range(2):
                    for i in range(4):
                        last = pe.transpose(ps[:, 2 + c, P * i:P * i + P], w1t[:, c, i, :], ident[:, :])
                last.then_inc(sem("w1_t"), 1)
                for i in range(4):
                    for c in range(2):
                        last = pe.matmul(ps[0:32, 4, P * i:P * i + P], bpair[:, c, 4 * qq + i, :, :].rearrange("p g h -> p (g h)"),
                                         cpw[:, c, i, 0:8, :].rearrange("p j h -> p (j h)"), start=(c == 0), stop=(c == 1))
                last.then_inc(sem("kk_t"), 1)

            def compress():
                for w in range(2):
                    pe.wait_ge(sem("flat"), w + 1)
                    if w == 1:
                        pe.wait_ge(sem("hid"), 4)
                    for i in range(4):
                        pi = 16 + 4 * w + i
                        pe.wait_ge(sem(f"p_in{pi % RING}"), 16 * (pi // RING + 1))
                        for m in range(4):
                            for half in range(2):
                                last = pe.matmul(ps[:, 2 + half, 0:62],
                                                 praw[:, pi % RING, 256 * m + P * half:256 * m + P * half + P],
                                                 flat[:, w, 4 * i + m, :],
                                                 start=(i == 0 and m == 0), stop=(i == 3 and m == 3))
                        last.then_inc(sem("p_used"), 1)
                pe.wait_ge(sem("hid"), 8)
                pe.wait_ge(sem("w2_in"), 48)
                pe.wait_ge(sem("par_ev"), 3)
                for half in range(2):
                    last = pe.matmul(ps[:, 4, 0:62], w2d[:, half, :, :].rearrange("p r d -> p (r d)"),
                                     hid[:, 0, half, :, 0:NCMP], start=(half == 0), stop=(half == 1))
                pe.wait_ge(sem("hidr"), 2)
                for g in range(2):
                    for half in range(2):
                        last = pe.matmul(ps[:, 5, DH * g:DH * g + DH],
                                         hidr[:, half, g, :, :].rearrange("p r n -> p (r n)"), w2v[:, half, :],
                                         start=(half == 0), stop=(half == 1))
                last.then_inc(sem("cmp_t"), 1)

            for i in range(len(A1_COLS)):
                u, g = U_A1 + i, G_A1 + i
                if i == 0:
                    pe.wait_ge(sem("par_ev"), 3)
                unit_ready(u)
                bank_free(g)
                if A1_COLS[i] in (C_VS, C_VW):
                    for t in range(TT):
                        for k in range(KD):
                            last = mm3(ps[:, bank(g), P * t:P * t + P], hhi[:, k, P * t:P * t + P], hlo[:, k, P * t:P * t + P],
                                       whi[:, slot(u), P * k:P * k + P], wlo[:, slot(u), P * k:P * k + P], k == 0, k == KD - 1)
                else:
                    last = dense(u, g, hhi, hlo, ready="n1_lo" if i == 0 else None)
                last.then_inc(sem("tile"), 1)
                if i == 3:
                    compress()
                if i >= 4:
                    for n in range(3 * (i - 4), min(3 * (i - 4) + 3, 32)):
                        ada(n, n + 24, 6)
                if i in (7, 9, 11, 13):
                    ssm_chunk((i - 7) // 2)
            u, g = U_TAIL, G_A1 + 15
            unit_ready(u)
            bank_free(g)
            dense(u, g, hhi, hlo).then_inc(sem("tile"), 1)
            pe.wait_ge(sem("zg"), 1)
            pe.wait_ge(sem("stg_ev"), 12)
            for t in range(TT):
                last = pe.transpose(ps[:, 2, 24 * t:24 * t + 24], zg[0:24, P * t:P * t + P], ident[0:24, 0:24])
            last.then_inc(sem("gate_t"), 1)
            pe.wait_ge(sem("modc"), 2)
            norm_stats("ncq")
            for h in range(HEADS):
                u, g = U_UQ + h // 2, G_UQ + h
                if h % 2 == 0:
                    unit_ready(u)
                bank_free(g)
                dense(u, g, cqhi, cqlo, kt=3, off=P * (h % 2), stride=2 * P,
                      ready="ncq_lo" if h == 0 else None).then_inc(sem("tile"), 1)
                if h == 0:
                    pe.wait_ge(sem("ncq_lo"), since("ncq_lo", 3))
                    norm_stats("nckv")
            u = U_UK
            unit_ready(u)
            for i in range(4):
                g = G_UK + i
                bank_free(g)
                dense(u, g, ckhi, cklo, kt=2, off=P * i, stride=512,
                      ready="nckv_lo" if i == 0 else None).then_inc(sem("tile"), 1)
            u = U_UV
            unit_ready(u)
            for t in range(TT):
                g = G_UV + t
                bank_free(g)
                for k in range(2):
                    last = mm3(ps[:, bank(g), :], ckhi[:, k, P * t:P * t + P], cklo[:, k, P * t:P * t + P],
                               whi[:, slot(u), 512 * k:512 * k + 512], wlo[:, slot(u), 512 * k:512 * k + 512], k == 0, k == 1)
                last.then_inc(sem("tile"), 1)
            last = None
            pe.wait_ge(sem("gates"), 1)
            for b in range(TT):
                for h in range(HEADS):
                    r = slice(64 * (h % 2), 64 * (h % 2) + 64)
                    c = 32 * (4 * b + h // 2)
                    last = pe.matmul(ps[:, 2 + h % 2, c:c + NCMP], qT[r, h // 2, P * b:P * b + P], kcT[r, h // 4, :],
                                     start=True, stop=True)
            last.then_inc(sem("cs_t"), 1)
            pe.wait_ge(sem("cp"), 1)
            for b in range(TT):
                for g in range(2):
                    last = pe.transpose(ps[:, 4 + b // 2, P * (2 * (b % 2) + g):P * (2 * (b % 2) + g) + P],
                                        cp[:, 8 * b + 4 * g:8 * b + 4 * g + 4, :].rearrange("p h n -> p (h n)"), ident[:, :])
            last.then_inc(sem("cp_t"), 1)
            pe.wait_ge(sem("cpt"), 2)
            for b in range(TT):
                for g in range(2):
                    last = pe.matmul(ps[:, (6, 7, 2, 3)[b], 256 * g:256 * g + 256],
                                     cpt[:, 2 * b + g, :], vblk[:, g, :, :].rearrange("p h d -> p (h d)"), start=True, stop=True)
            last.then_inc(sem("oc_t"), 1)
            pe.wait_ge(sem("oc_ev"), 2)
            attention("nsa")
            pe.wait_ge(sem("nsa_o"), since("nsa_o", 16))
            attention("mla")

            pe.wait_ge(sem("mla_o"), since("mla_o", 8))
            for i in range(8):
                src = (onsa, omla)[i // 4]
                if i >= 2:
                    pe.wait_ge(sem("ot_lo"), i - 1)
                for t in range(TT):
                    last = pe.transpose(ps[:, 4 + i % 2, P * t:P * t + P], src[:, t, P * (i % 4):P * (i % 4) + P], ident[:, :])
                last.then_inc(sem("ot_t"), 1)
            for n in range(KD):
                for j in range(2):
                    u, g = U_Y + 3 * n + j, G_Y + 4 * n + j
                    unit_ready(u)
                    bank_free(g)
                    dense(u, g, hhi, hlo).then_inc(sem("tile"), 1)
                u = U_Y + 3 * n + 2
                unit_ready(u)
                for j in range(2):
                    g = G_Y + 4 * n + 2 + j
                    bank_free(g)
                    if n == 0 and j == 0:
                        pe.wait_ge(sem("ot_lo"), 8)
                    dense(u, g, othi, otlo, kt=4, off=512 * j, first=4 * j).then_inc(sem("tile"), 1)

            def dense_loop(u0, g0, n, hi, lo, ready=None):
                with loop(pe, n // RING) as i:
                    for j in range(RING):
                        pe.wait_ge(sem("w_lo"), u0 + RING * i + j + 1)
                        freed(pe, g0 + j - 2, i)
                        if ready and j == 0:
                            pe.wait_ge(sem(ready[0]), since(*ready))
                        dense(u0 + j, g0 + j, hi, lo).then_inc(sem("tile"), 1)

            dense_loop(U_OUT, G_OUT, KD, yhi, ylo, ("y_lo", KD))
            norm_stats("n2")
            dense_loop(U_FC1, G_FC1, NF1, hhi, hlo, ("n2_lo", KD))

            def rows_acc(u0, n, nm, natural, g_last):
                freed(pe, g_last - 1)
                freed(pe, g_last)

                def step(j, idx, start, stop):
                    pe.wait_ge(sem("w_lo"), u0 + idx + 1)
                    pe.wait_ge(sem(nm + "_lo"), since(nm + "_lo", idx + 1))
                    u, f = u0 + j, j % 2
                    for b in range(8):
                        if natural:
                            t, c = b // 2, 512 * (b % 2)
                            last = mm3(ps[:, b, :], fhi[:, f, P * t:P * t + P], flo[:, f, P * t:P * t + P],
                                       whi[:, slot(u), c:c + 512], wlo[:, slot(u), c:c + 512], start, stop)
                        else:
                            last = mm3(ps[:, b, :], whi[:, slot(u), P * b:P * b + P], wlo[:, slot(u), P * b:P * b + P],
                                       fhi[:, f, :], flo[:, f, :], start, stop)
                    last.then_inc(sem(nm + "_used"), 1)
                for j in range(2):
                    step(j, j, j == 0, False)
                turns = (n - 4) // 4
                with loop(pe, turns) as i:
                    for j in range(4):
                        step(2 + j, 4 * i + 2 + j, False, False)
                for j in range(2 + 4 * turns, n):
                    step(j, j, False, j == n - 1)

            rows_acc(U_FC2, NF1, "f1", False, G_FC1 + NF1 - 1)
            pe.wait_ge(sem("fc2_evac"), 8)
            norm_stats("nf")
            pe.wait_ge(sem("xf"), KD)
            norm_stats("n3")
            dense_loop(U_IN2, G_IN2, 8, hhi, hlo, ("n3_lo", KD))
            pe.wait_ge(sem("u_in"), 16 * SSM_L)
            pe.wait_ge(sem("w1s_in"), 16)
            for c in range(2):
                for g in range(32):
                    q, r = g // 2, slice(64 * (g % 2), 64 * (g % 2) + 64)
                    last = pe.matmul(ps[r, 2 + 2 * c + q // 8, SSM_C * (q % 8):SSM_C * (q % 8) + SSM_C],
                                     w1s[:, c, q, r], ug[:, g, :], start=True, stop=True)
            last.then_inc(sem("s_done"), 1)
            dense_loop(U_IN2 + 8, G_IN2 + 8, 4, hhi, hlo)
            pe.wait_ge(sem("s_ev"), 4)
            for i in range(4):
                u = U_V2 + i
                unit_ready(u)
                for t in range(TT):
                    for k in range(2):
                        last = mm3(ps[:, 2 + t, :], hhi[:, 2 * i + k, P * t:P * t + P], hlo[:, 2 * i + k, P * t:P * t + P],
                                   whi[:, slot(u), 512 * k:512 * k + 512], wlo[:, slot(u), 512 * k:512 * k + 512],
                                   i == 0 and k == 0, i == 3 and k == 1)
                last.then_inc(sem("v2_t"), 1)
            pe.wait_ge(sem("v2_ev"), 4)
            pe.wait_ge(sem("xst"), 2)
            pe.wait_ge(sem("w2s_in"), 16)
            pe.wait_ge(sem("t_in"), 16 * 2 * SSM_L)
            for g in range(32):
                q, r = g // 2, slice(64 * (g % 2), 64 * (g % 2) + 64)
                o = ps[:, 2 + 2 * (g % 2) + q // 8, SSM_C * (q % 8):SSM_C * (q % 8) + SSM_C]
                pe.matmul(o, w2s[r, 0, q, :], sB[r, q, :], start=True, stop=False)
                pe.matmul(o, w2s[r, 1, q, :], sA[r, q, :], start=False, stop=False)
                last = pe.matmul(o, tmat[:, g, :], ug[:, g, :], start=False, stop=True)
            last.then_inc(sem("ssm_y"), 1)
            pe.wait_ge(sem("yg_ev"), 4)
            attention("chk")
            for i in range(4):
                u, g = U_GLU + i // 2, G_GLU + i
                unit_ready(u)
                bank_free(g)
                if i == 0:
                    pe.wait_ge(sem("g_lo"), 4)
                dense(u, g, ghi, glo, kt=4, off=P * (i % 2), stride=2 * P).then_inc(sem("tile"), 1)
            for i in range(4):
                if i >= 2:
                    pe.wait_ge(sem("ya_hb"), i - 1)
                for t in range(TT):
                    if i == 0:
                        pe.wait_ge(sem("ya_n"), t + 1)
                    last = pe.transpose(ps[:, 4 + i % 2, P * t:P * t + P], yatt[:, t, P * i:P * i + P], ident[:, :])
                last.then_inc(sem("ya_t"), 1)
            pe.wait_ge(sem("chk_o"), since("chk_o", 8))
            norm_stats("nssm")
            dense_loop(U_OUT2, G_OUT2, KD, hhi, hlo, ("nssm_lo", 4))
            norm_stats("n4")
            for t in range(TT):
                for half in range(2):
                    i = 2 * t + half
                    if i >= 4:
                        pe.wait_ge(sem("xn_ev"), i - 3)
                    for k in range(4):
                        last = pe.transpose(ps[:, 2 + i % 4, P * k:P * k + P], xT[:, 4 * half + k, P * t:P * t + P], ident[:, :])
                    last.then_inc(sem("xn_t"), 1)
            dense_loop(U_GU, G_GU, 2 * NF2, hhi, hlo, ("n4_lo", KD))
            pe.wait_ge(sem("xn_ev"), 8)
            rows_acc(U_DN, NF2, "f2", True, G_GU + 2 * NF2 - 1)

        @block.scalar
        def _(act):
            A = act.activation

            def split_hi(u):
                act.wait_ge(sem(f"w_in{slot(u)}"), 16 * w_count(u))
                if u >= RING:
                    name, value = used(u - RING)
                    act.wait_ge(sem(name), value)
                A(whi[:, slot(u), :], wraw[:, slot(u), :], ACT.Copy).then_inc(sem("w_hi"), 1)

            def split_hi_turn(u, i, name, value):
                act.wait_ge(sem(f"w_in{slot(u)}"), 16 * w_count(u) + 16 * i)
                act.wait_ge(sem(name), value)
                A(whi[:, slot(u), :], wraw[:, slot(u), :], ACT.Copy).then_inc(sem("w_hi"), 1)

            def ssm_out(qq):
                act.wait_ge(sem("w1t"), qq + 1)
                for c in range(2):
                    act.dma_start(scr["w2"][c, :, 4 * qq:4 * qq + 4, :],
                                  cpw[:, c, :, 1:9, :].rearrange("p q j h -> p q (j h)")).then_inc(sem("w2_out"), 16)
                act.wait_ge(sem("w1_t"), qq + 1)
                if qq >= 1:
                    act.wait_ge(sem("w1_out"), 32 * qq)
                    act.wait_ge(sem("kk_out"), 16 * qq)
                for c in range(2):
                    A(stg[:, c, :, :].rearrange("p q n -> p (q n)"), ps[:, 2 + c, :], ACT.Copy).then_inc(sem("stg_ev"), 1)
                act.wait_ge(sem("kk_t"), qq + 1)
                A(kst[0:32, :, :].rearrange("p g n -> p (g n)"), ps[0:32, 4, :], ACT.Copy).then_inc(sem("stg_ev"), 1)
                act.wait_ge(sem("stg_ev"), 3 * qq + 3)
                for c in range(2):
                    act.dma_start(scr["w1"][c, :, 4 * qq:4 * qq + 4, :], stg[:, c, :, :]).then_inc(sem("w1_out"), 16)
                act.dma_start(scr["kk"][:, 4 * qq:4 * qq + 4, :], kst[0:32, :, :]).then_inc(sem("kk_out"), 16)

            def nxt(u):
                if u + AHEAD < U_END:
                    split_hi(u + AHEAD)

            def norm_squares(nm, waits=None):
                src, n, buf = NORM[nm]
                for k in range(n):
                    if waits:
                        waits(k)
                    A(buf[:, k, :], src(k), ACT.Square).then_inc(sem(nm + "_sq"), 1)
                act.wait_ge(sem(nm + "_ms"), since(nm + "_ms", 1))
                A(stat[:, 1, :], stat[:, 0, :], ACT.Sqrt).then_inc(sem(nm + "_rt"), 1)

            def norm_hi(nm):
                hi = AFTER[nm][2]
                for k in range(NORM[nm][1]):
                    act.wait_ge(sem(nm + "_h"), since(nm + "_h", k + 1))
                    A(hi[:, k, :], hb[:, k % 2, :], ACT.Copy).then_inc(sem(nm + "_hi"), 1)

            def copy_out(dst, src, g, last=True):
                act.wait_ge(sem("tile"), g + 1)
                e = A(dst, src, ACT.Copy)
                return free(e, g) if last else e

            def attention(nm):
                heads, sb, pb, tb = ATT[nm]
                N = 4 * len(heads)
                for s in range(N + 1):
                    if s < N:
                        hd, b = heads[s // 4], s % 4
                        w = P * (b + 1)
                        act.wait_ge(sem(nm + "_s"), since(nm + "_s", s + 1))
                        if s >= 3:
                            act.wait_ge(sem(nm + "_t"), since(nm + "_t", s - 2))
                        if b == 0 and s >= 8:
                            act.wait_ge(sem(nm + "_o"), since(nm + "_o", s // 4 - 1))
                        A(pb[:, s % 3, 0:w], sb[:, s % 2, 0:w], ACT.Exp, bias=smax[:, s % 4:s % 4 + 1], scale=-1.0,
                          accum_out=rsum[:, (s // 4) % 2, b:b + 1]).then_inc(sem(nm + "_p"), 1)
                    r = s - 1
                    if r >= 0 and r % 2:
                        w = P * (r % 4 + 1)
                        act.wait_ge(sem(nm + "_t"), since(nm + "_t", r + 1))
                        if r >= 3:
                            act.wait_ge(sem(nm + "_pv"), since(nm + "_pv", r - 2))
                        A(tb[:, r % 3, 0:w], ps[:, 4 + r % 2, 0:w], ACT.Copy).then_inc(sem(nm + "_pta"), 1)

            act.dma_start(ident[:], a["identity"]).then_inc(sem("ident_in"), 16)
            for name, (r, n) in VROWS.items():
                v = a[name]
                act.dma_start(vrow[r:r + n, 0, :], bass.AP(v.tensor, 0, [[P, n], [1, P]])).then_inc(sem("vec_in"), 16)
            for i, name in enumerate(("pe_ck", "pe_cv")):
                act.dma_start(vrow[16 * i:16 * i + 16, 1, :], bass.AP(a[name].tensor, 0, [[P, 16], [1, P]])).then_inc(sem("vec_in"), 16)
            for i, name in enumerate(("ssm_lam_re_2", "ssm_lam_im_2")):
                act.dma_start(pv[0:16, 20 + i, :], bass.AP(a[name].tensor, 0, [[P, 16], [1, P]])).then_inc(sem("par_in"), 16)
            act.dma_start(dtl[0:16, 0, :], bass.AP(a["ssm_log_dt_2"].tensor, 0, [[2, 16], [1, 2]])).then_inc(sem("par_in"), 16)
            for i, name in enumerate(("ssm_b_re_2", "ssm_b_im_2")):
                act.dma_start(braw[:, i, :, :], a[name][0].rearrange("(q g) p h -> (g p) q h", g=2)).then_inc(sem("par_in"), 16)
            for i, name in enumerate(("ssm_c_re_2", "ssm_c_im_2")):
                for r in range(2):
                    act.dma_start(craw[:, i, :, r, :],
                                  bass.AP(a[name].tensor, 0, [[64, P], [64 * P, 4], [1, 64]])).then_inc(sem("par_in"), 16)
            for r in range(2):
                act.dma_start(w2d[:, :, r, :], a["w_ck2"][0].rearrange("(k p) n -> p k n", p=P)).then_inc(sem("w2_in"), 16)
            act.dma_start(w2v[:], a["w_cv2"][0].rearrange("(k p) n -> p k n", p=P)).then_inc(sem("w2_in"), 16)
            act.dma_start(rel[0:8, 383:640], a["attn_rel_bias_2"][0]).then_inc(sem("rel_in"), 16)

            for k in range(KD):
                act.wait_ge(sem("xt_t"), k + 1)
                A(xT[:, k, :], ps[:, 2 + k % 2, :], ACT.Copy).then_inc(sem("xt_ev"), 1)
            norm_squares("n1", lambda k: act.wait_ge(sem("xt_ev"), k + 1))
            act.wait_ge(sem("rel_ok"), 1)
            act.dma_start(scr["rel"], rel[0:8, :]).then_inc(sem("rel_out"), 16)
            for u in range(AHEAD):
                split_hi(u)
            norm_hi("n1")
            for i in range(len(A1_COLS)):
                u, g, c = U_A1 + i, G_A1 + i, A1_COLS[i]
                nxt(u)
                if c in (C_KC, C_VC):
                    w = i
                    act.wait_ge(sem("tile"), g + 1)
                    if w == 0:
                        act.wait_ge(sem("n1_st"), since("n1_st", 1))
                    for gr in range(2):
                        A(x2[0:64, w, gr, :], ps[64 * gr:64 * gr + 64, bank(g), :], ACT.Copy).then_inc(sem("x2"), 1)
                        e = A(x2[64:128, w, gr, 0:T - 1], ps[64 * gr:64 * gr + 64, bank(g), 1:T], ACT.Copy)
                        e.then_inc(sem("x2"), 1) if gr == 0 else free(e, g)
                elif c in (C_VS, C_VW):
                    br = 0 if c == C_VS else 1
                    copy_out(vnat[:, :, br, :], ps[:, bank(g), :].rearrange("p (t n) -> p t n", t=TT), g)
                elif C_Q <= c < 512:
                    copy_out(qT[:, c // P, :], ps[:, bank(g), :], g)
                elif c >= C_QD:
                    j = i - 10
                    if j == 0:
                        act.wait_ge(sem("cmp_free"), 3)
                    copy_out(zl[:, j, :], ps[:, bank(g), :], g)
                if i == 3:
                    for w in range(2):
                        act.wait_ge(sem("p_used"), 16 + 4 * (w + 1))
                        for half in range(2):
                            for gr in range(2):
                                A(hid[:, w, half, gr, 0:NCMP], ps[:, 2 + half, NCMP * gr:NCMP * gr + NCMP],
                                  ACT.Silu).then_inc(sem("hid"), 1)
                    act.wait_ge(sem("cmp_t"), 1)
                    A(kcT[:].rearrange("p g n -> p (g n)"), ps[:, 4, 0:62], ACT.Copy).then_inc(sem("cmp_free"), 1)
                if i in (8, 10, 12):
                    ssm_out((i - 8) // 2)
            ssm_out(3)
            nxt(U_TAIL)
            act.wait_ge(sem("tile"), G_A1 + 16)
            A(zg[0:24, :], ps[0:24, bank(15), :], ACT.Sigmoid).then_inc(sem("zg"), 1)
            freed(act, 13)
            freed(act, 14)
            act.wait_ge(sem("kk_out"), 64)
            norm_squares("ncq")
            norm_hi("ncq")
            act.wait_ge(sem("w1_out"), 128)
            act.wait_ge(sem("w2_out"), 128)
            act.wait_ge(sem("gate_t"), 1)
            for h in range(HEADS):
                u, g = U_UQ + h // 2, G_UQ + h
                if h % 2 == 0:
                    nxt(u)
                copy_out(qm[0:64, h, :], ps[0:64, bank(g), :], g, last=False).then_inc(sem("qm"), 1)
                if h == 0:
                    norm_squares("nckv")
                    norm_hi("nckv")
            nxt(U_UK)
            for i in range(4):
                g = G_UK + i
                if i == 0:
                    act.wait_ge(sem("nckv_lo"), since("nckv_lo", 2))
                copy_out(km[0:64, 2 * i, :], ps[0:64, bank(g), :], g, last=False)
                free(A(km[0:64, 2 * i + 1, :], ps[64:128, bank(g), :], ACT.Copy), g)
            nxt(U_UV)
            for t in range(TT):
                g = G_UV + t
                copy_out(vm[:, t, :], ps[:, bank(g), :], g)
            act.wait_ge(sem("cs"), 1)
            A(cp[:, :, 0:NCMP], cs[:, :, :], ACT.Exp, scale=DH ** -0.5).then_inc(sem("ce"), 1)
            act.wait_ge(sem("cp_t"), 1)
            A(cpt[:, 0:4, :].rearrange("p b n -> p (b n)"), ps[:, 4, :], ACT.Copy).then_inc(sem("cpt"), 1)
            act.wait_ge(sem("oc_t"), 1)
            A(onsa[:, 0, :], ps[:, 6, :], ACT.Copy)
            A(onsa[:, 1, :], ps[:, 7, :], ACT.Copy).then_inc(sem("oc_ev"), 1)
            attention("nsa")
            attention("mla")
            for i in range(8):
                act.wait_ge(sem("ot_t"), i + 1)
                A(othi[:, i, :], ps[:, 4 + i % 2, :], ACT.Copy).then_inc(sem("ot_hi"), 1)
            for n in range(KD):
                for j in range(2):
                    u, g = U_Y + 3 * n + j, G_Y + 4 * n + j
                    nxt(u)
                    act.wait_ge(sem("tile"), g + 1)
                    if n >= 1:
                        freed(act, g - 2)
                    free(A(sg[:, j, :], ps[:, bank(g), :], ACT.Sigmoid), g)
                nxt(U_Y + 3 * n + 2)
                act.wait_ge(sem("y"), n + 1)
                A(yhi[:, n, :], ym[:, 2, :], ACT.Copy).then_inc(sem("y_hi"), 1)

            def hi_loop(u0, g0, n, evac):
                with loop(act, n // RING) as i:
                    for j in range(RING):
                        split_hi_turn(u0 + j + AHEAD, i, "tile", g0 + RING * i + j)
                        evac(i, j)
            hi_loop(U_OUT, G_OUT, KD, lambda i, j: None)
            norm_squares("n2", lambda k: freed(act, G_OUT + k))
            norm_hi("n2")

            def relu(i, j):
                g = G_FC1 + j
                act.wait_ge(sem("tile"), G_FC1 + RING * i + j + 1)
                act.wait_ge(sem("ff"), RING * i + j + 1)
                free(A(rb[:, j % 2, :], ps[:, bank(g), :], ACT.Relu), g)
            hi_loop(U_FC1, G_FC1, NF1, relu)

            def f_hi(nm, j, idx, counted):
                if counted:
                    act.wait_ge(sem(nm + "_used"), since(nm + "_used", idx - 1))
                A(fhi[:, j % 2, :], ff[:, idx, :] if isinstance(idx, int) else ff[:, bass.ds(idx, 1), :].rearrange("p a t -> p (a t)"),
                  ACT.Copy).then_inc(sem(nm + "_hi"), 1)

            def rows_hi(u0, n, nm):
                for j in range(2):
                    f_hi(nm, j, j, False)
                    split_hi(u0 + j + AHEAD)
                turns = (n - 4) // 4
                with loop(act, turns) as i:
                    for j in range(4):
                        f_hi(nm, j, 4 * i + 2 + j, True)
                        split_hi_turn(u0 + 2 + j + AHEAD, i, nm + "_used", 4 * i + 2 + j)
                for j in range(2 + 4 * turns, n):
                    f_hi(nm, j, j, True)
                    if u0 + j + AHEAD < U_END:
                        split_hi(u0 + j + AHEAD)
            act.wait_ge(sem("ff"), NF1 + 2)
            rows_hi(U_FC2, NF1, "f1")
            norm_squares("nf", lambda k: act.wait_ge(sem("fc2_evac"), k + 1))
            norm_squares("n3", lambda k: act.wait_ge(sem("xf"), k + 1))
            norm_hi("n3")
            for i in range(12):
                u, g = U_IN2 + i, G_IN2 + i
                nxt(u)
                if i < 4:
                    act.wait_ge(sem("tile"), g + 1)
                    free(A(uT[:, i, :, :].rearrange("p j c -> p c j"), ps[:, bank(g), :].rearrange("p (c j) -> p c j", j=SSM_L),
                           ACT.Copy), g)
                else:
                    copy_out((q2, k2)[(i - 4) // 4][:, i % 4, :], ps[:, bank(g), :], g)
                if i == 8:
                    act.wait_ge(sem("s_done"), 1)
                    for c in range(2):
                        for half in range(2):
                            A((sA, sB)[c][:, 8 * half:8 * half + 8, :].rearrange("p q c -> p (q c)"), ps[:, 2 + 2 * c + half, :],
                              ACT.Copy).then_inc(sem("s_ev"), 1)
            for i in range(4):
                nxt(U_V2 + i)
            act.wait_ge(sem("v2_t"), 4)
            for t in range(TT):
                A(v2[:, t, :], ps[:, 2 + t, :], ACT.Copy).then_inc(sem("v2_ev"), 1)
            for m in range(4):
                act.wait_ge(sem("ssm_y"), 1)
                A(yg[:, 16 * (m % 2) + m // 2:16 * (m % 2) + 16:2, :], ps[:, 2 + m, :].rearrange("p (q c) -> p q c", q=8),
                  ACT.Copy).then_inc(sem("yg_ev"), 1)
            attention("chk")
            for m in range(4):
                act.wait_ge(sem("yk"), m + 1)
                A(ygel[:, m, :].rearrange("p (c j) -> p c j", j=SSM_L), yssm[:, m, :, :].rearrange("p j c -> p c j"),
                  ACT.Gelu_apprx_tanh).then_inc(sem("gel"), 1)
            for m in range(4):
                act.wait_ge(sem("gel"), m + 1)
                A(ghi[:, m, :], ygel[:, m, :], ACT.Copy).then_inc(sem("g_hi"), 1)
            for i in range(4):
                g = G_GLU + i
                if i % 2 == 0:
                    nxt(U_GLU + i // 2)
                act.wait_ge(sem("tile"), g + 1)
                free(A(ysg[:, i, :], ps[:, bank(g), :], ACT.Sigmoid, bias=col("ssm_b_glu_2", i)), g)
            for t in range(TT):
                A(hb[:, t % 2, :], yatt[:, t, :], ACT.Square, accum_out=stat[:, 2, t:t + 1]).then_inc(sem("ya_sq"), 1)
                act.wait_ge(sem("ya_sq"), t + 1)
            act.wait_ge(sem("ya_ms"), 1)
            A(stat[:, 4, :], stat[:, 3, :], ACT.Sqrt).then_inc(sem("ya_rt"), 1)
            for i in range(4):
                act.wait_ge(sem("ya_hb"), i + 1)
                A(hhi[:, 4 + i, :], hb[:, i % 2, :], ACT.Copy).then_inc(sem("ya_hi"), 1)
            norm_squares("nssm", lambda k: act.wait_ge(sem("ysg"), k + 1))
            norm_hi("nssm")
            hi_loop(U_OUT2, G_OUT2, KD, lambda i, j: None)
            norm_squares("n4", lambda k: freed(act, G_OUT2 + k))
            norm_hi("n4")
            for i in range(8):
                act.wait_ge(sem("xn_t"), i + 1)
                A(xn[:, i // 2, 512 * (i % 2):512 * (i % 2) + 512], ps[:, 2 + i % 4, :], ACT.Copy).then_inc(sem("xn_ev"), 1)

            def silu(i, j):
                if j % 2 == 0:
                    g = G_GU + j
                    act.wait_ge(sem("tile"), G_GU + RING * i + j + 1)
                    freed(act, G_GU + j + 1 - RING, i)
                    free(A(rb[:, j // 2, :], ps[:, bank(g), :], ACT.Silu), g)
            hi_loop(U_GU, G_GU, 2 * NF2, silu)
            freed(act, G_GU + 2 * NF2 - 1)
            rows_hi(U_DN, NF2, "f2")
            for t in range(TT):
                act.wait_ge(sem("xo"), 2 * t + 2)
                A(ff[:, 2 * (t % 2):2 * (t % 2) + 2, :].rearrange("p a b -> p (a b)"), xn[:, t, :], ACT.Square,
                  accum_out=stat[:, 5, t:t + 1]).then_inc(sem("fin_sq"), 1)
                act.wait_ge(sem("fin_ms"), t + 1)
                A(stat[:, 6, t:t + 1], stat[:, 7, t:t + 1], ACT.Sqrt).then_inc(sem("fin_rt"), 1)

        @block.vector
        def _(dve):
            chain = [0]

            def link(i):
                chain[0] += 1
                i.then_inc(sem("dve_chain"), 1)
                dve.wait_ge(sem("dve_chain"), chain[0])

            TTo, TS, STT, CP = dve.tensor_tensor, dve.tensor_scalar, dve.scalar_tensor_tensor, dve.tensor_copy

            def split_lo(u):
                dve.wait_ge(sem("w_hi"), u + 1)
                TTo(out=wlo[:, slot(u), :], in0=wraw[:, slot(u), :], in1=whi[:, slot(u), :].bitcast(F32),
                    op=ALU.subtract).then_inc(sem("w_lo"), 1)

            def nxt(u):
                if u + AHEAD < U_END:
                    split_lo(u + AHEAD)

            def norm_rsqrt(nm, width):
                dve.wait_ge(sem(nm + "_st"), since(nm + "_st", 1))
                TS(stat[:, 0, :], ps[:, 6, 0:4], 1.0 / width, EPS, ALU.mult, ALU.add).then_inc(sem(nm + "_ms"), 1)
                dve.wait_ge(sem(nm + "_rt"), since(nm + "_rt", 1))
                link(dve.reciprocal(stat[:, 0, :], stat[:, 1, :]))
                for t in range(TT):
                    TS(diag[:, P * t:P * t + P], ident[:, :], stat[:, 0, t:t + 1], None, ALU.mult).then_inc(sem(nm + "_dg"), 1)

            def norm_apply(nm):
                src, n, _ = NORM[nm]
                mul, add, hi, lo = AFTER[nm]
                dve.wait_ge(sem(nm + "_r"), since(nm + "_r", 1))
                for k in range(n + 1):
                    if k < n:
                        if k >= 2:
                            dve.wait_ge(sem(nm + "_lo"), since(nm + "_lo", k - 1))
                        link(TTo(out=hb[:, k % 2, :], in0=src(k), in1=ps[:, 7, :], op=ALU.mult))
                        if add is None:
                            TS(hb[:, k % 2, :], hb[:, k % 2, :], mul(k), None, ALU.mult).then_inc(sem(nm + "_h"), 1)
                        else:
                            TS(hb[:, k % 2, :], hb[:, k % 2, :], mul(k), add(k), ALU.mult, ALU.add).then_inc(sem(nm + "_h"), 1)
                    if k >= 1:
                        dve.wait_ge(sem(nm + "_hi"), since(nm + "_hi", k))
                        TTo(out=lo[:, k - 1, :], in0=hb[:, (k - 1) % 2, :], in1=hi[:, k - 1, :].bitcast(F32),
                            op=ALU.subtract).then_inc(sem(nm + "_lo"), 1)
                dve.wait_ge(sem(nm + "_lo"), since(nm + "_lo", n))

            def attention(nm):
                heads, sb, pb, tb = ATT[nm]
                N = 4 * len(heads)
                for s in range(N + 4):
                    if s < N:
                        hd, b = heads[s // 4], s % 4
                        w = P * (b + 1)
                        if hd["rescale"] and b == 0:
                            link(TS(bias[:].rearrange("p h n -> p (h n)"), bias[:].rearrange("p h n -> p (h n)"), 1.0 / 16.0, None, ALU.mult))
                        dve.wait_ge(sem(nm + "_qk"), since(nm + "_qk", s + 1))
                        if s >= 2:
                            dve.wait_ge(sem(nm + "_p"), since(nm + "_p", s - 1))
                        dve.tensor_tensor_reduce(out=sb[:, s % 2, 0:w], in0=ps[:, 2 + s % 2, 0:w], in1=hd["bias"][:, T - w:T],
                                                 scale=-hd["scale"], scalar=3e38, op0=ALU.add, op1=ALU.min,
                                                 accum_out=smax[:, s % 4:s % 4 + 1]).then_inc(sem(nm + "_s"), 1)
                    r = s - 2
                    if 0 <= r < N and r % 2 == 0:
                        w = P * (r % 4 + 1)
                        dve.wait_ge(sem(nm + "_t"), since(nm + "_t", r + 1))
                        if r >= 3:
                            dve.wait_ge(sem(nm + "_pv"), since(nm + "_pv", r - 2))
                        CP(tb[:, r % 3, 0:w], ps[:, 4 + r % 2, 0:w]).then_inc(sem(nm + "_ptd"), 1)
                    r = s - 4
                    if r >= 0 and r % 4 == 3:
                        finish(nm, heads, r // 4)

            def finish(nm, heads, i):
                hd = heads[i]
                dve.wait_ge(sem(nm + "_p"), since(nm + "_p", 4 * i + 4))
                dve.wait_ge(sem(nm + "_pv"), since(nm + "_pv", 4 * i + 4))
                link(dve.reciprocal(rinv[:, :], rsum[:, i % 2, :]))
                if hd["gate"] is not None:
                    link(TTo(out=rinv[:, :], in0=rinv[:, :], in1=hd["gate"], op=ALU.mult))
                pso = ps[:, 6 + i % 2, 0:4 * DH].rearrange("p (b d) -> p b d", b=4)
                rb_ = rinv[:, :].unsqueeze(2).to_broadcast([P, 4, DH])
                dst = hd["o"][:, :, DH * hd["h"]:DH * hd["h"] + DH]
                if hd["gate"] is None:
                    e = TTo(out=dst, in0=pso, in1=rb_, op=ALU.mult)
                else:
                    t_ = hb[:, 0, 0:4 * DH].rearrange("p (b d) -> p b d", b=4)
                    link(TTo(out=t_, in0=pso, in1=rb_, op=ALU.mult))
                    e = TTo(out=dst, in0=dst, in1=t_, op=ALU.add)
                e.then_inc(sem(nm + "_o"), 1)
                dve.wait_ge(sem(nm + "_o"), since(nm + "_o", i + 1))

            dve.memset(ones[:], 1.0).then_inc(sem("ones_ok"), 1)
            dve.sem_inc(sem("ff"), 2)

            def v(i):
                return pv[0:16, i, :]

            def exp_(dst, x, t, ti):
                xc, n, f, q = t
                link(TS(xc, x, -87.3, 88.7, ALU.max, ALU.min))
                link(TS(n, xc, 1.4426950408889634, 12582912.0, ALU.mult, ALU.add))
                link(TS(n, n, -12582912.0, None, ALU.add))
                link(STT(out=f, in0=n, scalar=-0.693145751953125, in1=xc, op0=ALU.mult, op1=ALU.add))
                link(STT(out=f, in0=n, scalar=-1.42860682030941723212e-6, in1=f, op0=ALU.mult, op1=ALU.add))
                link(TS(q, f, 1.0 / 5040, None, ALU.mult))
                for c in (1.0 / 720, 1.0 / 120, 1.0 / 24, 1.0 / 6, 0.5, 1.0):
                    link(STT(out=q, in0=q, scalar=c, in1=f, op0=ALU.add, op1=ALU.mult))
                link(TS(ti, n, 127.0, 8388608.0, ALU.add, ALU.mult))
                link(STT(out=dst, in0=q, scalar=1.0, in1=ti.bitcast(F32), op0=ALU.add, op1=ALU.mult))

            def double(s, c1, t):
                link(STT(out=t, in0=c1, scalar=1.0, in1=s, op0=ALU.add, op1=ALU.mult))
                link(STT(out=c1, in0=s, scalar=-2.0, in1=s, op0=ALU.mult, op1=ALU.mult))
                link(TS(s, t, 2.0, None, ALU.mult))

            dve.wait_ge(sem("par_in"), 16 * 9)
            d = [dtl[0:16, i, :] for i in range(8)]
            exp_(d[1], d[0], d[2:6], dti[0:16, :])
            lre, lim = v(20), v(21)

            def by_dt(o, x):
                link(TTo(out=o.rearrange("q (g p) -> q g p", g=2), in0=x.rearrange("q (g p) -> q g p", g=2),
                         in1=d[1].unsqueeze(2).to_broadcast([16, 2, 64]), op=ALU.mult))
            by_dt(v(8), lre)
            by_dt(v(9), lim)
            exp_(v(10), v(8), [v(11), v(12), v(13), v(14)], pvi[0:16, :])
            link(TS(v(11), v(9), 0.15915494309189535, 12582912.0, ALU.mult, ALU.add))
            link(TS(v(11), v(11), -12582912.0, None, ALU.add))
            for c in (6.28125, 0.0019350051879882812, 3.0199159819567e-07):
                link(STT(out=v(9), in0=v(11), scalar=-c, in1=v(9), op0=ALU.mult, op1=ALU.add))
            link(TS(v(9), v(9), 0.125, None, ALU.mult))
            link(TTo(out=v(12), in0=v(9), in1=v(9), op=ALU.mult))
            link(TS(v(13), v(12), -1.0 / 5040, None, ALU.mult))
            for c in (1.0 / 120, -1.0 / 6):
                link(STT(out=v(13), in0=v(13), scalar=c, in1=v(12), op0=ALU.add, op1=ALU.mult))
            link(STT(out=v(13), in0=v(13), scalar=1.0, in1=v(9), op0=ALU.add, op1=ALU.mult))
            link(TS(v(14), v(12), 1.0 / 40320, None, ALU.mult))
            for c in (-1.0 / 720, 1.0 / 24, -0.5):
                link(STT(out=v(14), in0=v(14), scalar=c, in1=v(12), op0=ALU.add, op1=ALU.mult))
            for _i in range(3):
                double(v(13), v(14), v(15))
            link(TTo(out=v(15), in0=v(10), in1=v(14), op=ALU.mult))
            link(TTo(out=v(0), in0=v(10), in1=v(15), op=ALU.add))
            link(TTo(out=v(1), in0=v(10), in1=v(13), op=ALU.mult))
            link(STT(out=v(16), in0=v(10), scalar=-1.0, in1=v(15), op0=ALU.add, op1=ALU.add))
            link(TTo(out=v(17), in0=lre, in1=lre, op=ALU.mult))
            link(TTo(out=v(18), in0=lim, in1=lim, op=ALU.mult))
            link(TTo(out=v(17), in0=v(17), in1=v(18), op=ALU.add))
            link(dve.reciprocal(v(17), v(17)))
            link(TTo(out=v(18), in0=v(16), in1=lre, op=ALU.mult))
            link(TTo(out=v(19), in0=v(1), in1=lim, op=ALU.mult))
            link(TTo(out=v(18), in0=v(18), in1=v(19), op=ALU.add))
            link(TTo(out=v(2), in0=v(18), in1=v(17), op=ALU.mult))
            link(TTo(out=v(18), in0=v(1), in1=lre, op=ALU.mult))
            link(TTo(out=v(19), in0=v(16), in1=lim, op=ALU.mult))
            link(TTo(out=v(18), in0=v(18), in1=v(19), op=ALU.subtract))
            link(TTo(out=v(3), in0=v(18), in1=v(17), op=ALU.mult))
            link(TTo(out=v(4), in0=v(10), in1=v(10), op=ALU.mult))
            link(TTo(out=v(4), in0=v(4), in1=v(4), op=ALU.mult))
            link(TTo(out=v(4), in0=v(4), in1=v(4), op=ALU.mult))
            for _i in range(3):
                double(v(13), v(14), v(15))
            link(CP(v(5), v(14)))
            CP(v(6), v(13)).then_inc(sem("par"), 1)

            dve.wait_ge(sem("vec_t"), 1)
            CP(vcol[:, :], ps[:, 4, 0:NV + 32]).then_inc(sem("vec_ok"), 1)
            dve.wait_ge(sem("rel_in"), 16)
            link(TS(rel[0:8, 383:640], rel[0:8, 383:640], DH ** 0.5, None, ALU.mult))
            link(dve.memset(rel[0:8, 0:383], 0.0))
            TS(rel[0:8, 0:383], rel[0:8, 0:383], rel[0:8, 383:384], None, ALU.add).then_inc(sem("rel_ok"), 1)
            norm_rsqrt("n1", D)
            dve.wait_ge(sem("par_t"), 1)
            CP(apar[:].rearrange("p a q -> p (a q)"), ps[:, 0, 0:112]).then_inc(sem("par_ev"), 1)
            for c in range(2):
                for r in range(2):
                    e = CP(ctp[64 * r:64 * r + 64, c, :, :], ps[64 * r:64 * r + 64, (1, 4)[c], :].rearrange(
                        "p (q r h) -> p q r h", r=2, h=16)[:, :, r, :])
            e.then_inc(sem("par_ev"), 1)
            dve.wait_ge(sem("par_ev"), 2)
            CP(ssmc[:], apar[:, 4:7, :]).then_inc(sem("par_ev"), 1)
            dve.wait_ge(sem("p_used"), 16)
            link(TTo(out=modc[:, 0:16], in0=ps[:, 5, 0:16], in1=vcol[:, 0:16], op=ALU.add))
            STT(out=gain[:, 0, :], in0=modc[:, 8:16], scalar=1.0, in1=vcol[:, VROWS["g_mix"][0]:VROWS["g_mix"][0] + 8],
                op0=ALU.add, op1=ALU.mult).then_inc(sem("modc"), 1)
            dve.wait_ge(sem("modc"), 1)
            norm_apply("n1")
            for u in range(AHEAD):
                split_lo(u)

            def cmul(ore, oim, xre, xim, yre, yim, t1, t2, neg=False):
                link(TTo(out=t1, in0=xre, in1=yre, op=ALU.mult))
                link(TTo(out=t2, in0=xim, in1=yim, op=ALU.mult))
                link(TTo(out=ore, in0=t1, in1=t2, op=ALU.subtract))
                link(TTo(out=t1, in0=xre, in1=yim, op=ALU.mult))
                link(TTo(out=t2, in0=xim, in1=yre, op=ALU.mult))
                if neg:
                    link(STT(out=oim, in0=t1, scalar=-1.0, in1=t2, op0=ALU.mult, op1=ALU.subtract))
                else:
                    link(TTo(out=oim, in0=t1, in1=t2, op=ALU.add))

            def bc(x, n):
                return x.unsqueeze(2).to_broadcast([P, SSM_Q, n])

            def ssm_setup():
                t = [tmp[:, i, 0:256].rearrange("p (q h) -> p q h", h=16) for i in range(2)]
                cmul(bbar[:, 0], bbar[:, 1], bc(apar[:, 2, :], 16), bc(apar[:, 3, :], 16), braw[:, 0], braw[:, 1], *t)
                link(dve.memset(bpair[:], 0.0))
                for g in range(2):
                    r = slice(64 * g, 64 * g + 64)
                    for c in range(2):
                        link(CP(bpair[r, c, :, g, :], bbar[r, c, :, :]))
                link(dve.memset(pw[:, 0, :, 0:1], 1.0))
                link(dve.memset(pw[:, 1, :, 0:1], 0.0))
                link(CP(pw[:, :, :, 1:2].rearrange("p c q o -> p c (q o)"), apar[:, 0:2, :]))
                for n in (1, 2, 4):
                    t = [tmp[:, i, 0:16 * n].rearrange("p (q h) -> p q h", h=n) for i in range(2)]
                    cmul(pw[:, 0, :, n + 1:2 * n + 1], pw[:, 1, :, n + 1:2 * n + 1], pw[:, 0, :, 1:n + 1], pw[:, 1, :, 1:n + 1],
                         pw[:, 0, :, n:n + 1].to_broadcast([P, SSM_Q, n]), pw[:, 1, :, n:n + 1].to_broadcast([P, SSM_Q, n]), *t)
                for j in range(8):
                    link(CP(pwr[:, :, :, j:j + 1].rearrange("p c q o -> p c (q o)"),
                            pw[:, :, :, 7 - j:8 - j].rearrange("p c q o -> p c (q o)")))

            def ssm_products(qq):
                qs = slice(4 * qq, 4 * qq + 4)

                def b4(x, n):
                    return x.unsqueeze(3).to_broadcast([P, 4, n, 16])

                def b3(x, n):
                    return x.unsqueeze(2).to_broadcast([P, 4, n, 16])
                if qq >= 1:
                    dve.wait_ge(sem("w1_t"), qq)
                    dve.wait_ge(sem("kk_t"), qq)
                    dve.wait_ge(sem("w2_out"), 32 * qq)
                t = [tmp[:, i, 0:512].rearrange("p (q j h) -> p q j h", q=4, j=8) for i in range(2)]
                o = [w1t[:, c].rearrange("p q (j h) -> p q j h", j=8) for c in range(2)]
                cmul(o[0], o[1], b4(pwr[:, 0, qs, :], 8), b4(pwr[:, 1, qs, :], 8), b3(bbar[:, 0, qs, :], 8), b3(bbar[:, 1, qs, :], 8), *t)
                t = [tmp[:, i, :].rearrange("p (q j h) -> p q j h", q=4, j=9) for i in range(2)]
                cmul(cpw[:, 0], t[0], b4(pw[:, 0, qs, :], 9), b4(pw[:, 1, qs, :], 9), b3(ctp[:, 0, qs, :], 9), b3(ctp[:, 1, qs, :], 9), *t)
                link(TS(cpw[:, 1], t[0], -1.0, None, ALU.mult))
                dve.sem_inc(sem("w1t"), 1)

            def compress_in(w):
                dve.wait_ge(sem("x2"), 3 * (w + 1))
                freed(dve, G_A1 + w)
                for h in range(2):
                    src = x2[:, w, :, 16 * h:16 * h + 496].rearrange("p g (n b l) -> p g n b l", b=8, l=2)[:, :, :, :, 0]
                    for gr in range(2):
                        dst = flat[:, w, 8 * h:8 * h + 8, NCMP * gr:NCMP * gr + NCMP].rearrange("p b n -> p n b")
                        pe_ = vcol[:, NV + 16 * w + 8 * h:NV + 16 * w + 8 * h + 8].unsqueeze(1).to_broadcast([P, NCMP, 8])
                        TTo(out=dst, in0=src[:, gr], in1=pe_, op=ALU.add).then_inc(sem("flat_"), 1)
                dve.wait_ge(sem("flat_"), 4 * (w + 1))
                dve.sem_inc(sem("flat"), 1)

            for i in range(len(A1_COLS)):
                u, g, c = U_A1 + i, G_A1 + i, A1_COLS[i]
                nxt(u)
                if c in (C_KC, C_VC):
                    compress_in(i)
                elif c in (C_KS, C_KW):
                    br = 0 if c == C_KS else 1
                    dve.wait_ge(sem("tile"), g + 1)
                    for gr in range(2):
                        for half in range(2):
                            e = CP(kdup[64 * half:64 * half + 64, br, gr, :], ps[64 * gr:64 * gr + 64, bank(g), :])
                    free(e, g)
                if i == 3:
                    dve.memset(hidr[:, :, :, :, 31:32], 0.0).then_inc(sem("hidr"), 1)
                    dve.wait_ge(sem("hid"), 8)
                    for half in range(2):
                        for gr in range(2):
                            e = CP(hidr[:, half, gr, :, 0:NCMP], hid[:, 1, half, gr, 0:NCMP].unsqueeze(1).to_broadcast([P, 4, NCMP]))
                    e.then_inc(sem("hidr"), 1)
                    link(dve.memset(vblk[:], 0.0))
                    dve.wait_ge(sem("cmp_t"), 1)
                    for h in range(4):
                        e = CP(vblk[32 * h:32 * h + 32, :, h, :], ps[32 * h:32 * h + 32, 5, 0:2 * DH].rearrange("p (g d) -> p g d", g=2))
                    e.then_inc(sem("cmp_free"), 2)
                if i == 4:
                    ssm_setup()
                    ssm_products(0)
                if i in (8, 10, 12):
                    ssm_products((i - 6) // 2)
            dve.wait_ge(sem("p_used"), 56)
            link(TTo(out=modc[:, 16:48], in0=ps[:, 6, 0:32], in1=vcol[:, 16:48], op=ALU.add))
            STT(out=gain[:, 1, :], in0=modc[:, 32:40], scalar=1.0, in1=vcol[:, VROWS["g_mlp"][0]:VROWS["g_mlp"][0] + 8],
                op0=ALU.add, op1=ALU.mult).then_inc(sem("modc"), 1)
            nxt(U_TAIL)
            dve.wait_ge(sem("rope_in"), 16)
            dve.wait_ge(sem("tile"), G_A1 + 16)
            TTo(out=krot[64:96, :], in0=ps[64:96, bank(15), :], in1=rope[64:96, :], op=ALU.mult).then_inc(sem("krot"), 1)
            TTo(out=hb[64:96, 1, :], in0=ps[96:128, bank(15), :], in1=rope[96:128, :], op=ALU.mult).then_inc(sem("krot"), 1)
            dve.wait_ge(sem("krot"), 2)
            TTo(out=krot[64:96, :], in0=krot[64:96, :], in1=hb[64:96, 1, :], op=ALU.add).then_inc(sem("krot"), 1)
            dve.wait_ge(sem("zg"), 1)
            dve.wait_ge(sem("krot"), 3)
            dve.sem_inc(sem(f"t_free{15 % 2}"), 1)
            norm_rsqrt("ncq", 384)
            dve.wait_ge(sem("gate_t"), 1)
            CP(gates[:].rearrange("p t g -> p (t g)"), ps[:, 2, 0:96]).then_inc(sem("gates"), 1)
            norm_apply("ncq")
            for h in range(HEADS):
                u, g = U_UQ + h // 2, G_UQ + h
                if h % 2 == 0:
                    nxt(u)
                if h == 0:
                    norm_rsqrt("nckv", 256)
                    norm_apply("nckv")
                dve.wait_ge(sem("tile"), g + 1)
                link(TTo(out=hb[64:96, 0, :], in0=ps[64:96, bank(g), :], in1=rope[64:96, :], op=ALU.mult))
                link(TTo(out=hb[64:96, 1, :], in0=ps[96:128, bank(g), :], in1=rope[96:128, :], op=ALU.mult))
                dve.wait_ge(sem("qm"), h + 1)
                free(TTo(out=qm[64:96, h, :], in0=hb[64:96, 0, :], in1=hb[64:96, 1, :], op=ALU.add), g)
                freed(dve, g)
            nxt(U_UK)
            nxt(U_UV)
            freed(dve, G_Y - 2)
            freed(dve, G_Y - 1)
            dve.sem_inc(sem("ukv_done"), 1)
            dve.wait_ge(sem("cs_t"), 1)
            dve.wait_ge(sem("cbias_in"), 16)
            for half in range(2):
                own = [x[:].rearrange("p (i r) n -> p i r n", r=2)[:, :, half, :] for x in (cs, cbias)]
                link(TTo(out=own[0], in0=ps[:, 2 + half, :].rearrange("p (i n) -> p i n", n=32)[:, :, 0:NCMP],
                         in1=own[1], op=ALU.add))
            link(dve.tensor_reduce(out=cst[:, 0, :], in_=cs[:], op=ALU.max, axis=AX.X))
            link(TS(cst[:, 0, :], cst[:, 0, :], -1e25, None, ALU.max))
            link(dve.memset(cp[:, :, NCMP:32], 0.0))
            TTo(out=cs[:], in0=cs[:], in1=cst[:, 0, :].unsqueeze(2).to_broadcast([P, 32, NCMP]), op=ALU.subtract).then_inc(sem("cs"), 1)
            dve.wait_ge(sem("ce"), 1)
            link(dve.tensor_reduce(out=cst[:, 1, :], in_=cp[:, :, 0:NCMP], op=ALU.add, axis=AX.X))
            link(TS(cst[:, 1, :], cst[:, 1, :], 1e-30, None, ALU.max))
            link(dve.reciprocal(cst[:, 2, :], cst[:, 1, :]))
            link(TTo(out=cst[:, 3, :].rearrange("p (b h) -> p b h", b=TT), in0=cst[:, 2, :].rearrange("p (b h) -> p b h", b=TT),
                     in1=gates[:, :, 0:8], op=ALU.mult))
            TTo(out=cp[:, :, 0:NCMP], in0=cp[:, :, 0:NCMP], in1=cst[:, 3, :].unsqueeze(2).to_broadcast([P, 32, NCMP]),
                op=ALU.mult).then_inc(sem("cp"), 1)
            dve.wait_ge(sem("cp_t"), 1)
            CP(cpt[:, 4:8, :].rearrange("p b n -> p (b n)"), ps[:, 5, :]).then_inc(sem("cpt"), 1)
            dve.wait_ge(sem("oc_t"), 1)
            CP(onsa[:, 2, :], ps[:, 2, :])
            CP(onsa[:, 3, :], ps[:, 3, :]).then_inc(sem("oc_ev"), 1)
            dve.wait_ge(sem("oc_ev"), 2)
            dve.wait_ge(sem("bias_in"), 16)
            attention("nsa")
            dve.wait_ge(sem("cmask_in"), 16)
            attention("mla")
            for i in range(8):
                dve.wait_ge(sem("ot_hi"), i + 1)
                TTo(out=otlo[:, i, :], in0=ps[:, 4 + i % 2, :], in1=othi[:, i, :].bitcast(F32), op=ALU.subtract).then_inc(sem("ot_lo"), 1)
            for n in range(KD):
                u = U_Y + 3 * n
                for j in range(3):
                    nxt(u + j)
                for j in range(2):
                    g = G_Y + 4 * n + 2 + j
                    dve.wait_ge(sem("tile"), g + 1)
                    free(TTo(out=ym[:, j, :], in0=ps[:, bank(g), :], in1=sg[:, j, :], op=ALU.mult), g)
                    freed(dve, g)
                if n >= 1:
                    dve.wait_ge(sem("y_lo"), n)
                TTo(out=ym[:, 2, :], in0=ym[:, 0, :], in1=ym[:, 1, :], op=ALU.add).then_inc(sem("y"), 1)
                dve.wait_ge(sem("y_hi"), n + 1)
                TTo(out=ylo[:, n, :], in0=ym[:, 2, :], in1=yhi[:, n, :].bitcast(F32), op=ALU.subtract).then_inc(sem("y_lo"), 1)

            def lo_loop(u0, n, evac):
                with loop(dve, n // RING) as i:
                    for j in range(RING):
                        dve.wait_ge(sem("w_hi"), u0 + RING * i + j + AHEAD + 1)
                        s = slot(u0 + j + AHEAD)
                        TTo(out=wlo[:, s, :], in0=wraw[:, s, :], in1=whi[:, s, :].bitcast(F32), op=ALU.subtract).then_inc(sem("w_lo"), 1)
                        evac(i, j)

            def at1(t, idx):
                return t[:, bass.ds(idx, 1), :].rearrange("p a t -> p (a t)")

            def residual(g0, scale):
                def evac(i, j):
                    g = g0 + j
                    dve.wait_ge(sem("tile"), g0 + RING * i + j + 1)
                    x_ = at1(xT, RING * i + j)
                    if scale is None:
                        free(TTo(out=x_, in0=x_, in1=ps[:, bank(g), :], op=ALU.add), g)
                    else:
                        free(STT(out=x_, in0=ps[:, bank(g), :], scalar=modc[:, bass.ds(scale * KD + RING * i + j, 1)], in1=x_,
                                 op0=ALU.mult, op1=ALU.add), g)
                return evac
            lo_loop(U_OUT, KD, residual(G_OUT, 2))
            norm_rsqrt("n2", D)
            norm_apply("n2")

            def square(i, j):
                freed(dve, G_FC1 + j, i)
                TTo(out=at1(ff, RING * i + j), in0=rb[:, j % 2, :], in1=rb[:, j % 2, :], op=ALU.mult).then_inc(sem("ff"), 1)
            lo_loop(U_FC1, NF1, square)

            def f_lo(nm, j, idx):
                dve.wait_ge(sem(nm + "_hi"), since(nm + "_hi", idx + 1))
                TTo(out=flo[:, j % 2, :], in0=ff[:, idx, :] if isinstance(idx, int) else at1(ff, idx),
                    in1=fhi[:, j % 2, :].bitcast(F32), op=ALU.subtract).then_inc(sem(nm + "_lo"), 1)

            def rows_lo(u0, n, nm):
                for j in range(2):
                    f_lo(nm, j, j)
                    split_lo(u0 + j + AHEAD)
                turns = (n - 4) // 4
                with loop(dve, turns) as i:
                    for j in range(4):
                        f_lo(nm, j, 4 * i + 2 + j)
                        dve.wait_ge(sem("w_hi"), u0 + 2 + RING * i + j + AHEAD + 1)
                        s = slot(u0 + 2 + j + AHEAD)
                        TTo(out=wlo[:, s, :], in0=wraw[:, s, :], in1=whi[:, s, :].bitcast(F32), op=ALU.subtract).then_inc(sem("w_lo"), 1)
                for j in range(2 + 4 * turns, n):
                    f_lo(nm, j, j)
                    if u0 + j + AHEAD < U_END:
                        split_lo(u0 + j + AHEAD)
            rows_lo(U_FC2, NF1, "f1")
            dve.wait_ge(sem("f1_used"), NF1)
            for n in range(8):
                STT(out=xT[:, n, :], in0=ps[:, n, :], scalar=mod(5, n), in1=xT[:, n, :], op0=ALU.mult, op1=ALU.add).then_inc(sem("fc2_evac"), 1)
            norm_rsqrt("nf", D)
            dve.wait_ge(sem("nf_r"), since("nf_r", 1))
            for k in range(KD):
                STT(out=xT[:, k, :], in0=xT[:, k, :], scalar=col("g_final", k), in1=ps[:, 7, :], op0=ALU.mult, op1=ALU.mult
                    ).then_inc(sem("xf"), 1)
            norm_rsqrt("n3", D)
            norm_apply("n3")

            def turns_table():
                c1, s1, t = twc[:, 0, :], twc[:, 1, :], twc[:, 2, :]
                link(CP(c1, ssmc[:, 1, :]))
                link(CP(s1, ssmc[:, 2, :]))
                link(dve.memset(twr[:, :, 0:1], 1.0))
                link(dve.memset(twi[:, :, 0:1], 0.0))
                n = 1
                while n < SSM_C:
                    cc = twc[:, 3, :]
                    link(TS(cc, c1, 1.0, None, ALU.add))
                    t1, t2 = (x[:].rearrange("p q c -> p (q c)")[:, 0:16 * n].rearrange("p (q c) -> p q c", c=n) for x in (tA, tB))
                    cmul(twr[:, :, n:2 * n], twi[:, :, n:2 * n], twr[:, :, 0:n], twi[:, :, 0:n],
                         cc.unsqueeze(2).to_broadcast([P, SSM_Q, n]), s1.unsqueeze(2).to_broadcast([P, SSM_Q, n]), t1, t2)
                    n *= 2
                    if n < SSM_C:
                        double(s1, c1, t)

            def states():
                W = slice(1, SSM_C)
                Y_ = slice(0, SSM_C - 1)
                link(TTo(out=tA[:, :, W], in0=sA[:, :, Y_], in1=twr[:, :, W], op=ALU.mult))
                link(TTo(out=tB[:, :, W], in0=sB[:, :, Y_], in1=twi[:, :, W], op=ALU.mult))
                link(dve.memset(vA[:, :, 0:1], 0.0))
                link(TTo(out=vA[:, :, W], in0=tA[:, :, W], in1=tB[:, :, W], op=ALU.add))
                link(TTo(out=tA[:, :, W], in0=sB[:, :, Y_], in1=twr[:, :, W], op=ALU.mult))
                link(TTo(out=tB[:, :, W], in0=sA[:, :, Y_], in1=twi[:, :, W], op=ALU.mult))
                link(dve.memset(vB[:, :, 0:1], 0.0))
                link(TTo(out=vB[:, :, W], in0=tA[:, :, W], in1=tB[:, :, W], op=ALU.subtract))
                link(CP(sA[:], ssmc[:, 0, :].unsqueeze(2).to_broadcast([P, SSM_Q, SSM_C])))
                link(dve.memset(sA[:, :, 0:1], 0.0))
                fl = lambda x: x[:].rearrange("p q c -> p (q c)")
                link(dve.tensor_tensor_scan(fl(tA), fl(sA), fl(vA), 0.0, ALU.mult, ALU.add))
                link(dve.tensor_tensor_scan(fl(tB), fl(sA), fl(vB), 0.0, ALU.mult, ALU.add))
                link(TTo(out=vA[:], in0=twr[:], in1=tA[:], op=ALU.mult))
                link(TTo(out=vB[:], in0=twi[:], in1=tB[:], op=ALU.mult))
                link(TTo(out=sB[:], in0=vA[:], in1=vB[:], op=ALU.subtract))
                link(TTo(out=vA[:], in0=twr[:], in1=tB[:], op=ALU.mult))
                link(TTo(out=vB[:], in0=twi[:], in1=tA[:], op=ALU.mult))
                TTo(out=sA[:], in0=vA[:], in1=vB[:], op=ALU.add).then_inc(sem("xst"), 2)

            for i in range(12):
                u, g = U_IN2 + i, G_IN2 + i
                nxt(u)
                if i == 5:
                    turns_table()
            for i in range(4):
                nxt(U_V2 + i)
            dve.wait_ge(sem("s_ev"), 4)
            states()
            dve.wait_ge(sem("bias2_ok"), 1)
            attention("chk")
            dve.wait_ge(sem("y_in"), 16 * 32)
            for m in range(4):
                STT(out=yssm[:, m].rearrange("p j c -> p (j c)"), in0=uT[:, m].rearrange("p j c -> p (j c)"), scalar=col("ssm_d_2", m),
                    in1=yssm[:, m].rearrange("p j c -> p (j c)"), op0=ALU.mult, op1=ALU.add).then_inc(sem("yk"), 1)
            for m in range(4):
                dve.wait_ge(sem("g_hi"), m + 1)
                TTo(out=glo[:, m, :], in0=ygel[:, m, :], in1=ghi[:, m, :].bitcast(F32), op=ALU.subtract).then_inc(sem("g_lo"), 1)
            for i in range(4):
                g = G_GLU + i
                if i % 2 == 0:
                    nxt(U_GLU + i // 2)
                freed(dve, g)
                TTo(out=ysg[:, i, :], in0=ysg[:, i, :], in1=ygel[:, i, :], op=ALU.mult).then_inc(sem("ysg"), 1)
            dve.wait_ge(sem("ya_sq"), 4)
            TS(stat[:, 3, :], stat[:, 2, :], 1.0 / 512, EPS, ALU.mult, ALU.add).then_inc(sem("ya_ms"), 1)
            dve.wait_ge(sem("ya_rt"), 1)
            link(dve.reciprocal(stat[:, 3, :], stat[:, 4, :]))
            for t in range(TT):
                TS(yatt[:, t, :], yatt[:, t, :], stat[:, 3, t:t + 1], None, ALU.mult).then_inc(sem("ya_n"), 1)
            for i in range(4):
                dve.wait_ge(sem("ya_t"), i + 1)
                if i >= 2:
                    dve.wait_ge(sem("ya_lo"), i - 1)
                TS(hb[:, i % 2, :], ps[:, 4 + i % 2, :], col("norm_att_out_g_2", i), None, ALU.mult).then_inc(sem("ya_hb"), 1)
                dve.wait_ge(sem("ya_hi"), i + 1)
                TTo(out=hlo[:, 4 + i, :], in0=hb[:, i % 2, :], in1=hhi[:, 4 + i, :].bitcast(F32), op=ALU.subtract).then_inc(sem("ya_lo"), 1)
            dve.wait_ge(sem("ya_lo"), 4)
            norm_rsqrt("nssm", 512)
            norm_apply("nssm")
            lo_loop(U_OUT2, KD, residual(G_OUT2, None))
            norm_rsqrt("n4", D)
            norm_apply("n4")
            dve.sem_inc(sem("fc2b_free"), 1)

            def gate_up(i, j):
                if j % 2 == 1:
                    g = G_GU + j
                    dve.wait_ge(sem("tile"), G_GU + RING * i + j + 1)
                    freed(dve, g - 1, i)
                    free(TTo(out=at1(ff, 2 * i + j // 2), in0=rb[:, j // 2, :], in1=ps[:, bank(g), :], op=ALU.mult), g)
            lo_loop(U_GU, 2 * NF2, gate_up)
            rows_lo(U_DN, NF2, "f2")
            dve.wait_ge(sem("f2_used"), NF2)
            dve.wait_ge(sem("xn_ev"), 8)
            dve.wait_ge(sem("gfin_in"), 16)
            for t in range(TT):
                for half in range(2):
                    c = slice(512 * half, 512 * half + 512)
                    TTo(out=xn[:, t, c], in0=xn[:, t, c], in1=ps[:, 2 * t + half, :], op=ALU.add).then_inc(sem("xo"), 1)
                dve.wait_ge(sem("fin_sq"), t + 1)
                TS(stat[:, 7, t:t + 1], stat[:, 5, t:t + 1], 1.0 / D, EPS, ALU.mult, ALU.add).then_inc(sem("fin_ms"), 1)
                dve.wait_ge(sem("fin_rt"), t + 1)
                link(dve.reciprocal(stat[:, 4, t:t + 1], stat[:, 6, t:t + 1]))
                STT(out=xn[:, t, :], in0=xn[:, t, :], scalar=stat[:, 4, t:t + 1], in1=gfin[:, :], op0=ALU.mult, op1=ALU.mult).then_inc(sem("o_ready"), 1)


_INS = ["x", "c", "w_ada", "b_ada", "g_mix", "w_in", "pe_ck", "w_ck1", "w_ck2", "pe_cv", "w_cv1", "w_cv2", "g_cq", "w_uq",
        "g_ckv", "w_uk", "w_uv", "w_o_nsa", "w_o_mla", "w_out", "g_mlp", "w_fc1", "w_fc2", "g_final", "norm_mix_g_2",
        "w_in_2", "ssm_lam_re_2", "ssm_lam_im_2", "ssm_log_dt_2", "ssm_b_re_2", "ssm_b_im_2", "ssm_c_re_2",
        "ssm_c_im_2", "ssm_d_2", "ssm_w_glu_2", "ssm_b_glu_2", "attn_rel_bias_2", "norm_ssm_out_g_2",
        "norm_att_out_g_2", "w_out_2", "norm_ffn_g_2", "w_gate_2", "w_up_2", "w_down_2", "norm_final_g_2"]


def constants():
    f = np.float32
    p = np.arange(P)[:, None]
    j = np.arange(T)[None, :]
    dist = p - (j - (T - P))
    seen = dist >= 0
    alibi = np.stack([np.where(seen, -(8.0 * 2.0 ** -(h + 1)) * dist, NEG) for h in range(4)], axis=1)
    causal = np.where(seen, 0.0, NEG)
    block, head, n = np.meshgrid(np.arange(TT), np.arange(HEADS), np.arange(NCMP), indexing="ij")
    d = (P * block + 0)[None] + p[:, :, None, None] - (16 * n + 31)[None]
    cmp_bias = np.where(d >= 0, -(8.0 * 2.0 ** -(head + 1.0))[None] * d, NEG).reshape(P, 32, NCMP)
    ang = np.arange(T, dtype=f)[None, :] * (f(10000.0) ** (-np.arange(16, dtype=f) / f(16)))[:, None]
    cos, sin = np.cos(ang.astype(np.float64)), np.sin(ang.astype(np.float64))
    rope = np.zeros((P, T))
    rope[64:96] = np.concatenate([cos, cos])
    rope[96:128] = np.concatenate([-sin, sin])
    return {"identity": np.eye(P).astype(f), "alibi": alibi.astype(f), "causal": causal.astype(f),
            "cmp_bias": cmp_bias.astype(f), "rope_table": rope.astype(f)}


def kernel(**inputs):
    import concourse.bacc as _bacc
    from concourse.bass_utils import run_bass_kernel_spmd as _run

    nc = _bacc.Bacc("TRN2", target_bir_lowering=False, num_devices=1)
    arrays, aps = {}, {}
    given = {name: np.ascontiguousarray(inputs[name]) for name in _INS}
    given.update(constants())
    for name, v in given.items():
        arrays[f"in_{name}"] = v
        aps[name] = nc.dram_tensor(f"in_{name}", v.shape, mybir.dt.from_np(v.dtype), kind="ExternalInput").ap()
    scr = {"rel": [8, 640], "relp": [P, 8, 640], "w1": [2, P, SSM_Q, P], "w2": [2, P, SSM_Q, P], "kk": [32, SSM_Q, P],
           "u": [4, P, SSM_L, SSM_C], "y": [P, 32 * SSM_C]}
    scr = {k: nc.dram_tensor(f"scratch_{k}", v, F32, kind="Internal").ap() for k, v in scr.items()}
    out = nc.dram_tensor("out_0", [1, T, D], F32, kind="ExternalOutput").ap()
    program(nc, aps, out, scr)
    r = _run(nc, [arrays], core_ids=[0])
    return r.results[0]["out_0"]
```

```python
import concourse.bass as bass
from concourse import mybir
from contextlib import ExitStack
import numpy as np

F32 = mybir.dt.float32
F32R = mybir.dt.float32r
I32 = mybir.dt.int32
ACT = mybir.ActivationFunctionType
ALU = mybir.AluOpType
AX = mybir.AxisListType

P = 128
T = 512
D = 1024
KD = D // P
TT = T // P
EPS = 1e-6
NEG = -1e30
FF1, FF2 = 4096, 2816
NF1, NF2 = FF1 // P, FF2 // P
HEADS, DH = 8, 64
MLA_SCALE = 96.0 ** -0.5
NCMP = 31
SSM_L = 8
SSM_C = T // SSM_L
SSM_Q = 16
RING = 4
AHEAD = 3

C_Q, C_KC, C_VC, C_KS, C_VS, C_KW, C_VW, C_G, C_QD, C_KVD, C_KR, C_GA, C_GB = np.cumsum(
    [0, 512, 128, 128, 128, 128, 128, 128, 24, 384, 256, 32, 1024]).tolist()

U_A1 = 0
A1_COLS = [C_KC, C_VC, C_KS, C_KW, C_VS, C_VW] + [C_Q + P * i for i in range(4)] \
    + [C_QD + P * i for i in range(3)] + [C_KVD + P * i for i in range(2)]
U_TAIL = U_A1 + len(A1_COLS)
U_UQ = U_TAIL + 1
U_UK = U_UQ + 4
U_UV = U_UK + 1
U_Y = U_UV + 1
U_OUT = U_Y + 3 * KD
U_FC1 = U_OUT + KD
U_FC2 = U_FC1 + NF1
U_IN2 = U_FC2 + NF1
U_V2 = U_IN2 + 12
U_GLU = U_V2 + 4
U_OUT2 = U_GLU + 2
U_GU = U_OUT2 + KD
U_DN = U_GU + 2 * NF2
U_END = U_DN + NF2

G_A1 = 0
G_UQ = G_A1 + 16
G_UK = G_UQ + 8
G_UV = G_UK + 4
G_Y = G_UV + 4
G_OUT = G_Y + 4 * KD
G_FC1 = G_OUT + KD
G_IN2 = G_FC1 + NF1
G_GLU = G_IN2 + 12
G_OUT2 = G_GLU + 4
G_GU = G_OUT2 + KD
G_END = G_GU + 2 * NF2

VROWS = {}
_n = 0
for _name, _rows in (("b_ada", 48), ("g_mix", 8), ("c", 8), ("g_mlp", 8), ("g_cq", 3), ("g_ckv", 2),
                     ("norm_mix_g_2", 8), ("norm_ffn_g_2", 8), ("ssm_b_glu_2", 4), ("ssm_d_2", 4),
                     ("norm_ssm_out_g_2", 4), ("norm_att_out_g_2", 4), ("g_final", 8)):
    VROWS[_name] = (_n, _rows)
    _n += _rows
NV = _n


def program(nc, a, out, scr, dbg=None):
    with ExitStack() as ctx:
        S = {}

        ATTS = {"nsa": 16, "mla": 8, "chk": 8}
        NORMS = {"n1": 8, "ncq": 3, "nckv": 2, "n2": 8, "n3": 8, "nssm": 4, "n4": 8}

        def since(name, value):
            who, _, what = name.partition("_")
            for group in (NORMS, ATTS):
                if who in group:
                    who_before = list(group)[:list(group).index(who)]
                    before = [group[k] for k in who_before]
                    split = sum(before) if group is NORMS else 0
                    if group is NORMS and what in ("h", "hi", "lo"):
                        return split + value
                    per = (lambda n: n if what in ("sq", "ac") else 1) if group is NORMS else \
                        (lambda n: {"o": n, "pta": 2 * n, "ptd": 2 * n}.get(what, 4 * n))
                    return sum(map(per, before)) + value
            return value

        def sem(name):
            who, _, what = name.partition("_")
            name = "norm_" + what if who in NORMS else "att_" + what if who in ATTS else name
            if name not in S:
                S[name] = ctx.enter_context(nc.semaphore(name))
            return S[name]

        base = [(nc.sbuf_base + 31) // 32 * 32]
        limit = nc.sbuf_usable_end

        def at(name, offset, shape, dt=F32):
            n = int(np.prod(shape[1:])) * 4
            assert offset + n <= limit, (name, offset + n - limit)
            return nc.alloc_sbuf_tensor_at(name, shape, dt, offset=offset)

        def keep(name, shape, dt=F32):
            t = at(name, base[0], shape, dt)
            base[0] += (int(np.prod(shape[1:])) * 4 + 31) // 32 * 32
            return t

        ident = keep("ident", [P, P])
        ones = keep("ones", [P, P])
        vcol = keep("vcol", [P, NV + 32])
        modc = keep("modc", [P, 48])
        gain = keep("gain", [P, 2, KD])
        stat = keep("stat", [P, 8, 4])
        eps = keep("eps", [P, 2])
        gsq = keep("gsq", [P, KD])
        gmix2 = keep("gmix2", [P, KD])
        rsum = keep("rsum", [P, 2, 4])
        rinv = keep("rinv", [P, 4])
        smax = keep("smax", [P, 4])
        ssmc = keep("ssmc", [P, 3, SSM_Q])
        hb = keep("hb", [P, 2, T])
        xT = keep("xT", [P, KD, T])
        wraw = keep("wraw", [P, RING, D])
        whi = keep("whi", [P, RING, D], F32R)
        wlo = keep("wlo", [P, RING, D], F32R)
        H0 = base[0]
        hhi = keep("hhi", [P, KD, T], F32R)
        hlo = keep("hlo", [P, KD, T], F32R)
        X0 = base[0]
        K = 1024

        def x_at(name, kb, shape, dt=F32):
            return at(name, X0 + int(kb * K), shape, dt)

        xs = at("xs", H0, [P, TT, D])
        qT = x_at("qT", 0, [P, 4, T])
        kdup = x_at("kdup", 8, [P, 2, 2, T])
        vnat = x_at("vnat", 16, [P, TT, 2, P])
        vblk = x_at("vblk", 20, [P, 2, 4, DH])
        kcT = x_at("kcT", 22, [P, 2, NCMP])
        gates = x_at("gates", 22.5, [P, TT, 24])
        qm = x_at("qm", 23, [P, HEADS, T])
        km = x_at("km", 39, [P, HEADS, T])
        vm = x_at("vm", 55, [P, TT, HEADS * DH])
        bias = x_at("bias", 63, [P, 4, T])
        cmask = x_at("cmask", 71, [P, T])
        onsa = x_at("onsa", 73, [P, TT, T])
        omla = x_at("omla", 81, [P, TT, T])
        ssb = x_at("ssb", 89, [P, 2, T])
        ppb = x_at("ppb", 93, [P, 3, T])
        ptb = x_at("ptb", 99, [P, 3, T])
        sq = x_at("sq", 73, [P, 4, T])
        x2 = x_at("x2", 73, [P, 2, 2, T])
        flat = x_at("flat", 81, [P, 2, 16, 62])
        cmpw = [x_at(f"cmpw{i}", kb, [P, D]) for i, kb in enumerate((89, 93, 97, 101, 0, 4, 39, 43))]
        aring = x_at("aring", 0, [P, 4, D])
        ada1 = x_at("ada1", 81, [P, 2, D])
        aring2 = x_at("aring2", 85, [P, 2, T])
        ada2 = x_at("ada2", 81, [P, 2, T])
        cqhi = x_at("cqhi", 89, [P, 3, T], F32R)
        cqlo = x_at("cqlo", 95, [P, 3, T], F32R)
        krot = x_at("krot", 101, [P, T])
        rope = x_at("rope", 103, [P, T])
        ckhi = x_at("ckhi", 63, [P, 2, T], F32R)
        cklo = x_at("cklo", 67, [P, 2, T], F32R)
        zl = x_at("zl", 39, [P, 5, T])
        zg = x_at("zg", 49, [P, T])
        vrow = x_at("vrow", 55.5, [P, 2, P])
        hid = x_at("hid", 51, [P, 2, 2, 2, 32])
        hidr = x_at("hidr", 52, [P, 2, 2, 4, 32])
        w2d = x_at("w2d", 54, [P, 2, 2, DH])
        w2v = x_at("w2v", 55, [P, 2, DH])
        cbias = x_at("cbias", 89, [P, 32, NCMP])
        cs = x_at("cs", 93, [P, 32, NCMP])
        cp = x_at("cp", 97, [P, 32, 32])
        cpt = x_at("cpt", 101, [P, 8, P])
        cst = x_at("cst", 105, [P, 4, 32])
        othi = x_at("othi", 0, [P, 8, T], F32R)
        otlo = x_at("otlo", 16, [P, 8, T], F32R)
        yhi = x_at("yhi", 32, [P, KD, T], F32R)
        ylo = x_at("ylo", 48, [P, KD, T], F32R)
        sg = x_at("sg", 64, [P, 2, T])
        ym = x_at("ym", 89, [P, 3, T])
        ff = x_at("ff", 0, [P, NF1, T])
        fhi = x_at("fhi", 65, [P, 2, T], F32R)
        flo = x_at("flo", 69, [P, 2, T], F32R)
        rb = x_at("rb", 89, [P, 2, T])
        sq3 = x_at("sq3", 89, [P, KD, T])
        xn = x_at("xn", 47, [P, TT, D])
        gfin = x_at("gfin", 93, [P, D])
        uT = x_at("uT", 0, [P, 4, SSM_L, SSM_C])
        ug = x_at("ug", 8, [P, 32, SSM_C])
        q2 = x_at("q2", 16, [P, 4, T])
        k2 = x_at("k2", 24, [P, 4, T])
        v2 = x_at("v2", 32, [P, TT, T])
        w1s = x_at("w1s", 40, [P, 2, SSM_Q, P])
        w2s = x_at("w2s", 40, [P, 2, SSM_Q, P])
        tmat = x_at("tmat", 56, [P, 32, P])
        sA = x_at("sA", 72, [P, SSM_Q, SSM_C])
        sB = x_at("sB", 76, [P, SSM_Q, SSM_C])
        twr = x_at("twr", 80, [P, SSM_Q, SSM_C])
        twi = x_at("twi", 84, [P, SSM_Q, SSM_C])
        vA = x_at("vA", 88, [P, SSM_Q, SSM_C])
        vB = x_at("vB", 92, [P, SSM_Q, SSM_C])
        tA = x_at("tA", 96, [P, SSM_Q, SSM_C])
        tB = x_at("tB", 100, [P, SSM_Q, SSM_C])
        yg = x_at("yg", 96, [P, 32, SSM_C])
        bias2 = x_at("bias2", 72, [P, HEADS, T])
        yatt = x_at("yatt", 88, [P, TT, T])
        yssm = x_at("yssm", 40, [P, 4, SSM_L, SSM_C])
        ygel = x_at("ygel", 8, [P, 4, T])
        ghi = x_at("ghi", 48, [P, 4, T], F32R)
        glo = x_at("glo", 56, [P, 4, T], F32R)
        ysg = x_at("ysg", 64, [P, 4, T])
        sq2 = x_at("sq2", 72, [P, 4, T])
        ssb2 = at("ssb2", H0, [P, 2, T])
        ppb2 = at("ppb2", H0 + 4 * K, [P, 3, T])
        ptb2 = at("ptb2", H0 + 10 * K, [P, 3, T])
        twc = x_at("twc", 104.5, [P, 4, SSM_Q])
        pv = x_at("pv", 23, [16, 24, P])
        dtl = x_at("dtl", 36.75, [16, 8, 2])
        pvi = x_at("pvi", 36, [16, P], I32)
        dti = x_at("dti", 36.5, [16, 2], I32)
        w1t = x_at("w1t", 23, [P, 2, 4, P])
        cpw = x_at("cpw", 27, [P, 2, 4, 9, 16])
        tmp = x_at("tmp", 31.5, [P, 2, 4 * 9 * 16])
        stg = x_at("stg", 56.5, [P, 2, 4, P])
        kst = x_at("kst", 73, [32, 4, P])
        bpair = x_at("bpair", 77, [P, 2, SSM_Q, 2, 16])
        braw = x_at("braw", 63, [P, 2, SSM_Q, 16])
        bbar = x_at("bbar", 65, [P, 2, SSM_Q, 16])
        craw = x_at("craw", 49, [P, 2, 4, 2, 64])
        ctp = x_at("ctp", 67, [P, 2, SSM_Q, 16])
        pw = x_at("pw", 69, [P, 2, SSM_Q, 9])
        pwr = x_at("pwr", 70.25, [P, 2, SSM_Q, 8])
        apar = x_at("apar", 71.5, [P, 7, SSM_Q])
        rel = x_at("rel", 60.5, [8, 640])

        ps = ctx.enter_context(nc.psum_tensor("ps", [P, 8, T], F32))

        def col(name, i=0):
            return vcol[:, VROWS[name][0] + i:VROWS[name][0] + i + 1]

        def mod(part, i):
            return modc[:, part * KD + i:part * KD + i + 1]

        def slot(u):
            return u % RING

        def freed(eng, g, turn=0):
            eng.wait_ge(sem(f"t_free{g % 2}"), g // 2 + 1 + turn * (RING // 2))

        def free(ins, g):
            return ins.then_inc(sem(f"t_free{g % 2}"), 1)

        def used(u):
            for first, fn in ((U_DN, lambda i: ("f2_used", i + 1)), (U_GU, lambda i: ("tile", G_GU + i + 1)),
                              (U_OUT2, lambda i: ("tile", G_OUT2 + i + 1)), (U_GLU, lambda i: ("tile", G_GLU + 2 * i + 2)),
                              (U_V2, lambda i: ("v2_t", i + 1)), (U_IN2, lambda i: ("tile", G_IN2 + i + 1)),
                              (U_FC2, lambda i: ("f1_used", i + 1) if i < NF1 - 2 else ("f1_bank", 8)), (U_FC1, lambda i: ("tile", G_FC1 + i + 1)),
                              (U_OUT, lambda i: ("tile", G_OUT + i + 1)),
                              (U_Y, lambda i: ("tile", G_Y + 4 * (i // 3) + (i % 3 + 1 if i % 3 < 2 else 4))),
                              (U_UV, lambda i: ("tile", G_UV + 4)), (U_UK, lambda i: ("tile", G_UK + 4)),
                              (U_UQ, lambda i: ("tile", G_UQ + 2 * i + 2)), (0, lambda i: ("tile", i + 1))):
                if u >= first:
                    return fn(u - first)

        def bank(g):
            return g % 2

        win = a["w_in"][0].rearrange("(k p) n -> p k n", p=P)

        def loop(eng, n):
            return eng.Fori(0, n)

        def nsa_heads():
            res = []
            for g in range(2):
                for br in range(2):
                    for h in range(4 * g, 4 * g + 4):
                        r = slice(64 * (h % 2), 64 * (h % 2) + 64)
                        res.append(dict(q=qT[r, h // 2, :], k=kdup[r, br, g, :],
                                        v=lambda b, br=br, g=g: vnat[:, b, br, 64 * g:64 * g + 64],
                                        bias=bias[:, h % 4, :], scale=DH ** -0.5, o=onsa, h=h,
                                        gate=gates[:, :, 8 * (br + 1) + h], rescale=(g == 1 and br == 0 and h == 4)))
            return res

        def mla_heads():
            return [dict(q=qm[0:96, h, :], k=km[0:96, h, :], v=lambda b, h=h: vm[:, b, 64 * h:64 * h + 64],
                         bias=cmask[:, :], scale=MLA_SCALE, o=omla, h=h, gate=None, rescale=False)
                    for h in range(HEADS)]

        def chunk_heads():
            return [dict(q=q2[64 * (h % 2):64 * (h % 2) + 64, h // 2, :], k=k2[64 * (h % 2):64 * (h % 2) + 64, h // 2, :],
                         v=lambda b, h=h: v2[:, b, 64 * h:64 * h + 64],
                         bias=bias2[:, h, :], scale=DH ** -0.5, o=yatt, h=h, gate=None, rescale=False)
                    for h in range(HEADS)]

        ATT = {"nsa": (nsa_heads(), ssb, ppb, ptb), "mla": (mla_heads(), ssb, ppb, ptb),
               "chk": (chunk_heads(), ssb2, ppb2, ptb2)}

        NORM = {"n1": (lambda k: xT[:, k, :], 8, sq), "ncq": (lambda k: zl[:, k, :], 3, sq),
                "nckv": (lambda k: zl[:, 3 + k, :], 2, sq), "n2": (lambda k: xT[:, k, :], 8, sq),
                "n3": (lambda k: xT[:, k, :], 8, sq3), "nssm": (lambda k: ysg[:, k, :], 4, sq2),
                "n4": (lambda k: xT[:, k, :], 8, sq)}
        AFTER = {"n1": (lambda k: gain[:, 0, k:k + 1], lambda k: mod(0, k), hhi, hlo),
                 "ncq": (lambda k: col("g_cq", k), None, cqhi, cqlo),
                 "nckv": (lambda k: col("g_ckv", k), None, ckhi, cklo),
                 "n2": (lambda k: gain[:, 1, k:k + 1], lambda k: mod(3, k), hhi, hlo),
                 "n3": (lambda k: gmix2[:, k:k + 1], None, hhi, hlo),
                 "nssm": (lambda k: col("norm_ssm_out_g_2", k), None, hhi, hlo),
                 "n4": (lambda k: col("norm_ffn_g_2", k), None, hhi, hlo)}

        block = ctx.enter_context(nc.Block())

        @block.sync
        def _(sp):
            def slot_free(u):
                if u >= RING:
                    sp.wait_ge(sem("w_lo"), u - RING + 1)

            def load(u, dst, src):
                sp.dma_start(dst, src).then_inc(sem(f"w_in{slot(u)}"), 16)

            def raw(u, lo=0, hi=D):
                return wraw[:, slot(u), lo:hi]

            sp.dma_start(xs[:], a["x"][0].rearrange("(t p) d -> p t d", p=P)).then_inc(sem("x_in"), 16)
            for n in range(16):
                if n >= 4:
                    sp.wait_ge(sem("ada_used"), n - 3)
                sp.dma_start(aring[:, n % 4, :], a["w_ada"][0][P * (n % 8):P * (n % 8) + P, D * (n // 8):D * (n // 8) + D]
                             ).then_inc(sem(f"ada_in{n % 4}"), 16)
            for i, c in enumerate(A1_COLS):
                u = U_A1 + i
                slot_free(u)
                load(u, raw(u).rearrange("p (k n) -> p k n", k=KD), win[:, :, c:c + P])
                if i in (3, 5):
                    w = (i - 3) // 2
                    if w == 1:
                        sp.wait_ge(sem("ada_used"), 16)
                    for m in range(4):
                        sp.dma_start(cmpw[4 * w + m].rearrange("p (k n) -> p k n", k=4),
                                     a[("w_ck1", "w_cv1")[w]][0].rearrange("(k p) n -> p k n", p=P)[:, 4 * m:4 * m + 4, :]
                                     ).then_inc(sem(f"cmpw_in{w}"), 16)
            u = U_TAIL
            slot_free(u)
            tail = raw(u).rearrange("p (k n) -> p k n", k=KD)
            for lo, c, n in ((0, C_G, 24), (64, C_KR, 32), (96, C_KR + 16, 16), (112, C_KR, 16)):
                load(u, tail[:, :, lo:lo + n], win[:, :, c:c + n])
            wuq = a["w_uq"][0].rearrange("(k p) (h n) -> p k h n", p=P, n=96)
            for i in range(4):
                u = U_UQ + i
                slot_free(u)
                v = raw(u, 0, 768).rearrange("p (k h n) -> p k h n", k=3, h=2)
                for h in range(2):
                    load(u, v[:, :, h, 0:96], wuq[:, :, 2 * i + h, :])
                    load(u, v[:, :, h, 96:112], wuq[:, :, 2 * i + h, 80:96])
                    load(u, v[:, :, h, 112:128], wuq[:, :, 2 * i + h, 64:80])
            for u, name in ((U_UK, "w_uk"), (U_UV, "w_uv")):
                slot_free(u)
                load(u, raw(u).rearrange("p (k n) -> p k n", k=2), a[name][0].rearrange("(k p) n -> p k n", p=P))
            for n in range(KD):
                for j, c in enumerate((C_GA, C_GB)):
                    u = U_Y + 3 * n + j
                    slot_free(u)
                    load(u, raw(u).rearrange("p (k n) -> p k n", k=KD), win[:, :, c + n * P:c + n * P + P])
                u = U_Y + 3 * n + 2
                slot_free(u)
                for j, name in enumerate(("w_o_nsa", "w_o_mla")):
                    load(u, raw(u, 512 * j, 512 * j + 512).rearrange("p (k n) -> p k n", k=4),
                         a[name][0].rearrange("(k p) n -> p k n", p=P)[:, :, n * P:n * P + P])
                if n == 0:
                    for m in range(64):
                        part, k, half = 2 + m // 16, m // 2 % 8, m % 2
                        if m >= 2:
                            sp.wait_ge(sem("ada2_used"), m - 1)
                        c = D * part + T * half
                        sp.dma_start(aring2[:, m % 2, :], a["w_ada"][0][P * k:P * k + P, c:c + T]
                                     ).then_inc(sem(f"ada2_in{m % 2}"), 16)

            def columns(u0, n, src):
                with loop(sp, n // RING) as i:
                    for j in range(RING):
                        sp.wait_ge(sem("w_lo"), u0 + RING * i + j - RING + 1)
                        load(u0 + j, raw(u0 + j).rearrange("p (k n) -> p k n", k=KD),
                             src[:, :, bass.ds(P * RING * i + P * j, P)])
                return u0 + n // RING * RING

            def rows(u0, n, src):
                with loop(sp, n // RING) as i:
                    for j in range(RING):
                        sp.wait_ge(sem("w_lo"), u0 + RING * i + j - RING + 1)
                        load(u0 + j, raw(u0 + j), src[bass.ds(P * RING * i + P * j, P), :])
                for j in range(n // RING * RING, n):
                    slot_free(u0 + j)
                    load(u0 + j, raw(u0 + j), src[P * j:P * j + P, :])

            columns(U_OUT, KD, a["w_out"][0].rearrange("(k p) n -> p k n", p=P))
            columns(U_FC1, NF1, a["w_fc1"][0].rearrange("(k p) n -> p k n", p=P))
            rows(U_FC2, NF1, a["w_fc2"][0])
            win2 = a["w_in_2"][0].rearrange("(k p) n -> p k n", p=P)
            columns(U_IN2, 12, win2)
            for i in range(4):
                u = U_V2 + i
                slot_free(u)
                load(u, raw(u).rearrange("p (k n) -> p k n", k=2), win2[:, 2 * i:2 * i + 2, 1536:2048])
            for i in range(2):
                u = U_GLU + i
                slot_free(u)
                load(u, raw(u).rearrange("p (k n) -> p k n", k=4),
                     a["ssm_w_glu_2"][0].rearrange("(k p) n -> p k n", p=P)[:, :, 256 * i:256 * i + 256])
            columns(U_OUT2, KD, a["w_out_2"][0].rearrange("(k p) n -> p k n", p=P))
            wg = a["w_gate_2"][0].rearrange("(k p) n -> p k n", p=P)
            wu = a["w_up_2"][0].rearrange("(k p) n -> p k n", p=P)
            with loop(sp, NF2 // 2) as i:
                for j in range(4):
                    u = U_GU + j
                    sp.wait_ge(sem("w_lo"), U_GU + 4 * i + j - RING + 1)
                    load(u, raw(u).rearrange("p (k n) -> p k n", k=KD),
                         (wg, wu)[j % 2][:, :, bass.ds(2 * P * i + (j // 2) * P, P)])
            rows(U_DN, NF2, a["w_down_2"][0])
            for t in range(TT):
                sp.wait_ge(sem("o_ready"), t + 1)
                sp.dma_start(out[0, P * t:P * t + P, :], xn[:, t, :]).then_inc(sem("stored"), 16)
            sp.wait_ge(sem("stored"), 16 * TT)

        def w_count(u):
            n = 0
            for v in range(slot(u), u + 1, RING):
                n += 4 if v == U_TAIL else 6 if U_UQ <= v < U_UK else \
                    2 if U_Y <= v < U_OUT and (v - U_Y) % 3 == 2 else 1
            return n

        @block.gpsimd
        def _(pool):
            chain = [0]

            def link(i):
                chain[0] += 1
                i.then_inc(sem("pool_chain"), 1)
                pool.wait_ge(sem("pool_chain"), chain[0])

            TTo, TS, CP = pool.tensor_tensor, pool.tensor_scalar, pool.tensor_copy

            def STT(out, in0, scalar, in1, op0, op1):
                part = pv[0:16, 22, :] if out.shape[-1] == P else dtl[0:16, 6, :]
                link(TS(part, in0, scalar, None, op0))
                return TTo(out=out, in0=part, in1=in1, op=op1)

            def v(i):
                return pv[0:16, i, :]

            def exp_(dst, x, t, ti):
                xc, n, f, q = t
                link(TS(xc, x, -87.3, 88.7, ALU.max, ALU.min))
                link(TS(n, xc, 1.4426950408889634, 12582912.0, ALU.mult, ALU.add))
                link(TS(n, n, -12582912.0, None, ALU.add))
                link(STT(out=f, in0=n, scalar=-0.693145751953125, in1=xc, op0=ALU.mult, op1=ALU.add))
                link(STT(out=f, in0=n, scalar=-1.42860682030941723212e-6, in1=f, op0=ALU.mult, op1=ALU.add))
                link(TS(q, f, 1.0 / 5040, None, ALU.mult))
                for c in (1.0 / 720, 1.0 / 120, 1.0 / 24, 1.0 / 6, 0.5, 1.0):
                    link(STT(out=q, in0=q, scalar=c, in1=f, op0=ALU.add, op1=ALU.mult))
                link(TS(ti, n, 127.0, 8388608.0, ALU.add, ALU.mult))
                link(STT(out=dst, in0=q, scalar=1.0, in1=ti.bitcast(F32), op0=ALU.add, op1=ALU.mult))

            def double(s, c1, t):
                link(STT(out=t, in0=c1, scalar=1.0, in1=s, op0=ALU.add, op1=ALU.mult))
                link(STT(out=c1, in0=s, scalar=-2.0, in1=s, op0=ALU.mult, op1=ALU.mult))
                link(TS(s, t, 2.0, None, ALU.mult))

            pool.wait_ge(sem("par_in"), 16 * 3)
            d = [dtl[0:16, i, :] for i in range(8)]
            lre, lim = v(20), v(21)
            link(TTo(out=v(17), in0=lre, in1=lre, op=ALU.mult))
            link(TTo(out=v(18), in0=lim, in1=lim, op=ALU.mult))
            TTo(out=v(17), in0=v(17), in1=v(18), op=ALU.add).then_inc(sem("lam_sq"), 1)
            exp_(d[1], d[0], d[2:6], dti[0:16, :])

            def by_dt(o, x):
                link(TTo(out=o.rearrange("q (g p) -> q g p", g=2), in0=x.rearrange("q (g p) -> q g p", g=2),
                         in1=d[1].unsqueeze(2).to_broadcast([16, 2, 64]), op=ALU.mult))
            by_dt(v(8), lre)
            by_dt(v(9), lim)
            exp_(v(10), v(8), [v(11), v(12), v(13), v(14)], pvi[0:16, :])
            link(TS(v(11), v(9), 0.15915494309189535, 12582912.0, ALU.mult, ALU.add))
            link(TS(v(11), v(11), -12582912.0, None, ALU.add))
            for c in (6.28125, 0.0019350051879882812, 3.0199159819567e-07):
                link(STT(out=v(9), in0=v(11), scalar=-c, in1=v(9), op0=ALU.mult, op1=ALU.add))
            link(TS(v(9), v(9), 0.125, None, ALU.mult))
            link(TTo(out=v(12), in0=v(9), in1=v(9), op=ALU.mult))
            link(TS(v(13), v(12), -1.0 / 5040, None, ALU.mult))
            for c in (1.0 / 120, -1.0 / 6):
                link(STT(out=v(13), in0=v(13), scalar=c, in1=v(12), op0=ALU.add, op1=ALU.mult))
            link(STT(out=v(13), in0=v(13), scalar=1.0, in1=v(9), op0=ALU.add, op1=ALU.mult))
            link(TS(v(14), v(12), 1.0 / 40320, None, ALU.mult))
            for c in (-1.0 / 720, 1.0 / 24, -0.5):
                link(STT(out=v(14), in0=v(14), scalar=c, in1=v(12), op0=ALU.add, op1=ALU.mult))
            for _i in range(3):
                double(v(13), v(14), v(15))
            link(TTo(out=v(15), in0=v(10), in1=v(14), op=ALU.mult))
            link(TTo(out=v(0), in0=v(10), in1=v(15), op=ALU.add))
            link(TTo(out=v(1), in0=v(10), in1=v(13), op=ALU.mult))
            link(STT(out=v(16), in0=v(10), scalar=-1.0, in1=v(15), op0=ALU.add, op1=ALU.add))
            pool.wait_ge(sem("lam_inv"), 1)
            link(TTo(out=v(18), in0=v(16), in1=lre, op=ALU.mult))
            link(TTo(out=v(19), in0=v(1), in1=lim, op=ALU.mult))
            link(TTo(out=v(18), in0=v(18), in1=v(19), op=ALU.add))
            link(TTo(out=v(2), in0=v(18), in1=v(17), op=ALU.mult))
            link(TTo(out=v(18), in0=v(1), in1=lre, op=ALU.mult))
            link(TTo(out=v(19), in0=v(16), in1=lim, op=ALU.mult))
            link(TTo(out=v(18), in0=v(18), in1=v(19), op=ALU.subtract))
            link(TTo(out=v(3), in0=v(18), in1=v(17), op=ALU.mult))
            link(TTo(out=v(4), in0=v(10), in1=v(10), op=ALU.mult))
            link(TTo(out=v(4), in0=v(4), in1=v(4), op=ALU.mult))
            link(TTo(out=v(4), in0=v(4), in1=v(4), op=ALU.mult))
            for _i in range(3):
                double(v(13), v(14), v(15))
            link(CP(v(5), v(14)))
            CP(v(6), v(13)).then_inc(sem("par"), 1)

            pool.wait_ge(sem("par_ev"), 3)
            pool.wait_ge(sem("parb_in"), 16 * 6)
            def cmul(ore, oim, xre, xim, yre, yim, t1, t2):
                link(TTo(out=t1, in0=xre, in1=yre, op=ALU.mult))
                link(TTo(out=t2, in0=xim, in1=yim, op=ALU.mult))
                link(TTo(out=ore, in0=t1, in1=t2, op=ALU.subtract))
                link(TTo(out=t1, in0=xre, in1=yim, op=ALU.mult))
                link(TTo(out=t2, in0=xim, in1=yre, op=ALU.mult))
                link(TTo(out=oim, in0=t1, in1=t2, op=ALU.add))

            def bc(x, n):
                return x.unsqueeze(2).to_broadcast([P, SSM_Q, n])

            def ssm_setup():
                t = [tmp[:, i, 0:256].rearrange("p (q h) -> p q h", h=16) for i in range(2)]
                cmul(bbar[:, 0], bbar[:, 1], bc(apar[:, 2, :], 16), bc(apar[:, 3, :], 16), braw[:, 0], braw[:, 1], *t)
                link(pool.memset(bpair[:], 0.0))
                for g in range(2):
                    r = slice(64 * g, 64 * g + 64)
                    for c in range(2):
                        link(CP(bpair[r, c, :, g, :], bbar[r, c, :, :]))
                link(pool.memset(pw[:, 0, :, 0:1], 1.0))
                link(pool.memset(pw[:, 1, :, 0:1], 0.0))
                link(CP(pw[:, :, :, 1:2].rearrange("p c q o -> p c (q o)"), apar[:, 0:2, :]))
                for n in (1, 2, 4):
                    t = [tmp[:, i, 0:16 * n].rearrange("p (q h) -> p q h", h=n) for i in range(2)]
                    cmul(pw[:, 0, :, n + 1:2 * n + 1], pw[:, 1, :, n + 1:2 * n + 1], pw[:, 0, :, 1:n + 1], pw[:, 1, :, 1:n + 1],
                         pw[:, 0, :, n:n + 1].to_broadcast([P, SSM_Q, n]), pw[:, 1, :, n:n + 1].to_broadcast([P, SSM_Q, n]), *t)
                for j in range(8):
                    link(CP(pwr[:, :, :, j:j + 1].rearrange("p c q o -> p c (q o)"),
                            pw[:, :, :, 7 - j:8 - j].rearrange("p c q o -> p c (q o)")))

            def ssm_products(qq):
                qs = slice(4 * qq, 4 * qq + 4)

                def b4(x, n):
                    return x.unsqueeze(3).to_broadcast([P, 4, n, 16])

                def b3(x, n):
                    return x.unsqueeze(2).to_broadcast([P, 4, n, 16])
                if qq >= 1:
                    pool.wait_ge(sem("w1_t"), qq)
                    pool.wait_ge(sem("kk_t"), qq)
                    pool.wait_ge(sem("w2_out"), 32 * qq)
                t = [tmp[:, i, 0:512].rearrange("p (q j h) -> p q j h", q=4, j=8) for i in range(2)]
                o = [w1t[:, c].rearrange("p q (j h) -> p q j h", j=8) for c in range(2)]
                cmul(o[0], o[1], b4(pwr[:, 0, qs, :], 8), b4(pwr[:, 1, qs, :], 8), b3(bbar[:, 0, qs, :], 8), b3(bbar[:, 1, qs, :], 8), *t)
                t = [tmp[:, i, :].rearrange("p (q j h) -> p q j h", q=4, j=9) for i in range(2)]
                cmul(cpw[:, 0], t[0], b4(pw[:, 0, qs, :], 9), b4(pw[:, 1, qs, :], 9), b3(ctp[:, 0, qs, :], 9), b3(ctp[:, 1, qs, :], 9), *t)
                link(TS(cpw[:, 1], t[0], -1.0, None, ALU.mult))
                pool.sem_inc(sem("w1t"), 1)

            ssm_setup()
            for qq in range(SSM_Q // 4):
                ssm_products(qq)
            pool.wait_ge(sem("p_used"), 8)
            pool.dma_start(rope[:], a["rope_table"]).then_inc(sem("rope_in"), 16)
            pool.wait_ge(sem("krot"), 3)
            for h in range(HEADS):
                if h == 0:
                    pool.wait_ge(sem("nckv_lo"), since("nckv_lo", 2))
                pool.tensor_copy(km[64:96, h, :], krot[64:96, :]).then_inc(sem("km_rope"), 1)
            pool.wait_ge(sem("ukv_done"), 1)
            pool.wait_ge(sem("km_rope"), HEADS)
            pool.dma_start(cbias[:], a["cmp_bias"]).then_inc(sem("cbias_in"), 16)
            pool.dma_start(bias[:], a["alibi"]).then_inc(sem("bias_in"), 16)
            pool.dma_start(cmask[:], a["causal"]).then_inc(sem("cmask_in"), 16)

            pool.wait_ge(sem("rel_out"), 16)
            pool.dma_start(scr["relp"], bass.AP(scr["rel"].tensor, 0, [[0, P], [640, HEADS], [1, 640]])).then_inc(sem("relp_out"), 16)
            pool.wait_ge(sem("relp_out"), 16)
            pool.wait_ge(sem("fc2_evac"), 8)
            pool.memset(tmat[:], 0.0).then_inc(sem("tz"), 1)
            pool.dma_start(w1s[:], scr["w1"].rearrange("c p q n -> p c q n")).then_inc(sem("w1s_in"), 16)
            pool.wait_ge(sem("tz"), 1)
            for j in range(SSM_L):
                for g in range(2):
                    pool.dma_start(tmat[16 * j:16 * j + 16, g:32:2, 16 * j:P],
                                   scr["kk"][16 * g:16 * g + 16, :, 0:P - 16 * j]).then_inc(sem("t_in"), 16)
            for m in range(4):
                freed(pool, G_IN2 + m)
                pool.dma_start(scr["u"][m], uT[:, m, :, :]).then_inc(sem("u_out"), 16)
            pool.wait_ge(sem("u_out"), 16 * 4)
            for j in range(SSM_L):
                pool.dma_start(ug[16 * j:16 * j + 16, :, :],
                               bass.AP(scr["u"].tensor, j * SSM_C, [[T, 16], [16 * T, 32], [1, SSM_C]])).then_inc(sem("u_in"), 16)
            pool.wait_ge(sem("s_done"), 1)
            pool.dma_start(w2s[:], scr["w2"].rearrange("c p q n -> p c q n")).then_inc(sem("w2s_in"), 16)
            pool.wait_ge(sem("ssm_y"), 1)
            pool.dma_start(bias2[:], bass.AP(scr["relp"].tensor, P - 1, [[HEADS * 640 - 1, P], [640, HEADS], [1, T]])
                           ).then_inc(sem("bias2_in"), 16)
            pool.wait_ge(sem("bias2_in"), 16)
            pool.memset(bias2[0:64, :, T - 64:T], NEG).then_inc(sem("bias2_ok"), 1)
            pool.wait_ge(sem("yg_ev"), 4)
            pool.dma_start(scr["y"], yg[:].rearrange("p g c -> p (g c)")).then_inc(sem("y_out"), 16)
            pool.wait_ge(sem("y_out"), 16)
            for m in range(4):
                for g in range(8):
                    pool.dma_start(yssm[16 * g:16 * g + 16, m, :, :],
                                   bass.AP(scr["y"].tensor, (8 * m + g) * SSM_C, [[32 * SSM_C, 16], [16 * 32 * SSM_C, SSM_L], [1, SSM_C]])
                                   ).then_inc(sem("y_in"), 16)
            pool.wait_ge(sem("fc2b_free"), 1)
            pool.dma_start(gfin[:], a["norm_final_g_2"].partition_broadcast(P)).then_inc(sem("gfin_in"), 16)
            pool.wait_ge(sem("gfin_in"), 16)

        @block.tensor
        def _(pe):
            def mm3(o, lhi, llo, rhi, rlo, start, stop, skip=False):
                pe.matmul(o, lhi, rhi, start=start, stop=False, skip_group_check=skip)
                pe.matmul(o, lhi, rlo, start=False, stop=False, skip_group_check=skip)
                return pe.matmul(o, llo, rhi, start=False, stop=stop, skip_group_check=skip)

            def unit_ready(u):
                pe.wait_ge(sem("w_lo"), u + 1)

            def bank_free(g):
                if g >= 2:
                    freed(pe, g - 2)

            def dense(u, g, hi, lo, kt=KD, off=0, mcols=P, stride=P, ready=None, first=0):
                for k in range(kt):
                    if ready is not None:
                        pe.wait_ge(sem(ready), since(ready, k + 1))
                    last = mm3(ps[0:mcols, bank(g), :], whi[:, slot(u), off + k * stride:off + k * stride + mcols],
                               wlo[:, slot(u), off + k * stride:off + k * stride + mcols],
                               hi[:, first + k, :], lo[:, first + k, :], k == 0, k == kt - 1)
                return last

            def norm_sum(nm):
                pe.wait_ge(sem(nm + "_ac"), since(nm + "_ac", NORM[nm][1]))
                pe.matmul(ps[:, 7, :], ones[:, :], hb[:, 0, :], start=True, stop=True).then_inc(sem(nm + "_st"), 1)

            def attention(nm):
                heads, sb, pb, tb = ATT[nm]
                N = 4 * len(heads)
                for s in range(N + 2):
                    if nm == "nsa" and s > 0 and s % 16 == 0:
                        part = s // 16 - 1
                        pe.wait_ge(sem("ada2_used"), s)
                        for n in range(KD):
                            last = pe.matmul(ps[:, 0, KD * part + n:KD * part + n + 1], ada2[:, n // 4, P * (n % 4):P * (n % 4) + P],
                                             ones[:, 0:1], start=True, stop=True)
                        last.then_inc(sem("ada2_t"), 1)
                    if s < N:
                        hd, b = heads[s // 4], s % 4
                        if s >= 2:
                            pe.wait_ge(sem(nm + "_s"), since(nm + "_s", s - 1))
                        w = P * (b + 1)
                        pe.matmul(ps[:, 2 + s % 2, 0:w], hd["q"][:, P * b:P * b + P], hd["k"][:, 0:w],
                                  start=True, stop=True).then_inc(sem(nm + "_qk"), 1)
                    if 1 <= s <= N:
                        r = s - 1
                        b = r % 4
                        pe.wait_ge(sem(nm + "_p"), since(nm + "_p", r + 1))
                        if r >= 2:
                            pe.wait_ge(sem(nm + ("_pta" if r % 2 else "_ptd")), since(nm + ("_pta" if r % 2 else "_ptd"), r // 2))
                        for kb in range(b + 1):
                            last = pe.transpose(ps[:, 4 + r % 2, P * kb:P * kb + P], pb[:, r % 3, P * kb:P * kb + P], ident[:, :])
                        last.then_inc(sem(nm + "_t"), 1)
                    if s >= 2:
                        r = s - 2
                        hi_, b = r // 4, r % 4
                        pe.wait_ge(sem(nm + ("_pta" if r % 2 else "_ptd")), since(nm + ("_pta" if r % 2 else "_ptd"), r // 2 + 1))
                        if b == 0 and hi_ >= 2:
                            pe.wait_ge(sem(nm + "_o"), since(nm + "_o", hi_ - 1))
                        for kb in range(b + 1):
                            last = pe.matmul(ps[:, 6 + hi_ % 2, DH * b:DH * b + DH], tb[:, r % 3, P * kb:P * kb + P],
                                             heads[hi_]["v"](kb), start=(kb == 0), stop=(kb == b))
                        last.then_inc(sem(nm + "_pv"), 1)

            pe.wait_ge(sem("ident_in"), 16)
            pe.wait_ge(sem("x_in"), 16)
            for k in range(KD):
                if k >= 2:
                    pe.wait_ge(sem("xt_ev"), k - 1)
                for t in range(TT):
                    last = pe.transpose(ps[:, 2 + k % 2, P * t:P * t + P], xs[:, t, P * k:P * k + P], ident[:, :])
                last.then_inc(sem("xt_t"), 1)
                if k == 1:
                    pe.wait_ge(sem("vec_in"), 16 * (len(VROWS) + 2))
                    pe.transpose(ps[:, 4, 0:NV], vrow[0:NV, 0, :], ident[0:NV, 0:NV])
                    pe.transpose(ps[:, 4, NV:NV + 32], vrow[0:32, 1, :], ident[0:32, 0:32]).then_inc(sem("vec_t"), 1)
            pe.wait_ge(sem("ones_ok"), 1)
            norm_sum("n1")

            for part in range(2):
                pe.wait_ge(sem("ada_used"), 8 * part + 8)
                for n in range(KD):
                    last = pe.matmul(ps[:, 5, KD * part + n:KD * part + n + 1], ada1[:, part, P * n:P * n + P], ones[:, 0:1],
                                     start=True, stop=True)
                last.then_inc(sem("ada_t"), 1)

            def parameters():
                pe.wait_ge(sem("par"), 1)
                pe.wait_ge(sem("parb_in"), 16 * 6)
                for i in range(7):
                    pe.transpose(ps[:, 2, 16 * i:16 * i + 16], pv[0:16, i, :], ident[0:16, 0:16])
                for c in range(2):
                    for m in range(4):
                        last = pe.transpose(ps[:, 3 + c, P * m:P * m + P], craw[:, c, m, :, :].rearrange("p r n -> p (r n)"), ident[:, :])
                last.then_inc(sem("par_t"), 1)

            def ssm_chunk(qq):
                pe.wait_ge(sem("w1t"), qq + 1)
                if qq >= 1:
                    pe.wait_ge(sem("stg_ev"), 3 * qq)
                else:
                    pe.wait_ge(sem("cmp_free"), 3)
                for c in range(2):
                    for i in range(4):
                        last = pe.transpose(ps[:, 2 + c, P * i:P * i + P], w1t[:, c, i, :], ident[:, :])
                last.then_inc(sem("w1_t"), 1)
                for i in range(4):
                    for c in range(2):
                        last = pe.matmul(ps[0:32, 4, P * i:P * i + P], bpair[:, c, 4 * qq + i, :, :].rearrange("p g h -> p (g h)"),
                                         cpw[:, c, i, 0:8, :].rearrange("p j h -> p (j h)"), start=(c == 0), stop=(c == 1))
                last.then_inc(sem("kk_t"), 1)

            def compress():
                pe.wait_ge(sem("par_ev"), 3)
                for w in range(2):
                    pe.wait_ge(sem("flat"), w + 1)
                    if w == 1:
                        pe.wait_ge(sem("hid"), 4)
                    pe.wait_ge(sem(f"cmpw_in{w}"), 16 * 4)
                    for i in range(4):
                        for m in range(4):
                            for half in range(2):
                                last = pe.matmul(ps[:, 2 + half, 0:62],
                                                 cmpw[4 * w + i][:, 256 * m + P * half:256 * m + P * half + P],
                                                 flat[:, w, 4 * i + m, :],
                                                 start=(i == 0 and m == 0), stop=(i == 3 and m == 3))
                        last.then_inc(sem("p_used"), 1)
                pe.wait_ge(sem("hid"), 8)
                pe.wait_ge(sem("w2_in"), 48)
                for half in range(2):
                    last = pe.matmul(ps[:, 4, 0:62], w2d[:, half, :, :].rearrange("p r d -> p (r d)"),
                                     hid[:, 0, half, :, 0:NCMP], start=(half == 0), stop=(half == 1))
                pe.wait_ge(sem("hidr"), 2)
                for g in range(2):
                    for half in range(2):
                        last = pe.matmul(ps[:, 5, DH * g:DH * g + DH],
                                         hidr[:, half, g, :, :].rearrange("p r n -> p (r n)"), w2v[:, half, :],
                                         start=(half == 0), stop=(half == 1))
                last.then_inc(sem("cmp_t"), 1)

            for i in range(len(A1_COLS)):
                u, g = U_A1 + i, G_A1 + i
                unit_ready(u)
                bank_free(g)
                if A1_COLS[i] in (C_VS, C_VW):
                    for t in range(TT):
                        for k in range(KD):
                            last = mm3(ps[:, bank(g), P * t:P * t + P], hhi[:, k, P * t:P * t + P], hlo[:, k, P * t:P * t + P],
                                       whi[:, slot(u), P * k:P * k + P], wlo[:, slot(u), P * k:P * k + P], k == 0, k == KD - 1)
                else:
                    last = dense(u, g, hhi, hlo, ready="n1_lo" if i == 0 else None)
                last.then_inc(sem("tile"), 1)
                if i == 1:
                    parameters()
                if i == 4:
                    compress()
                if i in (8, 10, 12):
                    ssm_chunk((i - 8) // 2)
            ssm_chunk(3)
            u, g = U_TAIL, G_A1 + 15
            unit_ready(u)
            bank_free(g)
            dense(u, g, hhi, hlo).then_inc(sem("tile"), 1)
            pe.wait_ge(sem("zg"), 1)
            pe.wait_ge(sem("stg_ev"), 12)
            for t in range(TT):
                last = pe.transpose(ps[:, 2, 24 * t:24 * t + 24], zg[0:24, P * t:P * t + P], ident[0:24, 0:24])
            last.then_inc(sem("gate_t"), 1)
            norm_sum("ncq")
            for h in range(HEADS):
                u, g = U_UQ + h // 2, G_UQ + h
                if h % 2 == 0:
                    unit_ready(u)
                bank_free(g)
                dense(u, g, cqhi, cqlo, kt=3, off=P * (h % 2), stride=2 * P,
                      ready="ncq_lo" if h == 0 else None).then_inc(sem("tile"), 1)
                if h == 0:
                    pe.wait_ge(sem("ncq_lo"), since("ncq_lo", 3))
                    norm_sum("nckv")
            u = U_UK
            unit_ready(u)
            for i in range(4):
                g = G_UK + i
                bank_free(g)
                dense(u, g, ckhi, cklo, kt=2, off=P * i, stride=512,
                      ready="nckv_lo" if i == 0 else None).then_inc(sem("tile"), 1)
            u = U_UV
            unit_ready(u)
            for t in range(TT):
                g = G_UV + t
                bank_free(g)
                for k in range(2):
                    last = mm3(ps[:, bank(g), :], ckhi[:, k, P * t:P * t + P], cklo[:, k, P * t:P * t + P],
                               whi[:, slot(u), 512 * k:512 * k + 512], wlo[:, slot(u), 512 * k:512 * k + 512], k == 0, k == 1)
                last.then_inc(sem("tile"), 1)
            last = None
            pe.wait_ge(sem("gates"), 1)
            for b in range(TT):
                for h in range(HEADS):
                    r = slice(64 * (h % 2), 64 * (h % 2) + 64)
                    c = 32 * (4 * b + h // 2)
                    last = pe.matmul(ps[:, 2 + h % 2, c:c + NCMP], qT[r, h // 2, P * b:P * b + P], kcT[r, h // 4, :],
                                     start=True, stop=True)
            last.then_inc(sem("cs_t"), 1)
            pe.wait_ge(sem("cp"), 1)
            for b in range(TT):
                for g in range(2):
                    last = pe.transpose(ps[:, 4 + b // 2, P * (2 * (b % 2) + g):P * (2 * (b % 2) + g) + P],
                                        cp[:, 8 * b + 4 * g:8 * b + 4 * g + 4, :].rearrange("p h n -> p (h n)"), ident[:, :])
            last.then_inc(sem("cp_t"), 1)
            pe.wait_ge(sem("cpt"), 2)
            for b in range(TT):
                for g in range(2):
                    last = pe.matmul(ps[:, (6, 7, 2, 3)[b], 256 * g:256 * g + 256],
                                     cpt[:, 2 * b + g, :], vblk[:, g, :, :].rearrange("p h d -> p (h d)"), start=True, stop=True)
            last.then_inc(sem("oc_t"), 1)
            pe.wait_ge(sem("oc_ev"), 2)
            freed(pe, G_Y - 2)
            attention("nsa")
            pe.wait_ge(sem("nsa_o"), since("nsa_o", 16))
            attention("mla")

            pe.wait_ge(sem("mla_o"), since("mla_o", 8))
            for i in range(8):
                src = (onsa, omla)[i // 4]
                if i >= 2:
                    pe.wait_ge(sem("ot_lo"), i - 1)
                for t in range(TT):
                    last = pe.transpose(ps[:, 4 + i % 2, P * t:P * t + P], src[:, t, P * (i % 4):P * (i % 4) + P], ident[:, :])
                last.then_inc(sem("ot_t"), 1)
            pe.wait_ge(sem("modc"), 2)
            for n in range(KD):
                for j in range(2):
                    u, g = U_Y + 3 * n + j, G_Y + 4 * n + j
                    unit_ready(u)
                    bank_free(g)
                    dense(u, g, hhi, hlo).then_inc(sem("tile"), 1)
                u = U_Y + 3 * n + 2
                unit_ready(u)
                for j in range(2):
                    g = G_Y + 4 * n + 2 + j
                    bank_free(g)
                    if n == 0 and j == 0:
                        pe.wait_ge(sem("ot_lo"), 8)
                    dense(u, g, othi, otlo, kt=4, off=512 * j, first=4 * j).then_inc(sem("tile"), 1)

            def dense_loop(u0, g0, n, hi, lo, ready=None):
                with loop(pe, n // RING) as i:
                    for j in range(RING):
                        pe.wait_ge(sem("w_lo"), u0 + RING * i + j + 1)
                        freed(pe, g0 + j - 2, i)
                        if ready and j == 0:
                            pe.wait_ge(sem(ready[0]), since(*ready))
                        dense(u0 + j, g0 + j, hi, lo).then_inc(sem("tile"), 1)

            dense_loop(U_OUT, G_OUT, KD, yhi, ylo, ("y_lo", KD))
            norm_sum("n2")
            dense_loop(U_FC1, G_FC1, NF1, hhi, hlo, ("n2_lo", KD))

            def rows_acc(u0, n, nm, natural, g_last):
                freed(pe, g_last - 1)
                freed(pe, g_last)

                def product(j, b, start, stop):
                    u, f = u0 + j, j % 2
                    if natural:
                        t, c = b // 2, 512 * (b % 2)
                        return mm3(ps[:, b, :], fhi[:, f, P * t:P * t + P], flo[:, f, P * t:P * t + P],
                                   whi[:, slot(u), c:c + 512], wlo[:, slot(u), c:c + 512], start, stop)
                    return mm3(ps[:, b, :], whi[:, slot(u), P * b:P * b + P], wlo[:, slot(u), P * b:P * b + P],
                               fhi[:, f, :], flo[:, f, :], start, stop)

                def step(j, idx, start, stop):
                    pe.wait_ge(sem("w_lo"), u0 + idx + 1)
                    pe.wait_ge(sem(nm + "_lo"), since(nm + "_lo", idx + 1))
                    for b in range(8):
                        last = product(j, b, start, stop)
                    last.then_inc(sem(nm + "_used"), 1)
                for j in range(2):
                    step(j, j, j == 0, False)
                turns = (n - 4) // 4
                with loop(pe, turns) as i:
                    for j in range(4):
                        step(2 + j, 4 * i + 2 + j, False, False)
                for j in range(2 + 4 * turns, n - 2):
                    step(j, j, False, False)
                pe.wait_ge(sem("w_lo"), u0 + n)
                pe.wait_ge(sem(nm + "_lo"), since(nm + "_lo", n))
                for b in range(8):
                    for j in (n - 2, n - 1):
                        last = product(j, b, False, j == n - 1)
                    last.then_inc(sem(nm + "_bank"), 1)

            rows_acc(U_FC2, NF1, "f1", False, G_FC1 + NF1 - 1)
            for k in range(KD):
                pe.wait_ge(sem("n3_sq"), since("n3_sq", k + 1))
                if k == 0:
                    pe.wait_ge(sem("fc2_evac"), 1)
                last = pe.matmul(ps[:, 0, :], ones[:, :], sq3[:, k, :], start=(k == 0), stop=(k == KD - 1))
            last.then_inc(sem("xf_st"), 1)
            pe.wait_ge(sem("fc2_evac"), 8)
            norm_sum("n3")
            dense_loop(U_IN2, G_IN2, 8, hhi, hlo, ("n3_lo", KD))
            pe.wait_ge(sem("u_in"), 16 * SSM_L)
            pe.wait_ge(sem("w1s_in"), 16)
            for c in range(2):
                for g in range(32):
                    q, r = g // 2, slice(64 * (g % 2), 64 * (g % 2) + 64)
                    last = pe.matmul(ps[r, 2 + 2 * c + q // 8, SSM_C * (q % 8):SSM_C * (q % 8) + SSM_C],
                                     w1s[:, c, q, r], ug[:, g, :], start=True, stop=True)
            last.then_inc(sem("s_done"), 1)
            dense_loop(U_IN2 + 8, G_IN2 + 8, 4, hhi, hlo)
            pe.wait_ge(sem("s_ev"), 4)
            for i in range(4):
                u = U_V2 + i
                unit_ready(u)
                for t in range(TT):
                    for k in range(2):
                        last = mm3(ps[:, 2 + t, :], hhi[:, 2 * i + k, P * t:P * t + P], hlo[:, 2 * i + k, P * t:P * t + P],
                                   whi[:, slot(u), 512 * k:512 * k + 512], wlo[:, slot(u), 512 * k:512 * k + 512],
                                   i == 0 and k == 0, i == 3 and k == 1)
                last.then_inc(sem("v2_t"), 1)
            pe.wait_ge(sem("v2_ev"), 4)
            pe.wait_ge(sem("xst"), 2)
            pe.wait_ge(sem("w2s_in"), 16)
            pe.wait_ge(sem("t_in"), 16 * 2 * SSM_L)
            for g in range(32):
                q, r = g // 2, slice(64 * (g % 2), 64 * (g % 2) + 64)
                o = ps[:, 2 + 2 * (g % 2) + q // 8, SSM_C * (q % 8):SSM_C * (q % 8) + SSM_C]
                pe.matmul(o, w2s[r, 0, q, :], sB[r, q, :], start=True, stop=False)
                pe.matmul(o, w2s[r, 1, q, :], sA[r, q, :], start=False, stop=False)
                last = pe.matmul(o, tmat[:, g, :], ug[:, g, :], start=False, stop=True)
            last.then_inc(sem("ssm_y"), 1)
            pe.wait_ge(sem("yg_ev"), 4)
            attention("chk")
            for i in range(4):
                u, g = U_GLU + i // 2, G_GLU + i
                unit_ready(u)
                bank_free(g)
                if i == 0:
                    pe.wait_ge(sem("g_lo"), 4)
                dense(u, g, ghi, glo, kt=4, off=P * (i % 2), stride=2 * P).then_inc(sem("tile"), 1)
            for i in range(4):
                if i >= 2:
                    pe.wait_ge(sem("ya_hb"), i - 1)
                for t in range(TT):
                    if i == 0:
                        pe.wait_ge(sem("ya_n"), t + 1)
                    last = pe.transpose(ps[:, 4 + i % 2, P * t:P * t + P], yatt[:, t, P * i:P * i + P], ident[:, :])
                last.then_inc(sem("ya_t"), 1)
            pe.wait_ge(sem("chk_o"), since("chk_o", 8))
            norm_sum("nssm")
            dense_loop(U_OUT2, G_OUT2, KD, hhi, hlo, ("nssm_lo", 4))
            norm_sum("n4")
            for t in range(TT):
                for half in range(2):
                    i = 2 * t + half
                    if i >= 4:
                        pe.wait_ge(sem("xn_ev"), i - 3)
                    for k in range(4):
                        last = pe.transpose(ps[:, 2 + i % 4, P * k:P * k + P], xT[:, 4 * half + k, P * t:P * t + P], ident[:, :])
                    last.then_inc(sem("xn_t"), 1)
            dense_loop(U_GU, G_GU, 2 * NF2, hhi, hlo, ("n4_lo", KD))
            pe.wait_ge(sem("xn_ev"), 8)
            rows_acc(U_DN, NF2, "f2", True, G_GU + 2 * NF2 - 1)

        @block.scalar
        def _(act):
            A = act.activation

            def split_hi(u):
                act.wait_ge(sem(f"w_in{slot(u)}"), 16 * w_count(u))
                if u >= RING:
                    name, value = used(u - RING)
                    act.wait_ge(sem(name), value)
                A(whi[:, slot(u), :], wraw[:, slot(u), :], ACT.Copy).then_inc(sem("w_hi"), 1)

            def split_hi_turn(u, i, name, value):
                act.wait_ge(sem(f"w_in{slot(u)}"), 16 * w_count(u) + 16 * i)
                act.wait_ge(sem(name), value)
                A(whi[:, slot(u), :], wraw[:, slot(u), :], ACT.Copy).then_inc(sem("w_hi"), 1)

            def ssm_out(qq):
                act.wait_ge(sem("w1t"), qq + 1)
                for c in range(2):
                    act.dma_start(scr["w2"][c, :, 4 * qq:4 * qq + 4, :],
                                  cpw[:, c, :, 1:9, :].rearrange("p q j h -> p q (j h)")).then_inc(sem("w2_out"), 16)
                act.wait_ge(sem("w1_t"), qq + 1)
                if qq >= 1:
                    act.wait_ge(sem("w1_out"), 32 * qq)
                    act.wait_ge(sem("kk_out"), 16 * qq)
                for c in range(2):
                    A(stg[:, c, :, :].rearrange("p q n -> p (q n)"), ps[:, 2 + c, :], ACT.Copy).then_inc(sem("stg_ev"), 1)
                act.wait_ge(sem("kk_t"), qq + 1)
                A(kst[0:32, :, :].rearrange("p g n -> p (g n)"), ps[0:32, 4, :], ACT.Copy).then_inc(sem("stg_ev"), 1)
                act.wait_ge(sem("stg_ev"), 3 * qq + 3)
                for c in range(2):
                    act.dma_start(scr["w1"][c, :, 4 * qq:4 * qq + 4, :], stg[:, c, :, :]).then_inc(sem("w1_out"), 16)
                act.dma_start(scr["kk"][:, 4 * qq:4 * qq + 4, :], kst[0:32, :, :]).then_inc(sem("kk_out"), 16)

            def nxt(u):
                if u + AHEAD < U_END:
                    split_hi(u + AHEAD)

            def norm_square(nm, k):
                src, n, buf = NORM[nm]
                if k >= 4:
                    act.wait_ge(sem(nm + "_ac"), since(nm + "_ac", k - 3))
                A(buf[:, k % 4, :], src(k), ACT.Square).then_inc(sem(nm + "_sq"), 1)

            def norm_root(nm, width):
                act.wait_ge(sem(nm + "_st"), since(nm + "_st", 1))
                A(hb[:, 1, :], ps[:, 7, :], ACT.Sqrt, scale=1.0 / width, bias=eps[:, 0:1]).then_inc(sem(nm + "_rt"), 1)

            def norm_squares(nm, width, waits=None):
                for k in range(NORM[nm][1]):
                    if waits:
                        waits(k)
                    norm_square(nm, k)
                norm_root(nm, width)

            def norm_hi(nm):
                _, add, hi, _ = AFTER[nm]
                for k in range(NORM[nm][1]):
                    act.wait_ge(sem(nm + "_h"), since(nm + "_h", k + 1))
                    if add is None:
                        e = A(hi[:, k, :], hb[:, k % 2, :], ACT.Copy)
                    else:
                        e = A(hi[:, k, :], hb[:, k % 2, :], ACT.Identity, bias=add(k))
                    e.then_inc(sem(nm + "_hi"), 1)

            def copy_out(dst, src, g, last=True):
                act.wait_ge(sem("tile"), g + 1)
                e = A(dst, src, ACT.Copy)
                return free(e, g) if last else e

            def attention(nm):
                heads, sb, pb, tb = ATT[nm]
                N = 4 * len(heads)
                for s in range(N + 1):
                    if s < N:
                        hd, b = heads[s // 4], s % 4
                        w = P * (b + 1)
                        act.wait_ge(sem(nm + "_s"), since(nm + "_s", s + 1))
                        if s >= 3:
                            act.wait_ge(sem(nm + "_t"), since(nm + "_t", s - 2))
                        if b == 0 and s >= 8:
                            act.wait_ge(sem(nm + "_o"), since(nm + "_o", s // 4 - 1))
                        A(pb[:, s % 3, 0:w], sb[:, s % 2, 0:w], ACT.Exp, bias=smax[:, s % 4:s % 4 + 1], scale=-1.0,
                          accum_out=rsum[:, (s // 4) % 2, b:b + 1]).then_inc(sem(nm + "_p"), 1)
                    r = s - 1
                    if r >= 0 and r % 2:
                        w = P * (r % 4 + 1)
                        act.wait_ge(sem(nm + "_t"), since(nm + "_t", r + 1))
                        if r >= 3:
                            act.wait_ge(sem(nm + "_pv"), since(nm + "_pv", r - 2))
                        A(tb[:, r % 3, 0:w], ps[:, 4 + r % 2, 0:w], ACT.Copy).then_inc(sem(nm + "_pta"), 1)

            act.dma_start(ident[:], a["identity"]).then_inc(sem("ident_in"), 16)
            for i, name in enumerate(("ssm_lam_re_2", "ssm_lam_im_2")):
                act.dma_start(pv[0:16, 20 + i, :], bass.AP(a[name].tensor, 0, [[P, 16], [1, P]])).then_inc(sem("par_in"), 16)
            act.dma_start(dtl[0:16, 0, :], bass.AP(a["ssm_log_dt_2"].tensor, 0, [[2, 16], [1, 2]])).then_inc(sem("par_in"), 16)
            for name, (r, n) in VROWS.items():
                v = a[name]
                act.dma_start(vrow[r:r + n, 0, :], bass.AP(v.tensor, 0, [[P, n], [1, P]])).then_inc(sem("vec_in"), 16)
            for i, name in enumerate(("pe_ck", "pe_cv")):
                act.dma_start(vrow[16 * i:16 * i + 16, 1, :], bass.AP(a[name].tensor, 0, [[P, 16], [1, P]])).then_inc(sem("vec_in"), 16)
            for i, name in enumerate(("ssm_b_re_2", "ssm_b_im_2")):
                act.dma_start(braw[:, i, :, :], a[name][0].rearrange("(q g) p h -> (g p) q h", g=2)).then_inc(sem("parb_in"), 16)
            for i, name in enumerate(("ssm_c_re_2", "ssm_c_im_2")):
                for r in range(2):
                    act.dma_start(craw[:, i, :, r, :],
                                  bass.AP(a[name].tensor, 0, [[64, P], [64 * P, 4], [1, 64]])).then_inc(sem("parb_in"), 16)
            for r in range(2):
                act.dma_start(w2d[:, :, r, :], a["w_ck2"][0].rearrange("(k p) n -> p k n", p=P)).then_inc(sem("w2_in"), 16)
            act.dma_start(w2v[:], a["w_cv2"][0].rearrange("(k p) n -> p k n", p=P)).then_inc(sem("w2_in"), 16)
            act.dma_start(rel[0:8, 383:640], a["attn_rel_bias_2"][0]).then_inc(sem("rel_in"), 16)

            for k in range(KD):
                act.wait_ge(sem("xt_t"), k + 1)
                A(xT[:, k, :], ps[:, 2 + k % 2, :], ACT.Copy).then_inc(sem("xt_ev"), 1)
            act.wait_ge(sem("eps_ok"), 1)
            norm_squares("n1", D, lambda k: act.wait_ge(sem("xt_ev"), k + 1))
            act.wait_ge(sem("rel_ok"), 1)
            act.dma_start(scr["rel"], rel[0:8, :]).then_inc(sem("rel_out"), 16)
            for u in range(AHEAD):
                split_hi(u)
            norm_hi("n1")
            for i in range(len(A1_COLS)):
                u, g, c = U_A1 + i, G_A1 + i, A1_COLS[i]
                nxt(u)
                if c in (C_KC, C_VC):
                    w = i
                    act.wait_ge(sem("tile"), g + 1)
                    for gr in range(2):
                        A(x2[0:64, w, gr, :], ps[64 * gr:64 * gr + 64, bank(g), :], ACT.Copy).then_inc(sem("x2"), 1)
                        e = A(x2[64:128, w, gr, 0:T - 1], ps[64 * gr:64 * gr + 64, bank(g), 1:T], ACT.Copy)
                        e.then_inc(sem("x2"), 1) if gr == 0 else free(e, g)
                elif c in (C_VS, C_VW):
                    br = 0 if c == C_VS else 1
                    copy_out(vnat[:, :, br, :], ps[:, bank(g), :].rearrange("p (t n) -> p t n", t=TT), g)
                elif C_Q <= c < 512:
                    copy_out(qT[:, c // P, :], ps[:, bank(g), :], g)
                elif c >= C_QD:
                    j = i - 10
                    if j == 0:
                        act.wait_ge(sem("cmp_free"), 3)
                    copy_out(zl[:, j, :], ps[:, bank(g), :], g)
                if i == 4:
                    for w in range(2):
                        act.wait_ge(sem("p_used"), 4 * (w + 1))
                        for half in range(2):
                            for gr in range(2):
                                A(hid[:, w, half, gr, 0:NCMP], ps[:, 2 + half, NCMP * gr:NCMP * gr + NCMP],
                                  ACT.Silu).then_inc(sem("hid"), 1)
                    act.wait_ge(sem("cmp_t"), 1)
                    A(kcT[:].rearrange("p g n -> p (g n)"), ps[:, 4, 0:62], ACT.Copy).then_inc(sem("cmp_free"), 1)
                if i in (9, 11, 13):
                    ssm_out((i - 9) // 2)
            ssm_out(3)
            nxt(U_TAIL)
            act.wait_ge(sem("tile"), G_A1 + 16)
            A(zg[0:24, :], ps[0:24, bank(15), :], ACT.Sigmoid).then_inc(sem("zg"), 1)
            freed(act, 13)
            freed(act, 14)
            act.wait_ge(sem("kk_out"), 64)
            norm_squares("ncq", 384)
            norm_hi("ncq")
            act.wait_ge(sem("w1_out"), 128)
            act.wait_ge(sem("w2_out"), 128)
            act.wait_ge(sem("gate_t"), 1)
            for h in range(HEADS):
                u, g = U_UQ + h // 2, G_UQ + h
                if h % 2 == 0:
                    nxt(u)
                copy_out(qm[0:64, h, :], ps[0:64, bank(g), :], g, last=False).then_inc(sem("qm"), 1)
                if h == 0:
                    norm_squares("nckv", 256)
                    norm_hi("nckv")
            nxt(U_UK)
            for i in range(4):
                g = G_UK + i
                if i == 0:
                    act.wait_ge(sem("nckv_lo"), since("nckv_lo", 2))
                copy_out(km[0:64, 2 * i, :], ps[0:64, bank(g), :], g, last=False)
                free(A(km[0:64, 2 * i + 1, :], ps[64:128, bank(g), :], ACT.Copy), g)
            nxt(U_UV)
            for t in range(TT):
                g = G_UV + t
                copy_out(vm[:, t, :], ps[:, bank(g), :], g)
            act.wait_ge(sem("cs"), 1)
            A(cp[:, :, 0:NCMP], cs[:, :, :], ACT.Exp, scale=DH ** -0.5).then_inc(sem("ce"), 1)
            act.wait_ge(sem("cp_t"), 1)
            A(cpt[:, 0:4, :].rearrange("p b n -> p (b n)"), ps[:, 4, :], ACT.Copy).then_inc(sem("cpt"), 1)
            act.wait_ge(sem("oc_t"), 1)
            A(onsa[:, 0, :], ps[:, 6, :], ACT.Copy)
            A(onsa[:, 1, :], ps[:, 7, :], ACT.Copy).then_inc(sem("oc_ev"), 1)
            attention("nsa")
            attention("mla")
            for i in range(8):
                act.wait_ge(sem("ot_t"), i + 1)
                A(othi[:, i, :], ps[:, 4 + i % 2, :], ACT.Copy).then_inc(sem("ot_hi"), 1)
            for n in range(KD):
                for j in range(2):
                    u, g = U_Y + 3 * n + j, G_Y + 4 * n + j
                    nxt(u)
                    act.wait_ge(sem("tile"), g + 1)
                    if n >= 1:
                        freed(act, g - 2)
                    free(A(sg[:, j, :], ps[:, bank(g), :], ACT.Sigmoid), g)
                nxt(U_Y + 3 * n + 2)
                act.wait_ge(sem("y"), n + 1)
                A(yhi[:, n, :], ym[:, 2, :], ACT.Copy).then_inc(sem("y_hi"), 1)

            def residual_hi(u0, g0, nm):
                for k in range(KD):
                    split_hi(u0 + k + AHEAD)
                    freed(act, g0 + k)
                    norm_square(nm, k)
                norm_root(nm, D)
                norm_hi(nm)

            def hi_loop(u0, g0, n, evac):
                with loop(act, n // RING) as i:
                    for j in range(RING):
                        split_hi_turn(u0 + j + AHEAD, i, "tile", g0 + RING * i + j)
                        evac(i, j)
            residual_hi(U_OUT, G_OUT, "n2")

            def relu(i, j):
                g = G_FC1 + j
                act.wait_ge(sem("tile"), G_FC1 + RING * i + j + 1)
                act.wait_ge(sem("ff"), RING * i + j + 1)
                free(A(rb[:, j % 2, :], ps[:, bank(g), :], ACT.Relu), g)
            hi_loop(U_FC1, G_FC1, NF1, relu)

            def f_hi(nm, j, idx, counted):
                if counted:
                    act.wait_ge(sem(nm + "_used"), since(nm + "_used", idx - 1))
                A(fhi[:, j % 2, :], ff[:, idx, :] if isinstance(idx, int) else ff[:, bass.ds(idx, 1), :].rearrange("p a t -> p (a t)"),
                  ACT.Copy).then_inc(sem(nm + "_hi"), 1)

            def rows_hi(u0, n, nm):
                for j in range(2):
                    f_hi(nm, j, j, False)
                    split_hi(u0 + j + AHEAD)
                turns = (n - 4) // 4
                with loop(act, turns) as i:
                    for j in range(4):
                        f_hi(nm, j, 4 * i + 2 + j, True)
                        split_hi_turn(u0 + 2 + j + AHEAD, i, nm + "_used", 4 * i + 2 + j)
                for j in range(2 + 4 * turns, n):
                    f_hi(nm, j, j, True)
                    if u0 + j + AHEAD < U_END and j < n - 1:
                        split_hi(u0 + j + AHEAD)
            act.wait_ge(sem("ff"), NF1 + 2)
            rows_hi(U_FC2, NF1, "f1")
            for k in range(KD):
                act.wait_ge(sem("fc2_evac"), k + 1)
                A(sq3[:, k, :], xT[:, k, :], ACT.Square).then_inc(sem("n3_sq"), 1)
            act.wait_ge(sem("n3_ms"), 1)
            A(hb[:, 1, :], hb[:, 1, :], ACT.Sqrt, scale=1.0 / D, bias=eps[:, 1:2]).then_inc(sem("n3_rt"), 1)
            A(sq3[:, 0, :], ps[:, 0, :], ACT.Sqrt, scale=1.0 / D, bias=eps[:, 0:1]).then_inc(sem("xf_rt"), 1)
            split_hi(U_IN2 + AHEAD - 1)
            norm_hi("n3")
            for i in range(12):
                u, g = U_IN2 + i, G_IN2 + i
                nxt(u)
                if i < 4:
                    act.wait_ge(sem("tile"), g + 1)
                    free(A(uT[:, i, :, :].rearrange("p j c -> p c j"), ps[:, bank(g), :].rearrange("p (c j) -> p c j", j=SSM_L),
                           ACT.Copy), g)
                else:
                    copy_out((q2, k2)[(i - 4) // 4][:, i % 4, :], ps[:, bank(g), :], g)
                if i == 8:
                    act.wait_ge(sem("s_done"), 1)
                    for c in range(2):
                        for half in range(2):
                            A((sA, sB)[c][:, 8 * half:8 * half + 8, :].rearrange("p q c -> p (q c)"), ps[:, 2 + 2 * c + half, :],
                              ACT.Copy).then_inc(sem("s_ev"), 1)
            for i in range(4):
                nxt(U_V2 + i)
            act.wait_ge(sem("v2_t"), 4)
            for t in range(TT):
                A(v2[:, t, :], ps[:, 2 + t, :], ACT.Copy).then_inc(sem("v2_ev"), 1)
            for m in range(4):
                act.wait_ge(sem("ssm_y"), 1)
                A(yg[:, 16 * (m % 2) + m // 2:16 * (m % 2) + 16:2, :], ps[:, 2 + m, :].rearrange("p (q c) -> p q c", q=8),
                  ACT.Copy).then_inc(sem("yg_ev"), 1)
            attention("chk")
            for m in range(4):
                act.wait_ge(sem("yk"), m + 1)
                A(ygel[:, m, :].rearrange("p (c j) -> p c j", j=SSM_L), yssm[:, m, :, :].rearrange("p j c -> p c j"),
                  ACT.Gelu_apprx_tanh).then_inc(sem("gel"), 1)
            for m in range(4):
                act.wait_ge(sem("gel"), m + 1)
                A(ghi[:, m, :], ygel[:, m, :], ACT.Copy).then_inc(sem("g_hi"), 1)
            for i in range(4):
                g = G_GLU + i
                if i % 2 == 0:
                    nxt(U_GLU + i // 2)
                act.wait_ge(sem("tile"), g + 1)
                free(A(ysg[:, i, :], ps[:, bank(g), :], ACT.Sigmoid, bias=col("ssm_b_glu_2", i)), g)
            for t in range(TT):
                A(hb[:, t % 2, :], yatt[:, t, :], ACT.Square, accum_out=stat[:, 2, t:t + 1]).then_inc(sem("ya_sq"), 1)
                act.wait_ge(sem("ya_sq"), t + 1)
            act.wait_ge(sem("ya_ms"), 1)
            A(stat[:, 4, :], stat[:, 3, :], ACT.Sqrt).then_inc(sem("ya_rt"), 1)
            for i in range(4):
                act.wait_ge(sem("ya_hb"), i + 1)
                A(hhi[:, 4 + i, :], hb[:, i % 2, :], ACT.Copy).then_inc(sem("ya_hi"), 1)
            norm_squares("nssm", 512, lambda k: act.wait_ge(sem("ysg"), k + 1))
            norm_hi("nssm")
            residual_hi(U_OUT2, G_OUT2, "n4")
            for i in range(8):
                act.wait_ge(sem("xn_t"), i + 1)
                A(xn[:, i // 2, 512 * (i % 2):512 * (i % 2) + 512], ps[:, 2 + i % 4, :], ACT.Copy).then_inc(sem("xn_ev"), 1)

            def silu(i, j):
                if j % 2 == 0:
                    g = G_GU + j
                    act.wait_ge(sem("tile"), G_GU + RING * i + j + 1)
                    freed(act, G_GU + j + 1 - RING, i)
                    free(A(rb[:, j // 2, :], ps[:, bank(g), :], ACT.Silu), g)
            hi_loop(U_GU, G_GU, 2 * NF2, silu)
            freed(act, G_GU + 2 * NF2 - 1)
            rows_hi(U_DN, NF2, "f2")
            for t in range(TT):
                act.wait_ge(sem("xo"), 2 * t + 2)
                A(ff[:, 2 * (t % 2):2 * (t % 2) + 2, :].rearrange("p a b -> p (a b)"), xn[:, t, :], ACT.Square,
                  accum_out=stat[:, 5, t:t + 1]).then_inc(sem("fin_sq"), 1)
                act.wait_ge(sem("fin_ms"), t + 1)
                A(stat[:, 6, t:t + 1], stat[:, 7, t:t + 1], ACT.Sqrt).then_inc(sem("fin_rt"), 1)

        @block.vector
        def _(dve):
            chain = [0]

            def link(i):
                chain[0] += 1
                i.then_inc(sem("dve_chain"), 1)
                dve.wait_ge(sem("dve_chain"), chain[0])

            TTo, TS, STT, CP = dve.tensor_tensor, dve.tensor_scalar, dve.scalar_tensor_tensor, dve.tensor_copy

            def split_lo(u):
                dve.wait_ge(sem("w_hi"), u + 1)
                TTo(out=wlo[:, slot(u), :], in0=wraw[:, slot(u), :], in1=whi[:, slot(u), :].bitcast(F32),
                    op=ALU.subtract).then_inc(sem("w_lo"), 1)

            def nxt(u):
                if u + AHEAD < U_END:
                    split_lo(u + AHEAD)

            def norm_add(nm, k):
                buf = NORM[nm][2]
                if k == 0:
                    return
                dve.wait_ge(sem(nm + "_sq"), since(nm + "_sq", k + 1))
                if k >= 2:
                    dve.wait_ge(sem(nm + "_ac"), since(nm + "_ac", k))
                TTo(out=hb[:, 0, :], in0=buf[:, 0, :] if k == 1 else hb[:, 0, :], in1=buf[:, k % 4, :], op=ALU.add
                    ).then_inc(sem(nm + "_ac"), 2 if k == 1 else 1)

            def norm_adds(nm):
                for k in range(NORM[nm][1]):
                    norm_add(nm, k)

            def norm_inverse(nm):
                dve.wait_ge(sem(nm + "_rt"), since(nm + "_rt", 1))
                dve.reciprocal(ps[:, 7, :], hb[:, 1, :]).then_inc(sem(nm + "_r"), 1)

            def norm_apply(nm):
                src, n, _ = NORM[nm]
                mul, add, hi, lo = AFTER[nm]
                dve.wait_ge(sem(nm + "_r"), since(nm + "_r", 1))
                for k in range(n + 1):
                    if k < n:
                        if k >= 2:
                            dve.wait_ge(sem(nm + "_lo"), since(nm + "_lo", k - 1))
                        STT(out=hb[:, k % 2, :], in0=src(k), scalar=mul(k), in1=ps[:, 7, :], op0=ALU.mult, op1=ALU.mult
                            ).then_inc(sem(nm + "_h"), 1)
                    if k >= 1:
                        dve.wait_ge(sem(nm + "_hi"), since(nm + "_hi", k))
                        if add is None:
                            e = TTo(out=lo[:, k - 1, :], in0=hb[:, (k - 1) % 2, :], in1=hi[:, k - 1, :].bitcast(F32), op=ALU.subtract)
                        else:
                            e = STT(out=lo[:, k - 1, :], in0=hb[:, (k - 1) % 2, :], scalar=add(k - 1), in1=hi[:, k - 1, :].bitcast(F32),
                                    op0=ALU.add, op1=ALU.subtract)
                        e.then_inc(sem(nm + "_lo"), 1)
                dve.wait_ge(sem(nm + "_lo"), since(nm + "_lo", n))

            def attention(nm):
                heads, sb, pb, tb = ATT[nm]
                N = 4 * len(heads)
                for s in range(N + 4):
                    if nm == "nsa" and s < 64:
                        part, k, half = s // 16, s // 2 % 8, s % 2
                        dve.wait_ge(sem(f"ada2_in{s % 2}"), 16 * (s // 2 + 1))
                        if k == 0:
                            if part:
                                dve.wait_ge(sem("ada2_t"), part)
                            e = TS(ada2[:, half, :], aring2[:, half, :], col("c", k), None, ALU.mult)
                        else:
                            dve.wait_ge(sem("ada2_used"), s - 1)
                            e = STT(out=ada2[:, half, :], in0=aring2[:, half, :], scalar=col("c", k), in1=ada2[:, half, :],
                                    op0=ALU.mult, op1=ALU.add)
                        e.then_inc(sem("ada2_used"), 1)
                    if s < N:
                        hd, b = heads[s // 4], s % 4
                        w = P * (b + 1)
                        if hd["rescale"] and b == 0:
                            link(TS(bias[:].rearrange("p h n -> p (h n)"), bias[:].rearrange("p h n -> p (h n)"), 1.0 / 16.0, None, ALU.mult))
                        dve.wait_ge(sem(nm + "_qk"), since(nm + "_qk", s + 1))
                        if s >= 2:
                            dve.wait_ge(sem(nm + "_p"), since(nm + "_p", s - 1))
                        dve.tensor_tensor_reduce(out=sb[:, s % 2, 0:w], in0=ps[:, 2 + s % 2, 0:w], in1=hd["bias"][:, T - w:T],
                                                 scale=-hd["scale"], scalar=3e38, op0=ALU.add, op1=ALU.min,
                                                 accum_out=smax[:, s % 4:s % 4 + 1]).then_inc(sem(nm + "_s"), 1)
                    r = s - 2
                    if 0 <= r < N and r % 2 == 0:
                        w = P * (r % 4 + 1)
                        dve.wait_ge(sem(nm + "_t"), since(nm + "_t", r + 1))
                        if r >= 3:
                            dve.wait_ge(sem(nm + "_pv"), since(nm + "_pv", r - 2))
                        CP(tb[:, r % 3, 0:w], ps[:, 4 + r % 2, 0:w]).then_inc(sem(nm + "_ptd"), 1)
                    r = s - 4
                    if r >= 0 and r % 4 == 3:
                        finish(nm, heads, r // 4)

            def finish(nm, heads, i):
                hd = heads[i]
                dve.wait_ge(sem(nm + "_p"), since(nm + "_p", 4 * i + 4))
                dve.wait_ge(sem(nm + "_pv"), since(nm + "_pv", 4 * i + 4))
                link(dve.reciprocal(rinv[:, :], rsum[:, i % 2, :]))
                if hd["gate"] is not None:
                    link(TTo(out=rinv[:, :], in0=rinv[:, :], in1=hd["gate"], op=ALU.mult))
                pso = ps[:, 6 + i % 2, 0:4 * DH].rearrange("p (b d) -> p b d", b=4)
                rb_ = rinv[:, :].unsqueeze(2).to_broadcast([P, 4, DH])
                dst = hd["o"][:, :, DH * hd["h"]:DH * hd["h"] + DH]
                if hd["gate"] is None:
                    e = TTo(out=dst, in0=pso, in1=rb_, op=ALU.mult)
                else:
                    t_ = hb[:, 0, 0:4 * DH].rearrange("p (b d) -> p b d", b=4)
                    link(TTo(out=t_, in0=pso, in1=rb_, op=ALU.mult))
                    e = TTo(out=dst, in0=dst, in1=t_, op=ALU.add)
                e.then_inc(sem(nm + "_o"), 1)
                dve.wait_ge(sem(nm + "_o"), since(nm + "_o", i + 1))

            dve.memset(ones[:], 1.0).then_inc(sem("ones_ok"), 1)
            dve.memset(eps[:, 0:1], EPS)
            dve.memset(eps[:, 1:2], EPS * EPS).then_inc(sem("eps_ok"), 1)
            dve.sem_inc(sem("ff"), 2)

            dve.wait_ge(sem("lam_sq"), 1)
            dve.reciprocal(pv[0:16, 17, :], pv[0:16, 17, :]).then_inc(sem("lam_inv"), 1)
            dve.wait_ge(sem("vec_t"), 1)
            CP(vcol[:, :], ps[:, 4, 0:NV + 32]).then_inc(sem("vec_ok"), 1)
            dve.wait_ge(sem("vec_ok"), 1)
            gf = vcol[:, VROWS["g_final"][0]:VROWS["g_final"][0] + KD]
            TTo(out=gsq[:], in0=gf, in1=gf, op=ALU.mult)
            TTo(out=gmix2[:], in0=gf, in1=vcol[:, VROWS["norm_mix_g_2"][0]:VROWS["norm_mix_g_2"][0] + KD], op=ALU.mult)
            dve.wait_ge(sem("rel_in"), 16)
            link(TS(rel[0:8, 383:640], rel[0:8, 383:640], DH ** 0.5, None, ALU.mult))
            link(dve.memset(rel[0:8, 0:383], 0.0))
            TS(rel[0:8, 0:383], rel[0:8, 0:383], rel[0:8, 383:384], None, ALU.add).then_inc(sem("rel_ok"), 1)
            norm_adds("n1")
            norm_inverse("n1")
            for n in range(16):
                part, k = n // 8, n % 8
                dve.wait_ge(sem(f"ada_in{n % 4}"), 16 * (n // 4 + 1))
                if k == 0:
                    e = TS(ada1[:, part, :], aring[:, n % 4, :], col("c", k), None, ALU.mult)
                else:
                    dve.wait_ge(sem("ada_used"), n)
                    e = STT(out=ada1[:, part, :], in0=aring[:, n % 4, :], scalar=col("c", k), in1=ada1[:, part, :],
                            op0=ALU.mult, op1=ALU.add)
                e.then_inc(sem("ada_used"), 1)
            dve.wait_ge(sem("ada_t"), 2)
            link(TTo(out=modc[:, 0:16], in0=ps[:, 5, 0:16], in1=vcol[:, 0:16], op=ALU.add))
            STT(out=gain[:, 0, :], in0=modc[:, 8:16], scalar=1.0, in1=vcol[:, VROWS["g_mix"][0]:VROWS["g_mix"][0] + 8],
                op0=ALU.add, op1=ALU.mult).then_inc(sem("modc"), 1)
            dve.wait_ge(sem("modc"), 1)
            norm_apply("n1")
            for u in range(AHEAD):
                split_lo(u)

            def parameters():
                dve.wait_ge(sem("par_t"), 1)
                CP(apar[:].rearrange("p a q -> p (a q)"), ps[:, 2, 0:112]).then_inc(sem("par_ev"), 1)
                for c in range(2):
                    for r in range(2):
                        e = CP(ctp[64 * r:64 * r + 64, c, :, :], ps[64 * r:64 * r + 64, 3 + c, :].rearrange(
                            "p (q r h) -> p q r h", r=2, h=16)[:, :, r, :])
                e.then_inc(sem("par_ev"), 1)
                dve.wait_ge(sem("par_ev"), 1)
                CP(ssmc[:], apar[:, 4:7, :]).then_inc(sem("par_ev"), 1)

            def compress_in(w):
                dve.wait_ge(sem("x2"), 3 * (w + 1))
                freed(dve, G_A1 + w)
                for h in range(2):
                    src = x2[:, w, :, 16 * h:16 * h + 496].rearrange("p g (n b l) -> p g n b l", b=8, l=2)[:, :, :, :, 0]
                    for gr in range(2):
                        dst = flat[:, w, 8 * h:8 * h + 8, NCMP * gr:NCMP * gr + NCMP].rearrange("p b n -> p n b")
                        pe_ = vcol[:, NV + 16 * w + 8 * h:NV + 16 * w + 8 * h + 8].unsqueeze(1).to_broadcast([P, NCMP, 8])
                        TTo(out=dst, in0=src[:, gr], in1=pe_, op=ALU.add).then_inc(sem("flat_"), 1)
                dve.wait_ge(sem("flat_"), 4 * (w + 1))
                dve.sem_inc(sem("flat"), 1)

            for i in range(len(A1_COLS)):
                u, g, c = U_A1 + i, G_A1 + i, A1_COLS[i]
                nxt(u)
                if c in (C_KC, C_VC):
                    compress_in(i)
                    if i == 1:
                        parameters()
                elif c in (C_KS, C_KW):
                    br = 0 if c == C_KS else 1
                    dve.wait_ge(sem("tile"), g + 1)
                    for gr in range(2):
                        for half in range(2):
                            e = CP(kdup[64 * half:64 * half + 64, br, gr, :], ps[64 * gr:64 * gr + 64, bank(g), :])
                    free(e, g)
                if i == 4:
                    dve.memset(hidr[:, :, :, :, 31:32], 0.0).then_inc(sem("hidr"), 1)
                    dve.wait_ge(sem("hid"), 8)
                    for half in range(2):
                        for gr in range(2):
                            e = CP(hidr[:, half, gr, :, 0:NCMP], hid[:, 1, half, gr, 0:NCMP].unsqueeze(1).to_broadcast([P, 4, NCMP]))
                    e.then_inc(sem("hidr"), 1)
                    link(dve.memset(vblk[:], 0.0))
                    dve.wait_ge(sem("cmp_t"), 1)
                    for h in range(4):
                        e = CP(vblk[32 * h:32 * h + 32, :, h, :], ps[32 * h:32 * h + 32, 5, 0:2 * DH].rearrange("p (g d) -> p g d", g=2))
                    e.then_inc(sem("cmp_free"), 2)
            nxt(U_TAIL)
            dve.wait_ge(sem("rope_in"), 16)
            dve.wait_ge(sem("tile"), G_A1 + 16)
            TTo(out=krot[64:96, :], in0=ps[64:96, bank(15), :], in1=rope[64:96, :], op=ALU.mult).then_inc(sem("krot"), 1)
            TTo(out=hb[64:96, 1, :], in0=ps[96:128, bank(15), :], in1=rope[96:128, :], op=ALU.mult).then_inc(sem("krot"), 1)
            dve.wait_ge(sem("krot"), 2)
            TTo(out=krot[64:96, :], in0=krot[64:96, :], in1=hb[64:96, 1, :], op=ALU.add).then_inc(sem("krot"), 1)
            dve.wait_ge(sem("zg"), 1)
            dve.wait_ge(sem("krot"), 3)
            dve.sem_inc(sem(f"t_free{15 % 2}"), 1)
            norm_adds("ncq")
            norm_inverse("ncq")
            dve.wait_ge(sem("gate_t"), 1)
            CP(gates[:].rearrange("p t g -> p (t g)"), ps[:, 2, 0:96]).then_inc(sem("gates"), 1)
            norm_apply("ncq")
            for h in range(HEADS):
                u, g = U_UQ + h // 2, G_UQ + h
                if h % 2 == 0:
                    nxt(u)
                if h == 0:
                    norm_adds("nckv")
                    norm_inverse("nckv")
                    norm_apply("nckv")
                dve.wait_ge(sem("tile"), g + 1)
                link(TTo(out=hb[64:96, 0, :], in0=ps[64:96, bank(g), :], in1=rope[64:96, :], op=ALU.mult))
                link(TTo(out=hb[64:96, 1, :], in0=ps[96:128, bank(g), :], in1=rope[96:128, :], op=ALU.mult))
                dve.wait_ge(sem("qm"), h + 1)
                free(TTo(out=qm[64:96, h, :], in0=hb[64:96, 0, :], in1=hb[64:96, 1, :], op=ALU.add), g)
                freed(dve, g)
            nxt(U_UK)
            nxt(U_UV)
            freed(dve, G_Y - 2)
            freed(dve, G_Y - 1)
            dve.sem_inc(sem("ukv_done"), 1)
            dve.wait_ge(sem("cs_t"), 1)
            dve.wait_ge(sem("cbias_in"), 16)
            for half in range(2):
                own = [x[:].rearrange("p (i r) n -> p i r n", r=2)[:, :, half, :] for x in (cs, cbias)]
                link(TTo(out=own[0], in0=ps[:, 2 + half, :].rearrange("p (i n) -> p i n", n=32)[:, :, 0:NCMP],
                         in1=own[1], op=ALU.add))
            link(dve.tensor_reduce(out=cst[:, 0, :], in_=cs[:], op=ALU.max, axis=AX.X))
            link(TS(cst[:, 0, :], cst[:, 0, :], -1e25, None, ALU.max))
            link(dve.memset(cp[:, :, NCMP:32], 0.0))
            TTo(out=cs[:], in0=cs[:], in1=cst[:, 0, :].unsqueeze(2).to_broadcast([P, 32, NCMP]), op=ALU.subtract).then_inc(sem("cs"), 1)
            dve.wait_ge(sem("ce"), 1)
            link(dve.tensor_reduce(out=cst[:, 1, :], in_=cp[:, :, 0:NCMP], op=ALU.add, axis=AX.X))
            link(TS(cst[:, 1, :], cst[:, 1, :], 1e-30, None, ALU.max))
            link(dve.reciprocal(cst[:, 2, :], cst[:, 1, :]))
            link(TTo(out=cst[:, 3, :].rearrange("p (b h) -> p b h", b=TT), in0=cst[:, 2, :].rearrange("p (b h) -> p b h", b=TT),
                     in1=gates[:, :, 0:8], op=ALU.mult))
            TTo(out=cp[:, :, 0:NCMP], in0=cp[:, :, 0:NCMP], in1=cst[:, 3, :].unsqueeze(2).to_broadcast([P, 32, NCMP]),
                op=ALU.mult).then_inc(sem("cp"), 1)
            dve.wait_ge(sem("cp_t"), 1)
            CP(cpt[:, 4:8, :].rearrange("p b n -> p (b n)"), ps[:, 5, :]).then_inc(sem("cpt"), 1)
            dve.wait_ge(sem("oc_t"), 1)
            CP(onsa[:, 2, :], ps[:, 2, :])
            CP(onsa[:, 3, :], ps[:, 3, :]).then_inc(sem("oc_ev"), 1)
            dve.wait_ge(sem("oc_ev"), 2)
            dve.wait_ge(sem("bias_in"), 16)
            attention("nsa")
            dve.wait_ge(sem("ada2_t"), 4)
            link(TTo(out=modc[:, 16:48], in0=ps[:, 0, 0:32], in1=vcol[:, 16:48], op=ALU.add))
            STT(out=gain[:, 1, :], in0=modc[:, 32:40], scalar=1.0, in1=vcol[:, VROWS["g_mlp"][0]:VROWS["g_mlp"][0] + 8],
                op0=ALU.add, op1=ALU.mult).then_inc(sem("modc"), 1)
            dve.wait_ge(sem("cmask_in"), 16)
            attention("mla")
            for i in range(8):
                dve.wait_ge(sem("ot_hi"), i + 1)
                TTo(out=otlo[:, i, :], in0=ps[:, 4 + i % 2, :], in1=othi[:, i, :].bitcast(F32), op=ALU.subtract).then_inc(sem("ot_lo"), 1)
            for n in range(KD):
                u = U_Y + 3 * n
                for j in range(3):
                    nxt(u + j)
                for j in range(2):
                    g = G_Y + 4 * n + 2 + j
                    dve.wait_ge(sem("tile"), g + 1)
                    free(TTo(out=ym[:, j, :], in0=ps[:, bank(g), :], in1=sg[:, j, :], op=ALU.mult), g)
                    freed(dve, g)
                if n >= 1:
                    dve.wait_ge(sem("y_lo"), n)
                TTo(out=ym[:, 2, :], in0=ym[:, 0, :], in1=ym[:, 1, :], op=ALU.add).then_inc(sem("y"), 1)
                dve.wait_ge(sem("y_hi"), n + 1)
                TTo(out=ylo[:, n, :], in0=ym[:, 2, :], in1=yhi[:, n, :].bitcast(F32), op=ALU.subtract).then_inc(sem("y_lo"), 1)

            def lo_loop(u0, n, evac):
                with loop(dve, n // RING) as i:
                    for j in range(RING):
                        dve.wait_ge(sem("w_hi"), u0 + RING * i + j + AHEAD + 1)
                        s = slot(u0 + j + AHEAD)
                        TTo(out=wlo[:, s, :], in0=wraw[:, s, :], in1=whi[:, s, :].bitcast(F32), op=ALU.subtract).then_inc(sem("w_lo"), 1)
                        evac(i, j)

            def at1(t, idx):
                return t[:, bass.ds(idx, 1), :].rearrange("p a t -> p (a t)")

            def residual_lo(u0, g0, nm, scale):
                for k in range(KD):
                    split_lo(u0 + k + AHEAD)
                    g = g0 + k
                    dve.wait_ge(sem("tile"), g + 1)
                    if scale is None:
                        free(TTo(out=xT[:, k, :], in0=xT[:, k, :], in1=ps[:, bank(g), :], op=ALU.add), g)
                    else:
                        free(STT(out=xT[:, k, :], in0=ps[:, bank(g), :], scalar=mod(scale, k), in1=xT[:, k, :],
                                 op0=ALU.mult, op1=ALU.add), g)
                    if k >= 1:
                        norm_add(nm, k - 1)
                norm_add(nm, KD - 1)
                norm_inverse(nm)
                norm_apply(nm)
            residual_lo(U_OUT, G_OUT, "n2", 2)

            def square(i, j):
                freed(dve, G_FC1 + j, i)
                TTo(out=at1(ff, RING * i + j), in0=rb[:, j % 2, :], in1=rb[:, j % 2, :], op=ALU.mult).then_inc(sem("ff"), 1)
            lo_loop(U_FC1, NF1, square)

            def f_lo(nm, j, idx):
                dve.wait_ge(sem(nm + "_hi"), since(nm + "_hi", idx + 1))
                TTo(out=flo[:, j % 2, :], in0=ff[:, idx, :] if isinstance(idx, int) else at1(ff, idx),
                    in1=fhi[:, j % 2, :].bitcast(F32), op=ALU.subtract).then_inc(sem(nm + "_lo"), 1)

            def rows_lo(u0, n, nm):
                for j in range(2):
                    f_lo(nm, j, j)
                    split_lo(u0 + j + AHEAD)
                turns = (n - 4) // 4
                with loop(dve, turns) as i:
                    for j in range(4):
                        f_lo(nm, j, 4 * i + 2 + j)
                        dve.wait_ge(sem("w_hi"), u0 + 2 + RING * i + j + AHEAD + 1)
                        s = slot(u0 + 2 + j + AHEAD)
                        TTo(out=wlo[:, s, :], in0=wraw[:, s, :], in1=whi[:, s, :].bitcast(F32), op=ALU.subtract).then_inc(sem("w_lo"), 1)
                for j in range(2 + 4 * turns, n):
                    f_lo(nm, j, j)
                    if u0 + j + AHEAD < U_END and j < n - 1:
                        split_lo(u0 + j + AHEAD)
            rows_lo(U_FC2, NF1, "f1")
            def add3(k):
                dve.wait_ge(sem("n3_sq"), since("n3_sq", k + 1))
                if k == 0:
                    e = TS(hb[:, 0, :], sq3[:, 0, :], gsq[:, 0:1], None, ALU.mult)
                else:
                    dve.wait_ge(sem("n3_ac"), since("n3_ac", k))
                    e = STT(out=hb[:, 0, :], in0=sq3[:, k, :], scalar=gsq[:, k:k + 1], in1=hb[:, 0, :], op0=ALU.mult, op1=ALU.add)
                e.then_inc(sem("n3_ac"), 1)
            for n in range(KD):
                dve.wait_ge(sem("f1_bank"), n + 1)
                STT(out=xT[:, n, :], in0=ps[:, n, :], scalar=mod(5, n), in1=xT[:, n, :], op0=ALU.mult, op1=ALU.add).then_inc(sem("fc2_evac"), 1)
                if n >= 1:
                    add3(n - 1)
            add3(KD - 1)
            dve.wait_ge(sem("n3_st"), since("n3_st", 1))
            dve.wait_ge(sem("xf_st"), 1)
            CP(hb[:, 1, :], ps[:, 0, :]).then_inc(sem("xf_s"), 1)
            dve.wait_ge(sem("xf_s"), 1)
            STT(out=hb[:, 1, :], in0=hb[:, 1, :], scalar=EPS, in1=ps[:, 7, :], op0=ALU.mult, op1=ALU.add).then_inc(sem("n3_ms"), 1)
            norm_inverse("n3")
            norm_apply("n3")
            dve.wait_ge(sem("xf_rt"), 1)
            link(dve.reciprocal(ps[:, 6, :], sq3[:, 0, :]))
            split_lo(U_IN2 + AHEAD - 1)

            def cmul(ore, oim, xre, xim, yre, yim, t1, t2):
                link(TTo(out=t1, in0=xre, in1=yre, op=ALU.mult))
                link(TTo(out=t2, in0=xim, in1=yim, op=ALU.mult))
                link(TTo(out=ore, in0=t1, in1=t2, op=ALU.subtract))
                link(TTo(out=t1, in0=xre, in1=yim, op=ALU.mult))
                link(TTo(out=t2, in0=xim, in1=yre, op=ALU.mult))
                link(TTo(out=oim, in0=t1, in1=t2, op=ALU.add))

            def double(s, c1, t):
                link(STT(out=t, in0=c1, scalar=1.0, in1=s, op0=ALU.add, op1=ALU.mult))
                link(STT(out=c1, in0=s, scalar=-2.0, in1=s, op0=ALU.mult, op1=ALU.mult))
                link(TS(s, t, 2.0, None, ALU.mult))

            def turns_table():
                c1, s1, t = twc[:, 0, :], twc[:, 1, :], twc[:, 2, :]
                link(CP(c1, ssmc[:, 1, :]))
                link(CP(s1, ssmc[:, 2, :]))
                link(dve.memset(twr[:, :, 0:1], 1.0))
                link(dve.memset(twi[:, :, 0:1], 0.0))
                n = 1
                while n < SSM_C:
                    cc = twc[:, 3, :]
                    link(TS(cc, c1, 1.0, None, ALU.add))
                    t1, t2 = (x[:].rearrange("p q c -> p (q c)")[:, 0:16 * n].rearrange("p (q c) -> p q c", c=n) for x in (tA, tB))
                    cmul(twr[:, :, n:2 * n], twi[:, :, n:2 * n], twr[:, :, 0:n], twi[:, :, 0:n],
                         cc.unsqueeze(2).to_broadcast([P, SSM_Q, n]), s1.unsqueeze(2).to_broadcast([P, SSM_Q, n]), t1, t2)
                    n *= 2
                    if n < SSM_C:
                        double(s1, c1, t)

            def states():
                W = slice(1, SSM_C)
                Y_ = slice(0, SSM_C - 1)
                link(TTo(out=tA[:, :, W], in0=sA[:, :, Y_], in1=twr[:, :, W], op=ALU.mult))
                link(TTo(out=tB[:, :, W], in0=sB[:, :, Y_], in1=twi[:, :, W], op=ALU.mult))
                link(dve.memset(vA[:, :, 0:1], 0.0))
                link(TTo(out=vA[:, :, W], in0=tA[:, :, W], in1=tB[:, :, W], op=ALU.add))
                link(TTo(out=tA[:, :, W], in0=sB[:, :, Y_], in1=twr[:, :, W], op=ALU.mult))
                link(TTo(out=tB[:, :, W], in0=sA[:, :, Y_], in1=twi[:, :, W], op=ALU.mult))
                link(dve.memset(vB[:, :, 0:1], 0.0))
                link(TTo(out=vB[:, :, W], in0=tA[:, :, W], in1=tB[:, :, W], op=ALU.subtract))
                link(CP(sA[:], ssmc[:, 0, :].unsqueeze(2).to_broadcast([P, SSM_Q, SSM_C])))
                link(dve.memset(sA[:, :, 0:1], 0.0))
                fl = lambda x: x[:].rearrange("p q c -> p (q c)")
                link(dve.tensor_tensor_scan(fl(tA), fl(sA), fl(vA), 0.0, ALU.mult, ALU.add))
                link(dve.tensor_tensor_scan(fl(tB), fl(sA), fl(vB), 0.0, ALU.mult, ALU.add))
                link(TTo(out=vA[:], in0=twr[:], in1=tA[:], op=ALU.mult))
                link(TTo(out=vB[:], in0=twi[:], in1=tB[:], op=ALU.mult))
                link(TTo(out=sB[:], in0=vA[:], in1=vB[:], op=ALU.subtract))
                link(TTo(out=vA[:], in0=twr[:], in1=tB[:], op=ALU.mult))
                link(TTo(out=vB[:], in0=twi[:], in1=tA[:], op=ALU.mult))
                TTo(out=sA[:], in0=vA[:], in1=vB[:], op=ALU.add).then_inc(sem("xst"), 2)

            for i in range(12):
                u, g = U_IN2 + i, G_IN2 + i
                nxt(u)
                if i < KD:
                    STT(out=xT[:, i, :], in0=xT[:, i, :], scalar=col("g_final", i), in1=ps[:, 6, :], op0=ALU.mult, op1=ALU.mult
                        ).then_inc(sem("xf"), 1)
                if i == 8:
                    turns_table()
            for i in range(4):
                nxt(U_V2 + i)
            dve.wait_ge(sem("s_ev"), 4)
            states()
            dve.wait_ge(sem("bias2_ok"), 1)
            attention("chk")
            dve.wait_ge(sem("y_in"), 16 * 32)
            for m in range(4):
                STT(out=yssm[:, m].rearrange("p j c -> p (j c)"), in0=uT[:, m].rearrange("p j c -> p (j c)"), scalar=col("ssm_d_2", m),
                    in1=yssm[:, m].rearrange("p j c -> p (j c)"), op0=ALU.mult, op1=ALU.add).then_inc(sem("yk"), 1)
            for m in range(4):
                dve.wait_ge(sem("g_hi"), m + 1)
                TTo(out=glo[:, m, :], in0=ygel[:, m, :], in1=ghi[:, m, :].bitcast(F32), op=ALU.subtract).then_inc(sem("g_lo"), 1)
            for i in range(4):
                g = G_GLU + i
                if i % 2 == 0:
                    nxt(U_GLU + i // 2)
                freed(dve, g)
                TTo(out=ysg[:, i, :], in0=ysg[:, i, :], in1=ygel[:, i, :], op=ALU.mult).then_inc(sem("ysg"), 1)
            dve.wait_ge(sem("ya_sq"), 4)
            TS(stat[:, 3, :], stat[:, 2, :], 1.0 / 512, EPS, ALU.mult, ALU.add).then_inc(sem("ya_ms"), 1)
            dve.wait_ge(sem("ya_rt"), 1)
            link(dve.reciprocal(stat[:, 3, :], stat[:, 4, :]))
            for t in range(TT):
                TS(yatt[:, t, :], yatt[:, t, :], stat[:, 3, t:t + 1], None, ALU.mult).then_inc(sem("ya_n"), 1)
            for i in range(4):
                dve.wait_ge(sem("ya_t"), i + 1)
                if i >= 2:
                    dve.wait_ge(sem("ya_lo"), i - 1)
                TS(hb[:, i % 2, :], ps[:, 4 + i % 2, :], col("norm_att_out_g_2", i), None, ALU.mult).then_inc(sem("ya_hb"), 1)
                dve.wait_ge(sem("ya_hi"), i + 1)
                TTo(out=hlo[:, 4 + i, :], in0=hb[:, i % 2, :], in1=hhi[:, 4 + i, :].bitcast(F32), op=ALU.subtract).then_inc(sem("ya_lo"), 1)
            dve.wait_ge(sem("ya_lo"), 4)
            norm_adds("nssm")
            norm_inverse("nssm")
            norm_apply("nssm")
            residual_lo(U_OUT2, G_OUT2, "n4", None)
            dve.sem_inc(sem("fc2b_free"), 1)

            def gate_up(i, j):
                if j % 2 == 1:
                    g = G_GU + j
                    dve.wait_ge(sem("tile"), G_GU + RING * i + j + 1)
                    freed(dve, g - 1, i)
                    free(TTo(out=at1(ff, 2 * i + j // 2), in0=rb[:, j // 2, :], in1=ps[:, bank(g), :], op=ALU.mult), g)
            lo_loop(U_GU, 2 * NF2, gate_up)
            rows_lo(U_DN, NF2, "f2")
            dve.wait_ge(sem("xn_ev"), 8)
            dve.wait_ge(sem("gfin_in"), 16)
            for t in range(TT):
                for half in range(2):
                    c = slice(512 * half, 512 * half + 512)
                    dve.wait_ge(sem("f2_bank"), 2 * t + half + 1)
                    TTo(out=xn[:, t, c], in0=xn[:, t, c], in1=ps[:, 2 * t + half, :], op=ALU.add).then_inc(sem("xo"), 1)
                dve.wait_ge(sem("fin_sq"), t + 1)
                TS(stat[:, 7, t:t + 1], stat[:, 5, t:t + 1], 1.0 / D, EPS, ALU.mult, ALU.add).then_inc(sem("fin_ms"), 1)
                dve.wait_ge(sem("fin_rt"), t + 1)
                link(dve.reciprocal(stat[:, 4, t:t + 1], stat[:, 6, t:t + 1]))
                STT(out=xn[:, t, :], in0=xn[:, t, :], scalar=stat[:, 4, t:t + 1], in1=gfin[:, :], op0=ALU.mult, op1=ALU.mult).then_inc(sem("o_ready"), 1)


_INS = ["x", "c", "w_ada", "b_ada", "g_mix", "w_in", "pe_ck", "w_ck1", "w_ck2", "pe_cv", "w_cv1", "w_cv2", "g_cq", "w_uq",
        "g_ckv", "w_uk", "w_uv", "w_o_nsa", "w_o_mla", "w_out", "g_mlp", "w_fc1", "w_fc2", "g_final", "norm_mix_g_2",
        "w_in_2", "ssm_lam_re_2", "ssm_lam_im_2", "ssm_log_dt_2", "ssm_b_re_2", "ssm_b_im_2", "ssm_c_re_2",
        "ssm_c_im_2", "ssm_d_2", "ssm_w_glu_2", "ssm_b_glu_2", "attn_rel_bias_2", "norm_ssm_out_g_2",
        "norm_att_out_g_2", "w_out_2", "norm_ffn_g_2", "w_gate_2", "w_up_2", "w_down_2", "norm_final_g_2"]


def constants():
    f = np.float32
    p = np.arange(P)[:, None]
    j = np.arange(T)[None, :]
    dist = p - (j - (T - P))
    seen = dist >= 0
    alibi = np.stack([np.where(seen, -(8.0 * 2.0 ** -(h + 1)) * dist, NEG) for h in range(4)], axis=1)
    causal = np.where(seen, 0.0, NEG)
    block, head, n = np.meshgrid(np.arange(TT), np.arange(HEADS), np.arange(NCMP), indexing="ij")
    d = (P * block + 0)[None] + p[:, :, None, None] - (16 * n + 31)[None]
    cmp_bias = np.where(d >= 0, -(8.0 * 2.0 ** -(head + 1.0))[None] * d, NEG).reshape(P, 32, NCMP)
    ang = np.arange(T, dtype=f)[None, :] * (f(10000.0) ** (-np.arange(16, dtype=f) / f(16)))[:, None]
    cos, sin = np.cos(ang.astype(np.float64)), np.sin(ang.astype(np.float64))
    rope = np.zeros((P, T))
    rope[64:96] = np.concatenate([cos, cos])
    rope[96:128] = np.concatenate([-sin, sin])
    return {"identity": np.eye(P).astype(f), "alibi": alibi.astype(f), "causal": causal.astype(f),
            "cmp_bias": cmp_bias.astype(f), "rope_table": rope.astype(f)}


def kernel(**inputs):
    import concourse.bacc as _bacc
    from concourse.bass_utils import run_bass_kernel_spmd as _run

    nc = _bacc.Bacc("TRN2", target_bir_lowering=False, num_devices=1)
    arrays, aps = {}, {}
    given = {name: np.ascontiguousarray(inputs[name]) for name in _INS}
    given.update(constants())
    for name, v in given.items():
        arrays[f"in_{name}"] = v
        aps[name] = nc.dram_tensor(f"in_{name}", v.shape, mybir.dt.from_np(v.dtype), kind="ExternalInput").ap()
    scr = {"rel": [8, 640], "relp": [P, 8, 640], "w1": [2, P, SSM_Q, P], "w2": [2, P, SSM_Q, P], "kk": [32, SSM_Q, P],
           "u": [4, P, SSM_L, SSM_C], "y": [P, 32 * SSM_C]}
    scr = {k: nc.dram_tensor(f"scratch_{k}", v, F32, kind="Internal").ap() for k, v in scr.items()}
    out = nc.dram_tensor("out_0", [1, T, D], F32, kind="ExternalOutput").ap()
    program(nc, aps, out, scr)
    r = _run(nc, [arrays], core_ids=[0])
    return r.results[0]["out_0"]
```

```python
import concourse.bass as bass
from concourse import mybir
from contextlib import ExitStack
import numpy as np

F32 = mybir.dt.float32
F32R = mybir.dt.float32r
I32 = mybir.dt.int32
ACT = mybir.ActivationFunctionType
ALU = mybir.AluOpType
AX = mybir.AxisListType

P = 128
T = 512
D = 1024
KD = D // P
TT = T // P
EPS = 1e-6
NEG = -1e30
FF1, FF2 = 4096, 2816
NF1, NF2 = FF1 // P, FF2 // P
HEADS, DH = 8, 64
MLA_SCALE = 96.0 ** -0.5
NCMP = 31
SSM_L = 8
SSM_C = T // SSM_L
SSM_Q = 16
RING = 4
FC1_PARTS = [12, 4, 4, 4, 8]
AHEAD = 3

C_Q, C_KC, C_VC, C_KS, C_VS, C_KW, C_VW, C_G, C_QD, C_KVD, C_KR, C_GA, C_GB = np.cumsum(
    [0, 512, 128, 128, 128, 128, 128, 128, 24, 384, 256, 32, 1024]).tolist()

U_A1 = 0
A1_COLS = [C_KC, C_VC, C_KS, C_KW, C_VS, C_VW] + [C_Q + P * i for i in range(4)] \
    + [C_QD + P * i for i in range(3)] + [C_KVD + P * i for i in range(2)]
U_TAIL = U_A1 + len(A1_COLS)
U_UQ = U_TAIL + 1
U_UK = U_UQ + 4
U_UV = U_UK + 1
U_Y = U_UV + 1
U_OUT = U_Y + 3 * KD
U_FC1 = U_OUT + KD
U_FC2 = U_FC1 + NF1
U_IN2 = U_FC2 + NF1
U_V2 = U_IN2 + 12
U_GLU = U_V2 + 4
U_OUT2 = U_GLU + 2
U_GU = U_OUT2 + KD
U_DN = U_GU + 2 * NF2
U_END = U_DN + NF2

G_A1 = 0
G_UQ = G_A1 + 16
G_UK = G_UQ + 8
G_UV = G_UK + 4
G_Y = G_UV + 4
G_OUT = G_Y + 4 * KD
G_FC1 = G_OUT + KD
G_IN2 = G_FC1 + NF1
G_GLU = G_IN2 + 12
G_OUT2 = G_GLU + 4
G_GU = G_OUT2 + KD
G_END = G_GU + 2 * NF2

VROWS = {}
_n = 0
for _name, _rows in (("b_ada", 48), ("g_mix", 8), ("c", 8), ("g_mlp", 8), ("g_cq", 3), ("g_ckv", 2),
                     ("norm_mix_g_2", 8), ("norm_ffn_g_2", 8), ("ssm_b_glu_2", 4), ("ssm_d_2", 4),
                     ("norm_ssm_out_g_2", 4), ("norm_att_out_g_2", 4), ("g_final", 8)):
    VROWS[_name] = (_n, _rows)
    _n += _rows
NV = _n


def program(nc, a, out, scr, dbg=None):
    with ExitStack() as ctx:
        S = {}

        ATTS = {"nsa": 16, "mla": 8, "chk": 8}
        NORMS = {"n1": 8, "ncq": 3, "nckv": 2, "n2": 8, "n3": 8, "nssm": 4, "n4": 8}

        def since(name, value):
            who, _, what = name.partition("_")
            for group in (NORMS, ATTS):
                if who in group:
                    who_before = list(group)[:list(group).index(who)]
                    before = [group[k] for k in who_before]
                    split = sum(before) if group is NORMS else 0
                    if group is NORMS and what in ("h", "hi", "lo"):
                        return split + value
                    per = (lambda n: n if what in ("sq", "ac") else 1) if group is NORMS else \
                        (lambda n: {"o": n, "pta": 2 * n, "ptd": 2 * n}.get(what, 4 * n))
                    own = {"pta": 2 * ATTS["nsa"], "ptd": -2 * ATTS["nsa"]}.get(what, 0) if group is ATTS and who_before else 0
                    return sum(map(per, before)) + own + value
            return value

        def sem(name):
            who, _, what = name.partition("_")
            name = "norm_" + what if who in NORMS else "att_" + what if who in ATTS else name
            if name not in S:
                S[name] = ctx.enter_context(nc.semaphore(name))
            return S[name]

        base = [(nc.sbuf_base + 31) // 32 * 32]
        limit = nc.sbuf_usable_end

        def at(name, offset, shape, dt=F32):
            n = int(np.prod(shape[1:])) * 4
            assert offset + n <= limit, (name, offset + n - limit)
            return nc.alloc_sbuf_tensor_at(name, shape, dt, offset=offset)

        def keep(name, shape, dt=F32):
            t = at(name, base[0], shape, dt)
            base[0] += (int(np.prod(shape[1:])) * 4 + 31) // 32 * 32
            return t

        ident = keep("ident", [P, P])
        ones = keep("ones", [P, P])
        vcol = keep("vcol", [P, NV + 32])
        modc = keep("modc", [P, 48])
        gain = keep("gain", [P, 2, KD])
        stat = keep("stat", [P, 8, 4])
        eps = keep("eps", [P, 8])
        gsq = keep("gsq", [P, KD])
        gmix2 = keep("gmix2", [P, KD])
        rsum = keep("rsum", [P, 2, 4])
        rinv = keep("rinv", [P, 4])
        smax = keep("smax", [P, 4])
        ssmc = keep("ssmc", [P, 3, SSM_Q])
        hb = keep("hb", [P, 2, T])
        xT = keep("xT", [P, KD, T])
        wraw = keep("wraw", [P, RING, D])
        whi = keep("whi", [P, RING, D], F32R)
        wlo = keep("wlo", [P, RING, D], F32R)
        H0 = base[0]
        hhi = keep("hhi", [P, KD, T], F32R)
        hlo = keep("hlo", [P, KD, T], F32R)
        X0 = base[0]
        K = 1024

        def x_at(name, kb, shape, dt=F32):
            return at(name, X0 + int(kb * K), shape, dt)

        diag = hb[:, 1, :]
        xs = at("xs", H0, [P, TT, D])
        qT = x_at("qT", 0, [P, 4, T])
        kdup = x_at("kdup", 8, [P, 2, 2, T])
        vnat = x_at("vnat", 16, [P, TT, 2, P])
        vblk = x_at("vblk", 20, [P, 2, 4, DH])
        kcT = x_at("kcT", 22, [P, 2, NCMP])
        gates = x_at("gates", 22.5, [P, TT, 24])
        qm = x_at("qm", 23, [P, HEADS, T])
        km = x_at("km", 39, [P, HEADS, T])
        vm = x_at("vm", 55, [P, TT, HEADS * DH])
        bias = x_at("bias", 63, [P, 4, T])
        cmask = x_at("cmask", 71, [P, T])
        onsa = x_at("onsa", 73, [P, TT, T])
        omla = x_at("omla", 81, [P, TT, T])
        ppb = x_at("ppb", 89, [P, 4, T])
        ptb = x_at("ptb", 97, [P, 4, T])
        sq = x_at("sq", 71, [P, 3, T])
        x2 = x_at("x2", 73, [P, 2, 2, T])
        flat = x_at("flat", 81, [P, 2, 16, 62])
        cmpw = [x_at(f"cmpw{i}", kb, [P, D]) for i, kb in enumerate((89, 93, 97, 101, 0, 4, 39, 43))]
        aring = x_at("aring", 0, [P, 4, 2 * D])
        ada1 = x_at("ada1", 81, [P, D])
        aring2 = x_at("aring2", 85, [P, 2, T])
        ada2 = x_at("ada2", 81, [P, 2, T])
        cqhi = x_at("cqhi", 89, [P, 3, T], F32R)
        cqlo = x_at("cqlo", 95, [P, 3, T], F32R)
        krot = x_at("krot", 101, [P, T])
        rope = x_at("rope", 103, [P, T])
        ckhi = x_at("ckhi", 63, [P, 2, T], F32R)
        cklo = x_at("cklo", 67, [P, 2, T], F32R)
        zl = x_at("zl", 39, [P, 5, T])
        zv = x_at("zv", 47, [P, 2, T])
        zg = x_at("zg", 49, [P, T])
        vrow = x_at("vrow", 55.5, [P, 2, P])
        hid = x_at("hid", 51, [P, 2, 2, 2, 32])
        hidr = x_at("hidr", 52, [P, 2, 2, 4, 32])
        w2d = x_at("w2d", 54, [P, 2, 2, DH])
        w2v = x_at("w2v", 55, [P, 2, DH])
        cbias = x_at("cbias", 89, [P, 32, NCMP])
        cs = x_at("cs", 93, [P, 32, NCMP])
        cp = x_at("cp", 97, [P, 32, 32])
        cpt = x_at("cpt", 101, [P, 8, P])
        cst = x_at("cst", 105, [P, 4, 32])
        othi = x_at("othi", 0, [P, 8, T], F32R)
        otlo = x_at("otlo", 16, [P, 8, T], F32R)
        yhi = x_at("yhi", 32, [P, KD, T], F32R)
        ylo = x_at("ylo", 48, [P, KD, T], F32R)
        sg = x_at("sg", 64, [P, 2, T])
        ym = x_at("ym", 89, [P, 3, T])
        ff = x_at("ff", 0, [P, NF1, T])
        fhi = x_at("fhi", 65, [P, 2, T], F32R)
        flo = x_at("flo", 69, [P, 2, T], F32R)
        rb = x_at("rb", 89, [P, 2, T])
        sq3 = x_at("sq3", 89, [P, KD, T])
        xn = x_at("xn", 47, [P, TT, D])
        gfin = x_at("gfin", 93, [P, D])
        uT = x_at("uT", 0, [P, 4, SSM_L, SSM_C])
        ug = x_at("ug", 8, [P, 32, SSM_C])
        q2 = x_at("q2", 16, [P, 4, T])
        k2 = x_at("k2", 24, [P, 4, T])
        v2 = x_at("v2", 32, [P, TT, T])
        w1s = x_at("w1s", 40, [P, 2, SSM_Q, P])
        w2s = x_at("w2s", 40, [P, 2, SSM_Q, P])
        tmat = x_at("tmat", 56, [P, 32, P])
        sA = x_at("sA", 72, [P, SSM_Q, SSM_C])
        sB = x_at("sB", 76, [P, SSM_Q, SSM_C])
        twr = x_at("twr", 80, [P, SSM_Q, SSM_C])
        twi = x_at("twi", 84, [P, SSM_Q, SSM_C])
        vA = x_at("vA", 88, [P, SSM_Q, SSM_C])
        vB = x_at("vB", 92, [P, SSM_Q, SSM_C])
        tA = x_at("tA", 96, [P, SSM_Q, SSM_C])
        tB = x_at("tB", 100, [P, SSM_Q, SSM_C])
        yg = x_at("yg", 96, [P, 32, SSM_C])
        yatt = x_at("yatt", 88, [P, TT, T])
        yssm = x_at("yssm", 40, [P, 4, SSM_L, SSM_C])
        ygel = x_at("ygel", 8, [P, 4, T])
        ghi = x_at("ghi", 48, [P, 4, T], F32R)
        glo = x_at("glo", 56, [P, 4, T], F32R)
        ysg = x_at("ysg", 64, [P, 4, T])
        sq2 = x_at("sq2", 73, [P, 3, T])
        ppb2 = at("ppb2", H0, [P, 4, T])
        ptb2 = at("ptb2", H0 + 8 * K, [P, 4, T])
        bias2 = at("bias2", H0 + 16 * K, [P, HEADS, T])
        twc = x_at("twc", 104.5, [P, 4, SSM_Q])
        pv = x_at("pv", 77, [16, 23, P])
        pvi = x_at("pvi", 88.5, [16, P], I32)
        dtl = x_at("dtl", 68, [16, 8, 2])
        dti = x_at("dti", 68.25, [16, 2], I32)
        craw = x_at("craw", 95, [P, 2, 4, 2, 64])
        braw = x_at("braw", 99, [P, 2, SSM_Q, 16])
        apar = x_at("apar", 101.5, [P, 7, SSM_Q])
        pw = x_at("pw", 102, [P, 2, SSM_Q, 9])
        pwr = x_at("pwr", 103.25, [P, 2, SSM_Q, 8])
        bbar = x_at("bbar", 95, [P, 2, SSM_Q, 16])
        cpw = x_at("cpw", 97, [P, 2, 4, 9, 16])
        tmp = x_at("tmp", 77, [P, 2, 4 * 9 * 16])
        w1t = x_at("w1t", 81.5, [P, 2, 4, P])
        ctp = x_at("ctp", 85.5, [P, 2, SSM_Q, 16])
        bpair = x_at("bpair", 65, [P, 2, SSM_Q, 2, 16])
        stg = x_at("stg", 69, [P, 2, 4, P])
        kst = x_at("kst", 93, [32, 4, P])
        rel = x_at("rel", 60.5, [8, 640])

        ps = ctx.enter_context(nc.psum_tensor("ps", [P, 8, T], F32))

        def col(name, i=0):
            return vcol[:, VROWS[name][0] + i:VROWS[name][0] + i + 1]

        def mod(part, i):
            return modc[:, part * KD + i:part * KD + i + 1]

        def slot(u):
            return u % RING

        def freed(eng, g, turn=0):
            eng.wait_ge(sem(f"t_free{g % 2}"), g // 2 + 1 + turn * (RING // 2))

        def free(ins, g):
            return ins.then_inc(sem(f"t_free{g % 2}"), 1)

        def used(u):
            for first, fn in ((U_DN, lambda i: ("f2_used", i + 1)), (U_GU, lambda i: ("tile", G_GU + i + 1)),
                              (U_OUT2, lambda i: ("tile", G_OUT2 + i + 1)), (U_GLU, lambda i: ("tile", G_GLU + 2 * i + 2)),
                              (U_V2, lambda i: ("v2_t", i + 1)), (U_IN2, lambda i: ("tile", G_IN2 + i + 1)),
                              (U_FC2, lambda i: ("f1_used", i + 1) if i < NF1 - 2 else ("f1_bank", 8)), (U_FC1, lambda i: ("tile", G_FC1 + i + 1)),
                              (U_OUT, lambda i: ("tile", G_OUT + i + 1)),
                              (U_Y, lambda i: ("tile", G_Y + 4 * (i // 3) + (i % 3 + 1 if i % 3 < 2 else 4))),
                              (U_UV, lambda i: ("tile", G_UV + 4)), (U_UK, lambda i: ("tile", G_UK + 4)),
                              (U_UQ, lambda i: ("tile", G_UQ + 2 * i + 2)), (0, lambda i: ("tile", i + 1))):
                if u >= first:
                    return fn(u - first)

        def bank(g):
            return g % 2

        win = a["w_in"][0].rearrange("(k p) n -> p k n", p=P)

        def loop(eng, n):
            return eng.Fori(0, n)

        def nsa_heads():
            res = []
            for g in range(2):
                for br in range(2):
                    for h in range(4 * g, 4 * g + 4):
                        r = slice(64 * (h % 2), 64 * (h % 2) + 64)
                        res.append(dict(q=qT[r, h // 2, :], k=kdup[r, br, g, :],
                                        v=lambda b, br=br, g=g: vnat[:, b, br, 64 * g:64 * g + 64],
                                        bias=bias[:, h % 4, :], scale=DH ** -0.5, o=onsa, h=h,
                                        gate=gates[:, :, 8 * (br + 1) + h], rescale=(g == 1 and br == 0 and h == 4)))
            return res

        def mla_heads():
            return [dict(q=qm[0:96, h, :], k=km[0:96, h, :], v=lambda b, h=h: vm[:, b, 64 * h:64 * h + 64],
                         bias=cmask[:, :], scale=MLA_SCALE, o=omla, h=h, gate=None, rescale=False)
                    for h in range(HEADS)]

        def chunk_heads():
            return [dict(q=q2[64 * (h % 2):64 * (h % 2) + 64, h // 2, :], k=k2[64 * (h % 2):64 * (h % 2) + 64, h // 2, :],
                         v=lambda b, h=h: v2[:, b, 64 * h:64 * h + 64],
                         bias=bias2[:, h, :], scale=DH ** -0.5, o=yatt, h=h, gate=None, rescale=False)
                    for h in range(HEADS)]

        ATT = {"nsa": (nsa_heads(), ppb, ptb), "mla": (mla_heads(), ppb, ptb), "chk": (chunk_heads(), ppb2, ptb2)}

        def score_bank(s):
            return 1 + s % 3

        def turned(nm, r):
            if nm == "nsa":
                return nm + "_pta", since(nm + "_pta", r + 1)
            what = nm + ("_pta" if r % 2 else "_ptd")
            return what, since(what, r // 2 + 1)

        NORM = {"n1": (lambda k: xT[:, k, :], 8, sq), "ncq": (lambda k: zl[:, k, :], 3, sq),
                "nckv": (lambda k: zl[:, 3 + k, :], 2, sq), "n2": (lambda k: xT[:, k, :], 8, sq),
                "n3": (lambda k: xT[:, k, :], 8, sq3), "nssm": (lambda k: ysg[:, k, :], 4, sq2),
                "n4": (lambda k: xT[:, k, :], 8, sq)}
        AFTER = {"n1": (lambda k: gain[:, 0, k:k + 1], lambda k: mod(0, k), hhi, hlo),
                 "ncq": (lambda k: col("g_cq", k), None, cqhi, cqlo),
                 "nckv": (lambda k: col("g_ckv", k), None, ckhi, cklo),
                 "n2": (lambda k: gain[:, 1, k:k + 1], lambda k: mod(3, k), hhi, hlo),
                 "n3": (lambda k: gmix2[:, k:k + 1], None, hhi, hlo),
                 "nssm": (lambda k: col("norm_ssm_out_g_2", k), None, hhi, hlo),
                 "n4": (lambda k: col("norm_ffn_g_2", k), None, hhi, hlo)}

        block = ctx.enter_context(nc.Block())

        @block.sync
        def _(sp):
            def slot_free(u):
                if u >= RING:
                    sp.wait_ge(sem("w_lo"), u - RING + 1)

            def load(u, dst, src):
                sp.dma_start(dst, src).then_inc(sem(f"w_in{slot(u)}"), 16)

            def raw(u, lo=0, hi=D):
                return wraw[:, slot(u), lo:hi]

            sp.dma_start(xs[:], a["x"][0].rearrange("(t p) d -> p t d", p=P)).then_inc(sem("x_in"), 16)
            def load_a1(i):
                u = U_A1 + i
                slot_free(u)
                load(u, raw(u).rearrange("p (k n) -> p k n", k=KD), win[:, :, A1_COLS[i]:A1_COLS[i] + P])

            for k in range(KD):
                if k == 2:
                    sp.wait_ge(sem("vec_t"), 1)
                if k >= 4:
                    sp.wait_ge(sem("ada_used"), k - 3)
                    sp.wait_ge(sem("ada_pe"), k - 3)
                sp.dma_start(aring[:, k % 4, :], a["w_ada"][0][P * k:P * k + P, 0:2 * D]).then_inc(sem(f"ada_in{k % 4}"), 16)
                if k in (3, 5, 7):
                    load_a1((k - 3) // 2)
            for i in range(3, len(A1_COLS)):
                load_a1(i)
                if i in (3, 5):
                    w = (i - 3) // 2
                    sp.wait_ge(sem("ada_used"), 8)
                    sp.wait_ge(sem("ada_pe"), 8)
                    for m in range(4):
                        sp.dma_start(cmpw[4 * w + m].rearrange("p (k n) -> p k n", k=4),
                                     a[("w_ck1", "w_cv1")[w]][0].rearrange("(k p) n -> p k n", p=P)[:, 4 * m:4 * m + 4, :]
                                     ).then_inc(sem(f"ada_in{2 + w}"), 16)
            u = U_TAIL
            slot_free(u)
            tail = raw(u).rearrange("p (k n) -> p k n", k=KD)
            for lo, c, n in ((0, C_G, 24), (64, C_KR, 32), (96, C_KR + 16, 16), (112, C_KR, 16)):
                load(u, tail[:, :, lo:lo + n], win[:, :, c:c + n])
            wuq = a["w_uq"][0].rearrange("(k p) (h n) -> p k h n", p=P, n=96)
            for i in range(4):
                u = U_UQ + i
                slot_free(u)
                v = raw(u, 0, 768).rearrange("p (k h n) -> p k h n", k=3, h=2)
                for h in range(2):
                    load(u, v[:, :, h, 0:96], wuq[:, :, 2 * i + h, :])
                    load(u, v[:, :, h, 96:112], wuq[:, :, 2 * i + h, 80:96])
                    load(u, v[:, :, h, 112:128], wuq[:, :, 2 * i + h, 64:80])
            for u, name in ((U_UK, "w_uk"), (U_UV, "w_uv")):
                slot_free(u)
                load(u, raw(u).rearrange("p (k n) -> p k n", k=2), a[name][0].rearrange("(k p) n -> p k n", p=P))
            for n in range(KD):
                for j, c in enumerate((C_GA, C_GB)):
                    u = U_Y + 3 * n + j
                    slot_free(u)
                    load(u, raw(u).rearrange("p (k n) -> p k n", k=KD), win[:, :, c + n * P:c + n * P + P])
                u = U_Y + 3 * n + 2
                slot_free(u)
                for j, name in enumerate(("w_o_nsa", "w_o_mla")):
                    load(u, raw(u, 512 * j, 512 * j + 512).rearrange("p (k n) -> p k n", k=4),
                         a[name][0].rearrange("(k p) n -> p k n", p=P)[:, :, n * P:n * P + P])
                if n == 0:
                    for m in range(64):
                        part, k, half = 2 + m // 16, m // 2 % 8, m % 2
                        if m >= 2:
                            sp.wait_ge(sem("ada2_used"), m - 1)
                        c = D * part + T * half
                        sp.dma_start(aring2[:, m % 2, :], a["w_ada"][0][P * k:P * k + P, c:c + T]
                                     ).then_inc(sem(f"ada_in{m % 2}"), 16)

            def columns(u0, n, src):
                with loop(sp, n // RING) as i:
                    for j in range(RING):
                        sp.wait_ge(sem("w_lo"), u0 + RING * i + j - RING + 1)
                        load(u0 + j, raw(u0 + j).rearrange("p (k n) -> p k n", k=KD),
                             src[:, :, bass.ds(P * RING * i + P * j, P)])
                return u0 + n // RING * RING

            def rows(u0, n, src):
                with loop(sp, n // RING) as i:
                    for j in range(RING):
                        sp.wait_ge(sem("w_lo"), u0 + RING * i + j - RING + 1)
                        load(u0 + j, raw(u0 + j), src[bass.ds(P * RING * i + P * j, P), :])
                for j in range(n // RING * RING, n):
                    slot_free(u0 + j)
                    load(u0 + j, raw(u0 + j), src[P * j:P * j + P, :])

            columns(U_OUT, KD, a["w_out"][0].rearrange("(k p) n -> p k n", p=P))
            columns(U_FC1, NF1, a["w_fc1"][0].rearrange("(k p) n -> p k n", p=P))
            rows(U_FC2, NF1, a["w_fc2"][0])
            win2 = a["w_in_2"][0].rearrange("(k p) n -> p k n", p=P)
            columns(U_IN2, 12, win2)
            for i in range(4):
                u = U_V2 + i
                slot_free(u)
                load(u, raw(u).rearrange("p (k n) -> p k n", k=2), win2[:, 2 * i:2 * i + 2, 1536:2048])
            for i in range(2):
                u = U_GLU + i
                slot_free(u)
                load(u, raw(u).rearrange("p (k n) -> p k n", k=4),
                     a["ssm_w_glu_2"][0].rearrange("(k p) n -> p k n", p=P)[:, :, 256 * i:256 * i + 256])
            columns(U_OUT2, KD, a["w_out_2"][0].rearrange("(k p) n -> p k n", p=P))
            wg = a["w_gate_2"][0].rearrange("(k p) n -> p k n", p=P)
            wu = a["w_up_2"][0].rearrange("(k p) n -> p k n", p=P)
            with loop(sp, NF2 // 2) as i:
                for j in range(4):
                    u = U_GU + j
                    sp.wait_ge(sem("w_lo"), U_GU + 4 * i + j - RING + 1)
                    load(u, raw(u).rearrange("p (k n) -> p k n", k=KD),
                         (wg, wu)[j % 2][:, :, bass.ds(2 * P * i + (j // 2) * P, P)])
            rows(U_DN, NF2, a["w_down_2"][0])
            for t in range(TT):
                sp.wait_ge(sem("o_ready"), t + 1)
                sp.dma_start(out[0, P * t:P * t + P, :], xn[:, t, :]).then_inc(sem("stored"), 16)
            sp.wait_ge(sem("stored"), 16 * TT)

        def w_count(u):
            n = 0
            for v in range(slot(u), u + 1, RING):
                n += 4 if v == U_TAIL else 6 if U_UQ <= v < U_UK else \
                    2 if U_Y <= v < U_OUT and (v - U_Y) % 3 == 2 else 1
            return n

        @block.gpsimd
        def _(pool):
            chain = [0]

            def link(i):
                chain[0] += 1
                i.then_inc(sem("pool_chain"), 1)
                pool.wait_ge(sem("pool_chain"), chain[0])

            for i, (name, (r, n)) in enumerate(VROWS.items()):
                if i >= 6:
                    pool.dma_start(vrow[r:r + n, 0, :], bass.AP(a[name].tensor, 0, [[P, n], [1, P]])).then_inc(sem("vec2_in"), 16)
            for i, name in enumerate(("pe_ck", "pe_cv")):
                pool.dma_start(vrow[16 * i:16 * i + 16, 1, :], bass.AP(a[name].tensor, 0, [[P, 16], [1, P]])).then_inc(sem("vec2_in"), 16)
            for r in range(2):
                pool.dma_start(w2d[:, :, r, :], a["w_ck2"][0].rearrange("(k p) n -> p k n", p=P)).then_inc(sem("w2_in"), 16)
            pool.dma_start(w2v[:], a["w_cv2"][0].rearrange("(k p) n -> p k n", p=P)).then_inc(sem("w2_in"), 16)
            pool.dma_start(rel[0:8, 383:640], a["attn_rel_bias_2"][0]).then_inc(sem("rel_in"), 16)
            pool.wait_ge(sem("rel_ok"), 1)
            pool.dma_start(scr["rel"], rel[0:8, :]).then_inc(sem("rel_out"), 16)

            TTo, TS, CP = pool.tensor_tensor, pool.tensor_scalar, pool.tensor_copy

            def STT(out, in0, scalar, in1, op0, op1):
                part = pv[0:16, 22, :] if out.shape[-1] == P else dtl[0:16, 6, :]
                link(TS(part, in0, scalar, None, op0))
                return TTo(out=out, in0=part, in1=in1, op=op1)

            pool.wait_ge(sem("p_used"), 8)
            pool.dma_start(rope[:], a["rope_table"]).then_inc(sem("rope_in"), 16)
            pool.wait_ge(sem("krot"), 3)
            for h in range(HEADS):
                if h == 0:
                    pool.wait_ge(sem("nckv_lo"), since("nckv_lo", 2))
                pool.tensor_copy(km[64:96, h, :], krot[64:96, :]).then_inc(sem("km_rope"), 1)
            pool.wait_ge(sem("ukv_done"), 1)
            pool.wait_ge(sem("km_rope"), HEADS)
            pool.dma_start(cbias[:], a["cmp_bias"]).then_inc(sem("cbias_in"), 16)
            pool.dma_start(bias[:], a["alibi"]).then_inc(sem("bias_in"), 16)
            pool.dma_start(cmask[:], a["causal"]).then_inc(sem("cmask_in"), 16)

            pool.wait_ge(sem("rel_out"), 16)
            pool.dma_start(scr["relp"], bass.AP(scr["rel"].tensor, 0, [[0, P], [640, HEADS], [1, 640]])).then_inc(sem("relp_out"), 16)
            pool.wait_ge(sem("relp_out"), 16)
            def v(i):
                return pv[0:16, i, :]

            def exp_(dst, x, t, ti):
                xc, n, f, q = t
                link(TS(xc, x, -87.3, 88.7, ALU.max, ALU.min))
                link(TS(n, xc, 1.4426950408889634, 12582912.0, ALU.mult, ALU.add))
                link(TS(n, n, -12582912.0, None, ALU.add))
                link(STT(out=f, in0=n, scalar=-0.693145751953125, in1=xc, op0=ALU.mult, op1=ALU.add))
                link(STT(out=f, in0=n, scalar=-1.42860682030941723212e-6, in1=f, op0=ALU.mult, op1=ALU.add))
                link(TS(q, f, 1.0 / 5040, None, ALU.mult))
                for c in (1.0 / 720, 1.0 / 120, 1.0 / 24, 1.0 / 6, 0.5, 1.0):
                    link(STT(out=q, in0=q, scalar=c, in1=f, op0=ALU.add, op1=ALU.mult))
                link(TS(ti, n, 127.0, 8388608.0, ALU.add, ALU.mult))
                link(STT(out=dst, in0=q, scalar=1.0, in1=ti.bitcast(F32), op0=ALU.add, op1=ALU.mult))

            def double(s, c1, t):
                link(STT(out=t, in0=c1, scalar=1.0, in1=s, op0=ALU.add, op1=ALU.mult))
                link(STT(out=c1, in0=s, scalar=-2.0, in1=s, op0=ALU.mult, op1=ALU.mult))
                link(TS(s, t, 2.0, None, ALU.mult))

            pool.wait_ge(sem("ot_hi"), 8)
            pool.wait_ge(sem("ot_lo"), 8)
            for i, name in enumerate(("ssm_lam_re_2", "ssm_lam_im_2")):
                pool.dma_start(pv[0:16, 20 + i, :], bass.AP(a[name].tensor, 0, [[P, 16], [1, P]])).then_inc(sem("par_in"), 16)
            pool.dma_start(dtl[0:16, 0, :], bass.AP(a["ssm_log_dt_2"].tensor, 0, [[2, 16], [1, 2]])).then_inc(sem("par_in"), 16)
            for i, name in enumerate(("ssm_b_re_2", "ssm_b_im_2")):
                pool.dma_start(braw[:, i, :, :], a[name][0].rearrange("(q g) p h -> (g p) q h", g=2)).then_inc(sem("parb_in"), 16)
            for i, name in enumerate(("ssm_c_re_2", "ssm_c_im_2")):
                for r in range(2):
                    pool.dma_start(craw[:, i, :, r, :],
                                   bass.AP(a[name].tensor, 0, [[64, P], [64 * P, 4], [1, 64]])).then_inc(sem("parb_in"), 16)
            pool.wait_ge(sem("par_in"), 16 * 3)
            d = [dtl[0:16, i, :] for i in range(8)]
            lre, lim = v(20), v(21)
            link(TTo(out=v(17), in0=lre, in1=lre, op=ALU.mult))
            link(TTo(out=v(18), in0=lim, in1=lim, op=ALU.mult))
            TTo(out=v(17), in0=v(17), in1=v(18), op=ALU.add).then_inc(sem("lam_sq"), 1)
            exp_(d[1], d[0], d[2:6], dti[0:16, :])

            def by_dt(o, x):
                link(TTo(out=o.rearrange("q (g p) -> q g p", g=2), in0=x.rearrange("q (g p) -> q g p", g=2),
                         in1=d[1].unsqueeze(2).to_broadcast([16, 2, 64]), op=ALU.mult))
            by_dt(v(8), lre)
            by_dt(v(9), lim)
            exp_(v(10), v(8), [v(11), v(12), v(13), v(14)], pvi[0:16, :])
            link(TS(v(11), v(9), 0.15915494309189535, 12582912.0, ALU.mult, ALU.add))
            link(TS(v(11), v(11), -12582912.0, None, ALU.add))
            for c in (6.28125, 0.0019350051879882812, 3.0199159819567e-07):
                link(STT(out=v(9), in0=v(11), scalar=-c, in1=v(9), op0=ALU.mult, op1=ALU.add))
            link(TS(v(9), v(9), 0.125, None, ALU.mult))
            link(TTo(out=v(12), in0=v(9), in1=v(9), op=ALU.mult))
            link(TS(v(13), v(12), -1.0 / 5040, None, ALU.mult))
            for c in (1.0 / 120, -1.0 / 6):
                link(STT(out=v(13), in0=v(13), scalar=c, in1=v(12), op0=ALU.add, op1=ALU.mult))
            link(STT(out=v(13), in0=v(13), scalar=1.0, in1=v(9), op0=ALU.add, op1=ALU.mult))
            link(TS(v(14), v(12), 1.0 / 40320, None, ALU.mult))
            for c in (-1.0 / 720, 1.0 / 24, -0.5):
                link(STT(out=v(14), in0=v(14), scalar=c, in1=v(12), op0=ALU.add, op1=ALU.mult))
            for _i in range(3):
                double(v(13), v(14), v(15))
            link(TTo(out=v(15), in0=v(10), in1=v(14), op=ALU.mult))
            link(TTo(out=v(0), in0=v(10), in1=v(15), op=ALU.add))
            link(TTo(out=v(1), in0=v(10), in1=v(13), op=ALU.mult))
            link(STT(out=v(16), in0=v(10), scalar=-1.0, in1=v(15), op0=ALU.add, op1=ALU.add))
            pool.wait_ge(sem("lam_inv"), 1)
            link(TTo(out=v(18), in0=v(16), in1=lre, op=ALU.mult))
            link(TTo(out=v(19), in0=v(1), in1=lim, op=ALU.mult))
            link(TTo(out=v(18), in0=v(18), in1=v(19), op=ALU.add))
            link(TTo(out=v(2), in0=v(18), in1=v(17), op=ALU.mult))
            link(TTo(out=v(18), in0=v(1), in1=lre, op=ALU.mult))
            link(TTo(out=v(19), in0=v(16), in1=lim, op=ALU.mult))
            link(TTo(out=v(18), in0=v(18), in1=v(19), op=ALU.subtract))
            link(TTo(out=v(3), in0=v(18), in1=v(17), op=ALU.mult))
            link(TTo(out=v(4), in0=v(10), in1=v(10), op=ALU.mult))
            link(TTo(out=v(4), in0=v(4), in1=v(4), op=ALU.mult))
            link(TTo(out=v(4), in0=v(4), in1=v(4), op=ALU.mult))
            for _i in range(3):
                double(v(13), v(14), v(15))
            link(CP(v(5), v(14)))
            CP(v(6), v(13)).then_inc(sem("par"), 1)

            pool.wait_ge(sem("par_ev"), 3)
            def cmul(ore, oim, xre, xim, yre, yim, t1, t2):
                link(TTo(out=t1, in0=xre, in1=yre, op=ALU.mult))
                link(TTo(out=t2, in0=xim, in1=yim, op=ALU.mult))
                link(TTo(out=ore, in0=t1, in1=t2, op=ALU.subtract))
                link(TTo(out=t1, in0=xre, in1=yim, op=ALU.mult))
                link(TTo(out=t2, in0=xim, in1=yre, op=ALU.mult))
                link(TTo(out=oim, in0=t1, in1=t2, op=ALU.add))

            def bc(x, n):
                return x.unsqueeze(2).to_broadcast([P, SSM_Q, n])

            def ssm_setup():
                t = [tmp[:, i, 0:256].rearrange("p (q h) -> p q h", h=16) for i in range(2)]
                cmul(bbar[:, 0], bbar[:, 1], bc(apar[:, 2, :], 16), bc(apar[:, 3, :], 16), braw[:, 0], braw[:, 1], *t)
                link(pool.memset(bpair[:], 0.0))
                for g in range(2):
                    r = slice(64 * g, 64 * g + 64)
                    for c in range(2):
                        link(CP(bpair[r, c, :, g, :], bbar[r, c, :, :]))
                link(pool.memset(pw[:, 0, :, 0:1], 1.0))
                link(pool.memset(pw[:, 1, :, 0:1], 0.0))
                link(CP(pw[:, :, :, 1:2].rearrange("p c q o -> p c (q o)"), apar[:, 0:2, :]))
                for n in (1, 2, 4):
                    t = [tmp[:, i, 0:16 * n].rearrange("p (q h) -> p q h", h=n) for i in range(2)]
                    cmul(pw[:, 0, :, n + 1:2 * n + 1], pw[:, 1, :, n + 1:2 * n + 1], pw[:, 0, :, 1:n + 1], pw[:, 1, :, 1:n + 1],
                         pw[:, 0, :, n:n + 1].to_broadcast([P, SSM_Q, n]), pw[:, 1, :, n:n + 1].to_broadcast([P, SSM_Q, n]), *t)
                for j in range(8):
                    link(CP(pwr[:, :, :, j:j + 1].rearrange("p c q o -> p c (q o)"),
                            pw[:, :, :, 7 - j:8 - j].rearrange("p c q o -> p c (q o)")))

            def ssm_products(qq):
                qs = slice(4 * qq, 4 * qq + 4)

                def b4(x, n):
                    return x.unsqueeze(3).to_broadcast([P, 4, n, 16])

                def b3(x, n):
                    return x.unsqueeze(2).to_broadcast([P, 4, n, 16])
                if qq >= 1:
                    pool.wait_ge(sem("w1_t"), qq)
                    pool.wait_ge(sem("kk_t"), qq)
                    pool.wait_ge(sem("w2_out"), 32 * qq)
                t = [tmp[:, i, 0:512].rearrange("p (q j h) -> p q j h", q=4, j=8) for i in range(2)]
                o = [w1t[:, c].rearrange("p q (j h) -> p q j h", j=8) for c in range(2)]
                cmul(o[0], o[1], b4(pwr[:, 0, qs, :], 8), b4(pwr[:, 1, qs, :], 8), b3(bbar[:, 0, qs, :], 8), b3(bbar[:, 1, qs, :], 8), *t)
                t = [tmp[:, i, :].rearrange("p (q j h) -> p q j h", q=4, j=9) for i in range(2)]
                cmul(cpw[:, 0], t[0], b4(pw[:, 0, qs, :], 9), b4(pw[:, 1, qs, :], 9), b3(ctp[:, 0, qs, :], 9), b3(ctp[:, 1, qs, :], 9), *t)
                link(TS(cpw[:, 1], t[0], -1.0, None, ALU.mult))
                pool.sem_inc(sem("w1t"), 1)

            pool.wait_ge(sem("n2_lo"), since("n2_lo", KD))
            ssm_setup()
            for qq in range(SSM_Q // 4):
                ssm_products(qq)
            for k in range(1, KD):
                pool.wait_ge(sem("n3_sq"), since("n3_sq", k + 1))
                if k == 1:
                    pool.wait_ge(sem("n3_ac"), since("n3_ac", 1))
                else:
                    pool.wait_ge(sem("xf_ac"), k)
                TTo(out=sq3[:, 0, :], in0=sq3[:, 0, :], in1=sq3[:, k, :], op=ALU.add).then_inc(sem("xf_ac"), 2 if k == 1 else 1)
            pool.wait_ge(sem("fc2_evac"), 8)
            pool.memset(tmat[:], 0.0).then_inc(sem("tz"), 1)
            pool.dma_start(w1s[:], scr["w1"].rearrange("c p q n -> p c q n")).then_inc(sem("w1s_in"), 16)
            pool.wait_ge(sem("tz"), 1)
            for j in range(SSM_L):
                for g in range(2):
                    pool.dma_start(tmat[16 * j:16 * j + 16, g:32:2, 16 * j:P],
                                   scr["kk"][16 * g:16 * g + 16, :, 0:P - 16 * j]).then_inc(sem("t_in"), 16)
            for m in range(4):
                freed(pool, G_IN2 + m)
                pool.dma_start(scr["u"][m], uT[:, m, :, :]).then_inc(sem("u_out"), 16)
            pool.wait_ge(sem("u_out"), 16 * 4)
            for j in range(SSM_L):
                pool.dma_start(ug[16 * j:16 * j + 16, :, :],
                               bass.AP(scr["u"].tensor, j * SSM_C, [[T, 16], [16 * T, 32], [1, SSM_C]])).then_inc(sem("u_in"), 16)
            pool.wait_ge(sem("s_done"), 1)
            pool.dma_start(w2s[:], scr["w2"].rearrange("c p q n -> p c q n")).then_inc(sem("w2s_in"), 16)
            pool.wait_ge(sem("v2_t"), 4)
            pool.dma_start(bias2[:], bass.AP(scr["relp"].tensor, P - 1, [[HEADS * 640 - 1, P], [640, HEADS], [1, T]])
                           ).then_inc(sem("bias2_in"), 16)
            pool.wait_ge(sem("bias2_in"), 16)
            pool.memset(bias2[0:64, :, T - 64:T], NEG).then_inc(sem("bias2_ok"), 1)
            pool.wait_ge(sem("yg_ev"), 4)
            pool.dma_start(scr["y"], yg[:].rearrange("p g c -> p (g c)")).then_inc(sem("y_out"), 16)
            pool.wait_ge(sem("y_out"), 16)
            for m in range(4):
                for g in range(8):
                    pool.dma_start(yssm[16 * g:16 * g + 16, m, :, :],
                                   bass.AP(scr["y"].tensor, (8 * m + g) * SSM_C, [[32 * SSM_C, 16], [16 * 32 * SSM_C, SSM_L], [1, SSM_C]])
                                   ).then_inc(sem("y_in"), 16)
            pool.wait_ge(sem("fc2b_free"), 1)
            pool.dma_start(gfin[:], a["norm_final_g_2"].partition_broadcast(P)).then_inc(sem("gfin_in"), 16)
            pool.wait_ge(sem("gfin_in"), 16)

        @block.tensor
        def _(pe):
            def mm3(o, lhi, llo, rhi, rlo, start, stop, skip=False):
                pe.matmul(o, lhi, rhi, start=start, stop=False, skip_group_check=skip)
                pe.matmul(o, lhi, rlo, start=False, stop=False, skip_group_check=skip)
                return pe.matmul(o, llo, rhi, start=False, stop=stop, skip_group_check=skip)

            def unit_ready(u):
                pe.wait_ge(sem("w_lo"), u + 1)

            def bank_free(g):
                if g >= 2:
                    freed(pe, g - 2)

            def dense(u, g, hi, lo, kt=KD, off=0, stride=P, ready=None, first=0):
                for k in range(kt):
                    if ready is not None:
                        pe.wait_ge(sem(ready), since(ready, k + 1))
                    w = slice(off + k * stride, off + k * stride + P)
                    last = mm3(ps[:, bank(g), :], whi[:, slot(u), w], wlo[:, slot(u), w],
                               hi[:, first + k, :], lo[:, first + k, :], k == 0, k == kt - 1)
                return last

            def norm_rows(nm):
                pe.wait_ge(sem(nm + "_ac"), since(nm + "_ac", NORM[nm][1]))
                for t in range(TT):
                    last = pe.matmul(ps[:, 6, t:t + 1], hb[:, 0, P * t:P * t + P], ones[:, 0:1], start=True, stop=True)
                last.then_inc(sem(nm + "_st"), 1)

            def norm_spread(nm):
                pe.wait_ge(sem(nm + "_dg"), since(nm + "_dg", 1))
                pe.matmul(ps[:, 7, :], ones[:, :], diag, start=True, stop=True).then_inc(sem(nm + "_r"), 1)

            def norm_sum(nm):
                norm_rows(nm)
                norm_spread(nm)

            def attention(nm):
                heads, pb, tb = ATT[nm]
                N = 4 * len(heads)
                for s in range(N + 3):
                    if nm == "nsa" and s > 0 and s % 16 == 0:
                        part = s // 16 - 1
                        pe.wait_ge(sem("ada2_used"), s)
                        for n in range(KD):
                            last = pe.matmul(ps[:, 0, KD * part + n:KD * part + n + 1], ada2[:, n // 4, P * (n % 4):P * (n % 4) + P],
                                             ones[:, 0:1], start=True, stop=True)
                        last.then_inc(sem("ada2_t"), 1)
                    if s < N:
                        hd, b = heads[s // 4], s % 4
                        if s >= 3:
                            pe.wait_ge(sem(nm + "_p"), since(nm + "_p", s - 2))
                        w = P * (b + 1)
                        pe.matmul(ps[:, score_bank(s), 0:w], hd["q"][:, P * b:P * b + P], hd["k"][:, 0:w],
                                  start=True, stop=True).then_inc(sem(nm + "_qk"), 1)
                    r = s - 2
                    if 0 <= r < N:
                        pe.wait_ge(sem(nm + "_p"), since(nm + "_p", r + 1))
                        if r >= 2:
                            what, count = turned(nm, r - 2)
                            pe.wait_ge(sem(what), count)
                        for kb in range(r % 4 + 1):
                            last = pe.transpose(ps[:, 4 + r % 2, P * kb:P * kb + P], pb[:, r % 4, P * kb:P * kb + P], ident[:, :])
                        last.then_inc(sem(nm + "_t"), 1)
                    r = s - 3
                    if r >= 0:
                        hi_, b = r // 4, r % 4
                        what, count = turned(nm, r)
                        pe.wait_ge(sem(what), count)
                        if b == 0 and hi_ >= 2:
                            pe.wait_ge(sem(nm + "_o"), since(nm + "_o", hi_ - 1))
                        for kb in range(b + 1):
                            last = pe.matmul(ps[:, 6 + hi_ % 2, DH * b:DH * b + DH], tb[:, r % 4, P * kb:P * kb + P],
                                             heads[hi_]["v"](kb), start=(kb == 0), stop=(kb == b))
                        last.then_inc(sem(nm + "_pv"), 1)

            pe.wait_ge(sem("ident_in"), 16)
            pe.wait_ge(sem("x_in"), 16)
            for k in range(KD):
                if k >= 2:
                    pe.wait_ge(sem(("xt_ev", "xt_ev2")[k % 2]), k // 2)
                for t in range(TT):
                    last = pe.transpose(ps[:, 2 + k % 2, P * t:P * t + P], xs[:, t, P * k:P * k + P], ident[:, :])
                last.then_inc(sem("xt_t"), 1)
            pe.wait_ge(sem("vec_in"), 16 * 6)
            pe.wait_ge(sem("vec2_in"), 16 * (len(VROWS) - 6 + 2))
            pe.transpose(ps[:, 4, 0:NV], vrow[0:NV, 0, :], ident[0:NV, 0:NV])
            pe.transpose(ps[:, 4, NV:NV + 32], vrow[0:32, 1, :], ident[0:32, 0:32]).then_inc(sem("vec_t"), 1)

            pe.wait_ge(sem("vec_ok"), 1)
            pe.wait_ge(sem("ones_ok"), 1)
            for k in range(KD):
                pe.wait_ge(sem(f"ada_in{k % 4}"), 16 * (k // 4 + 1))
                for n in range(KD):
                    last = pe.matmul(ps[:, 4, n:n + 1], aring[:, k % 4, D + P * n:D + P * n + P], col("c", k),
                                     start=(k == 0 and n == 0), stop=(k == KD - 1), skip_group_check=True)
                last.then_inc(sem("ada_pe"), 1)
                if k == 5:
                    norm_rows("n1")
            pe.wait_ge(sem("ada_used"), KD)
            for n in range(KD):
                last = pe.matmul(ps[:, 5, n:n + 1], ada1[:, P * n:P * n + P], ones[:, 0:1], start=True, stop=True)
            last.then_inc(sem("ada_t"), 1)
            norm_spread("n1")

            def parameters():
                pe.wait_ge(sem("par"), 1)
                pe.wait_ge(sem("parb_in"), 16 * 6)
                for i in range(7):
                    pe.transpose(ps[:, 2, 16 * i:16 * i + 16], pv[0:16, i, :], ident[0:16, 0:16])
                for c in range(2):
                    for m in range(4):
                        last = pe.transpose(ps[:, (3, 6)[c], P * m:P * m + P], craw[:, c, m, :, :].rearrange("p r n -> p (r n)"), ident[:, :])
                last.then_inc(sem("par_t"), 1)

            def ssm_chunk(qq):
                pe.wait_ge(sem("w1t"), qq + 1)
                if qq >= 1:
                    pe.wait_ge(sem("stg_ev"), 3 * qq)
                for c in range(2):
                    for i in range(4):
                        last = pe.transpose(ps[:, 2 + c, P * i:P * i + P], w1t[:, c, i, :], ident[:, :])
                last.then_inc(sem("w1_t"), 1)
                for i in range(4):
                    for c in range(2):
                        last = pe.matmul(ps[0:32, 4, P * i:P * i + P], bpair[:, c, 4 * qq + i, :, :].rearrange("p g h -> p (g h)"),
                                         cpw[:, c, i, 0:8, :].rearrange("p j h -> p (j h)"), start=(c == 0), stop=(c == 1))
                last.then_inc(sem("kk_t"), 1)

            def compress():
                for w in range(2):
                    pe.wait_ge(sem("flat"), w + 1)
                    if w == 1:
                        pe.wait_ge(sem("hid"), 4)
                    pe.wait_ge(sem(f"ada_in{2 + w}"), 16 * (2 + 4))
                    for i in range(4):
                        for m in range(4):
                            for half in range(2):
                                last = pe.matmul(ps[:, 2 + half, 0:62],
                                                 cmpw[4 * w + i][:, 256 * m + P * half:256 * m + P * half + P],
                                                 flat[:, w, 4 * i + m, :],
                                                 start=(i == 0 and m == 0), stop=(i == 3 and m == 3))
                        last.then_inc(sem("p_used"), 1)
                pe.wait_ge(sem("hid"), 8)
                pe.wait_ge(sem("w2_in"), 48)
                for half in range(2):
                    last = pe.matmul(ps[:, 4, 0:62], w2d[:, half, :, :].rearrange("p r d -> p (r d)"),
                                     hid[:, 0, half, :, 0:NCMP], start=(half == 0), stop=(half == 1))
                pe.wait_ge(sem("hidr"), 2)
                for g in range(2):
                    for half in range(2):
                        last = pe.matmul(ps[:, 5, DH * g:DH * g + DH],
                                         hidr[:, half, g, :, :].rearrange("p r n -> p (r n)"), w2v[:, half, :],
                                         start=(half == 0), stop=(half == 1))
                last.then_inc(sem("cmp_t"), 1)

            for i in range(len(A1_COLS)):
                u, g = U_A1 + i, G_A1 + i
                unit_ready(u)
                bank_free(g)
                dense(u, g, hhi, hlo, ready="n1_lo" if i == 0 else None).then_inc(sem("tile"), 1)
                if i == 6:
                    for br in range(2):
                        freed(pe, G_A1 + 4 + br)
                        for t in range(TT):
                            last = pe.transpose(ps[:, 2 + br, P * t:P * t + P], zv[:, br, P * t:P * t + P], ident[:, :])
                    last.then_inc(sem("vt_t"), 1)
                if i == 4:
                    compress()
            u, g = U_TAIL, G_A1 + 15
            unit_ready(u)
            bank_free(g)
            dense(u, g, hhi, hlo).then_inc(sem("tile"), 1)
            pe.wait_ge(sem("zg"), 1)
            for t in range(TT):
                last = pe.transpose(ps[:, 2, 24 * t:24 * t + 24], zg[0:24, P * t:P * t + P], ident[0:24, 0:24])
            last.then_inc(sem("gate_t"), 1)
            norm_sum("ncq")
            for h in range(HEADS):
                u, g = U_UQ + h // 2, G_UQ + h
                if h % 2 == 0:
                    unit_ready(u)
                bank_free(g)
                dense(u, g, cqhi, cqlo, kt=3, off=P * (h % 2), stride=2 * P,
                      ready="ncq_lo" if h == 0 else None).then_inc(sem("tile"), 1)
                if h == 0:
                    pe.wait_ge(sem("ncq_lo"), since("ncq_lo", 3))
                    norm_sum("nckv")
            u = U_UK
            unit_ready(u)
            for i in range(4):
                g = G_UK + i
                bank_free(g)
                dense(u, g, ckhi, cklo, kt=2, off=P * i, stride=512,
                      ready="nckv_lo" if i == 0 else None).then_inc(sem("tile"), 1)
            u = U_UV
            unit_ready(u)
            for t in range(TT):
                g = G_UV + t
                bank_free(g)
                for k in range(2):
                    last = mm3(ps[:, bank(g), :], ckhi[:, k, P * t:P * t + P], cklo[:, k, P * t:P * t + P],
                               whi[:, slot(u), 512 * k:512 * k + 512], wlo[:, slot(u), 512 * k:512 * k + 512], k == 0, k == 1)
                last.then_inc(sem("tile"), 1)
            pe.wait_ge(sem("gates"), 1)
            for b in range(TT):
                for h in range(HEADS):
                    r = slice(64 * (h % 2), 64 * (h % 2) + 64)
                    c = 32 * (4 * b + h // 2)
                    last = pe.matmul(ps[:, 2 + h % 2, c:c + NCMP], qT[r, h // 2, P * b:P * b + P], kcT[r, h // 4, :],
                                     start=True, stop=True)
            last.then_inc(sem("cs_t"), 1)
            pe.wait_ge(sem("cp"), 1)
            for b in range(TT):
                for g in range(2):
                    last = pe.transpose(ps[:, 4 + b // 2, P * (2 * (b % 2) + g):P * (2 * (b % 2) + g) + P],
                                        cp[:, 8 * b + 4 * g:8 * b + 4 * g + 4, :].rearrange("p h n -> p (h n)"), ident[:, :])
            last.then_inc(sem("cp_t"), 1)
            pe.wait_ge(sem("cpt"), 2)
            for b in range(TT):
                for g in range(2):
                    last = pe.matmul(ps[:, (6, 7, 2, 3)[b], 256 * g:256 * g + 256],
                                     cpt[:, 2 * b + g, :], vblk[:, g, :, :].rearrange("p h d -> p (h d)"), start=True, stop=True)
            last.then_inc(sem("oc_t"), 1)
            pe.wait_ge(sem("oc_ev"), 2)
            freed(pe, G_Y - 2)
            freed(pe, G_Y - 1)
            attention("nsa")
            pe.wait_ge(sem("nsa_o"), since("nsa_o", 16))
            attention("mla")

            pe.wait_ge(sem("mla_o"), since("mla_o", 8))
            for i in range(8):
                src = (onsa, omla)[i // 4]
                if i >= 2:
                    pe.wait_ge(sem("ot_lo"), i - 1)
                for t in range(TT):
                    last = pe.transpose(ps[:, 4 + i % 2, P * t:P * t + P], src[:, t, P * (i % 4):P * (i % 4) + P], ident[:, :])
                last.then_inc(sem("ot_t"), 1)
            pe.wait_ge(sem("modc"), 2)
            for n in range(KD):
                for j in range(2):
                    u, g = U_Y + 3 * n + j, G_Y + 4 * n + j
                    unit_ready(u)
                    bank_free(g)
                    dense(u, g, hhi, hlo).then_inc(sem("tile"), 1)
                u = U_Y + 3 * n + 2
                unit_ready(u)
                for j in range(2):
                    g = G_Y + 4 * n + 2 + j
                    bank_free(g)
                    if n == 0 and j == 0:
                        pe.wait_ge(sem("ot_lo"), 8)
                    dense(u, g, othi, otlo, kt=4, off=512 * j, first=4 * j).then_inc(sem("tile"), 1)
                if n == 6:
                    parameters()

            def fc1_part(first, n, ready=None):
                dense_loop(U_FC1 + first, G_FC1 + first, n, hhi, hlo, ready)

            def dense_loop(u0, g0, n, hi, lo, ready=None, order=range(KD)):
                if ready:
                    for j in range(RING):
                        unit_ready(u0 + j)
                        freed(pe, g0 + j - 2)
                        for m, k in enumerate(order):
                            if j == 0 and k < ready[1]:
                                pe.wait_ge(sem(ready[0]), since(ready[0], k + 1))
                            w = slice(P * k, P * k + P)
                            last = mm3(ps[:, bank(g0 + j), :], whi[:, slot(u0 + j), w], wlo[:, slot(u0 + j), w],
                                       hi[:, k, :], lo[:, k, :], m == 0, m == KD - 1)
                        last.then_inc(sem("tile"), 1)
                    u0, g0, n = u0 + RING, g0 + RING, n - RING
                with loop(pe, n // RING) as i:
                    for j in range(RING):
                        pe.wait_ge(sem("w_lo"), u0 + RING * i + j + 1)
                        freed(pe, g0 + j - 2, i)
                        dense(u0 + j, g0 + j, hi, lo).then_inc(sem("tile"), 1)

            dense_loop(U_OUT, G_OUT, KD, yhi, ylo, ("y_lo", KD))
            norm_sum("n2")
            fc1_part(0, FC1_PARTS[0], ("n2_lo", KD))
            for qq in range(4):
                ssm_chunk(qq)
                fc1_part(sum(FC1_PARTS[:qq + 1]), FC1_PARTS[qq + 1])
            pe.wait_ge(sem("stg_ev"), 12)

            def rows_acc(u0, n, nm, natural, g_last):
                freed(pe, g_last - 1)
                freed(pe, g_last)

                def product(j, b, start, stop):
                    u, f = u0 + j, j % 2
                    if natural:
                        t, c = b // 2, 512 * (b % 2)
                        return mm3(ps[:, b, :], fhi[:, f, P * t:P * t + P], flo[:, f, P * t:P * t + P],
                                   whi[:, slot(u), c:c + 512], wlo[:, slot(u), c:c + 512], start, stop)
                    return mm3(ps[:, b, :], whi[:, slot(u), P * b:P * b + P], wlo[:, slot(u), P * b:P * b + P],
                               fhi[:, f, :], flo[:, f, :], start, stop)

                def step(j, idx, start, stop):
                    pe.wait_ge(sem("w_lo"), u0 + idx + 1)
                    pe.wait_ge(sem(nm + "_lo"), since(nm + "_lo", idx + 1))
                    for b in range(8):
                        last = product(j, b, start, stop)
                    last.then_inc(sem(nm + "_used"), 1)
                for j in range(2):
                    step(j, j, j == 0, False)
                turns = (n - 4) // 4
                with loop(pe, turns) as i:
                    for j in range(4):
                        step(2 + j, 4 * i + 2 + j, False, False)
                for j in range(2 + 4 * turns, n - 2):
                    step(j, j, False, False)
                pe.wait_ge(sem("w_lo"), u0 + n)
                pe.wait_ge(sem(nm + "_lo"), since(nm + "_lo", n))
                for b in range(8):
                    for j in (n - 2, n - 1):
                        last = product(j, b, False, j == n - 1)
                    last.then_inc(sem(nm + "_bank"), 1)

            rows_acc(U_FC2, NF1, "f1", False, G_FC1 + NF1 - 1)
            pe.wait_ge(sem("xf_ac"), KD)
            for t in range(TT):
                last = pe.matmul(ps[:, 0, t:t + 1], sq3[:, 0, P * t:P * t + P], ones[:, 0:1], start=True, stop=True)
            last.then_inc(sem("xf_st"), 1)
            pe.wait_ge(sem("fc2_evac"), 8)
            norm_sum("n3")
            pe.wait_ge(sem("xf_dg"), 1)
            pe.matmul(ps[:, 6, :], ones[:, :], hb[:, 0, :], start=True, stop=True).then_inc(sem("xf_r"), 1)
            dense_loop(U_IN2, G_IN2, 8, hhi, hlo, ("n3_lo", KD))
            pe.wait_ge(sem("u_in"), 16 * SSM_L)
            pe.wait_ge(sem("w1s_in"), 16)
            for c in range(2):
                for g in range(32):
                    q, r = g // 2, slice(64 * (g % 2), 64 * (g % 2) + 64)
                    last = pe.matmul(ps[r, 2 + 2 * c + q // 8, SSM_C * (q % 8):SSM_C * (q % 8) + SSM_C],
                                     w1s[:, c, q, r], ug[:, g, :], start=True, stop=True)
            last.then_inc(sem("s_done"), 1)
            dense_loop(U_IN2 + 8, G_IN2 + 8, 4, hhi, hlo)
            pe.wait_ge(sem("s_ev"), 4)
            for i in range(4):
                u = U_V2 + i
                unit_ready(u)
                for t in range(TT):
                    for k in range(2):
                        last = mm3(ps[:, 2 + t, :], hhi[:, 2 * i + k, P * t:P * t + P], hlo[:, 2 * i + k, P * t:P * t + P],
                                   whi[:, slot(u), 512 * k:512 * k + 512], wlo[:, slot(u), 512 * k:512 * k + 512],
                                   i == 0 and k == 0, i == 3 and k == 1)
                last.then_inc(sem("v2_t"), 1)
            pe.wait_ge(sem("v2_ev"), 4)
            pe.wait_ge(sem("xst"), 2)
            pe.wait_ge(sem("w2s_in"), 16)
            pe.wait_ge(sem("t_in"), 16 * 2 * SSM_L)
            for g in range(32):
                q, r = g // 2, slice(64 * (g % 2), 64 * (g % 2) + 64)
                o = ps[:, 2 + 2 * (g % 2) + q // 8, SSM_C * (q % 8):SSM_C * (q % 8) + SSM_C]
                pe.matmul(o, w2s[r, 0, q, :], sB[r, q, :], start=True, stop=False)
                pe.matmul(o, w2s[r, 1, q, :], sA[r, q, :], start=False, stop=False)
                last = pe.matmul(o, tmat[:, g, :], ug[:, g, :], start=False, stop=True)
            last.then_inc(sem("ssm_y"), 1)
            pe.wait_ge(sem("yg_ev"), 4)
            freed(pe, G_GLU - 1)
            attention("chk")
            for i in range(4):
                u, g = U_GLU + i // 2, G_GLU + i
                unit_ready(u)
                bank_free(g)
                if i == 0:
                    pe.wait_ge(sem("g_lo"), 4)
                dense(u, g, ghi, glo, kt=4, off=P * (i % 2), stride=2 * P).then_inc(sem("tile"), 1)
                if i % 2 == 1:
                    for m in (i - 1, i):
                        if m >= 2:
                            pe.wait_ge(sem("ya_hb"), m - 1)
                        for t in range(TT):
                            if m == 0:
                                pe.wait_ge(sem("ya_n"), t + 1)
                            last = pe.transpose(ps[:, 4 + m % 2, P * t:P * t + P], yatt[:, t, P * m:P * m + P], ident[:, :])
                        last.then_inc(sem("ya_t"), 1)
            pe.wait_ge(sem("chk_o"), since("chk_o", 8))
            norm_sum("nssm")
            dense_loop(U_OUT2, G_OUT2, KD, hhi, hlo, ("nssm_lo", 4), order=[4, 5, 6, 7, 0, 1, 2, 3])
            norm_sum("n4")
            for t in range(TT):
                for half in range(2):
                    i = 2 * t + half
                    if i >= 4:
                        pe.wait_ge(sem("xn_ev"), i - 3)
                    for k in range(4):
                        last = pe.transpose(ps[:, 2 + i % 4, P * k:P * k + P], xT[:, 4 * half + k, P * t:P * t + P], ident[:, :])
                    last.then_inc(sem("xn_t"), 1)
            dense_loop(U_GU, G_GU, 2 * NF2, hhi, hlo, ("n4_lo", KD))
            pe.wait_ge(sem("xn_ev"), 8)
            rows_acc(U_DN, NF2, "f2", True, G_GU + 2 * NF2 - 1)

        @block.scalar
        def _(act):
            A = act.activation

            def split_hi(u):
                act.wait_ge(sem(f"w_in{slot(u)}"), 16 * w_count(u))
                if u >= RING:
                    name, value = used(u - RING)
                    act.wait_ge(sem(name), value)
                A(whi[:, slot(u), :], wraw[:, slot(u), :], ACT.Copy).then_inc(sem("w_hi"), 1)

            def split_hi_turn(u, i, name, value):
                act.wait_ge(sem(f"w_in{slot(u)}"), 16 * w_count(u) + 16 * i)
                act.wait_ge(sem(name), value)
                A(whi[:, slot(u), :], wraw[:, slot(u), :], ACT.Copy).then_inc(sem("w_hi"), 1)

            def ssm_out(qq):
                act.wait_ge(sem("w1t"), qq + 1)
                for c in range(2):
                    act.dma_start(scr["w2"][c, :, 4 * qq:4 * qq + 4, :],
                                  cpw[:, c, :, 1:9, :].rearrange("p q j h -> p q (j h)")).then_inc(sem("w2_out"), 16)
                act.wait_ge(sem("w1_t"), qq + 1)
                if qq >= 1:
                    act.wait_ge(sem("w1_out"), 32 * qq)
                    act.wait_ge(sem("kk_out"), 16 * qq)
                for c in range(2):
                    A(stg[:, c, :, :].rearrange("p q n -> p (q n)"), ps[:, 2 + c, :], ACT.Copy).then_inc(sem("stg_ev"), 1)
                act.wait_ge(sem("kk_t"), qq + 1)
                A(kst[0:32, :, :].rearrange("p g n -> p (g n)"), ps[0:32, 4, :], ACT.Copy).then_inc(sem("stg_ev"), 1)
                act.wait_ge(sem("stg_ev"), 3 * qq + 3)
                for c in range(2):
                    act.dma_start(scr["w1"][c, :, 4 * qq:4 * qq + 4, :], stg[:, c, :, :]).then_inc(sem("w1_out"), 16)
                act.dma_start(scr["kk"][:, 4 * qq:4 * qq + 4, :], kst[0:32, :, :]).then_inc(sem("kk_out"), 16)

            def nxt(u):
                if u + AHEAD < U_END:
                    split_hi(u + AHEAD)

            tables = [0]

            def table_for(func):
                tables[0] += 1
                spare = 2 + tables[0] % 6
                A(eps[:, spare:spare + 1], eps[:, 0:1], func)

            def norm_square(nm, k):
                src, n, buf = NORM[nm]
                if k >= 3:
                    act.wait_ge(sem(nm + "_ac"), since(nm + "_ac", k - 2))
                A(buf[:, k % 3, :], src(k), ACT.Square).then_inc(sem(nm + "_sq"), 1)

            def norm_root(nm, width):
                table_for(ACT.Sqrt)
                act.wait_ge(sem(nm + "_st"), since(nm + "_st", 1))
                A(stat[:, 1, :], ps[:, 6, 0:4], ACT.Sqrt, scale=1.0 / width, bias=eps[:, 0:1]).then_inc(sem(nm + "_rt"), 1)

            def norm_squares(nm, width, waits=None):
                for k in range(NORM[nm][1]):
                    if waits:
                        waits(k)
                    norm_square(nm, k)
                norm_root(nm, width)

            def norm_hi(nm):
                _, add, hi, _ = AFTER[nm]
                for k in range(NORM[nm][1]):
                    act.wait_ge(sem(nm + "_h"), since(nm + "_h", k + 1))
                    if add is None:
                        e = A(hi[:, k, :], hb[:, k % 2, :], ACT.Copy)
                    else:
                        e = A(hi[:, k, :], hb[:, k % 2, :], ACT.Identity, bias=add(k))
                    e.then_inc(sem(nm + "_hi"), 1)

            def copy_out(dst, src, g, last=True):
                act.wait_ge(sem("tile"), g + 1)
                e = A(dst, src, ACT.Copy)
                return free(e, g) if last else e

            def attention(nm):
                heads, pb, tb = ATT[nm]
                N = 4 * len(heads)
                for s in range(N + 2):
                    if s < N:
                        b = s % 4
                        w = P * (b + 1)
                        act.wait_ge(sem(nm + "_s"), since(nm + "_s", s + 1))
                        if s >= 4:
                            act.wait_ge(sem(nm + "_t"), since(nm + "_t", s - 3))
                        if b == 0 and s >= 8:
                            act.wait_ge(sem(nm + "_o"), since(nm + "_o", s // 4 - 1))
                        A(pb[:, s % 4, 0:w], ps[:, score_bank(s), 0:w], ACT.Exp, bias=smax[:, s % 4:s % 4 + 1], scale=-1.0,
                          accum_out=rsum[:, (s // 4) % 2, b:b + 1]).then_inc(sem(nm + "_p"), 1)
                    r = s - 2
                    if r >= 0 and turned(nm, r)[0] == nm + "_pta":
                        w = P * (r % 4 + 1)
                        act.wait_ge(sem(nm + "_t"), since(nm + "_t", r + 1))
                        if r >= 4:
                            act.wait_ge(sem(nm + "_pv"), since(nm + "_pv", r - 3))
                        A(tb[:, r % 4, 0:w], ps[:, 4 + r % 2, 0:w], ACT.Copy).then_inc(sem(nm + "_pta"), 1)

            act.dma_start(ident[:], a["identity"]).then_inc(sem("ident_in"), 16)
            for i, (name, (r, n)) in enumerate(VROWS.items()):
                if i < 6:
                    act.dma_start(vrow[r:r + n, 0, :], bass.AP(a[name].tensor, 0, [[P, n], [1, P]])).then_inc(sem("vec_in"), 16)

            for k in range(0, KD, 2):
                act.wait_ge(sem("xt_t"), k + 1)
                A(xT[:, k, :], ps[:, 2, :], ACT.Copy).then_inc(sem("xt_ev"), 1)
            act.wait_ge(sem("ones_ok"), 2)
            norm_squares("n1", D, lambda k: act.wait_ge(sem(("xt_ev", "xt_ev2")[k % 2]), k // 2 + 1))
            for u in range(AHEAD):
                split_hi(u)
            norm_hi("n1")
            for i in range(len(A1_COLS)):
                u, g, c = U_A1 + i, G_A1 + i, A1_COLS[i]
                nxt(u)
                if c in (C_KC, C_VC):
                    w = i
                    act.wait_ge(sem("tile"), g + 1)
                    for gr in range(2):
                        A(x2[0:64, w, gr, :], ps[64 * gr:64 * gr + 64, bank(g), :], ACT.Copy).then_inc(sem("x2"), 1)
                        e = A(x2[64:128, w, gr, 0:T - 1], ps[64 * gr:64 * gr + 64, bank(g), 1:T], ACT.Copy)
                        e.then_inc(sem("x2"), 1) if gr == 0 else free(e, g)
                elif c in (C_VS, C_VW):
                    br = 0 if c == C_VS else 1
                    copy_out(zv[:, br, :], ps[:, bank(g), :], g)
                elif C_Q <= c < 512:
                    copy_out(qT[:, c // P, :], ps[:, bank(g), :], g)
                    if i == 6:
                        act.wait_ge(sem("vt_t"), 1)
                        for br in range(2):
                            A(vnat[:, :, br, :], ps[:, 2 + br, :].rearrange("p (t n) -> p t n", t=TT), ACT.Copy)
                elif c >= C_QD:
                    j = i - 10
                    if j == 0:
                        act.wait_ge(sem("cmp_free"), 3)
                    copy_out(zl[:, j, :], ps[:, bank(g), :], g)
                if i == 4:
                    table_for(ACT.Silu)
                    for w in range(2):
                        act.wait_ge(sem("p_used"), 4 * (w + 1))
                        for half in range(2):
                            for gr in range(2):
                                A(hid[:, w, half, gr, 0:NCMP], ps[:, 2 + half, NCMP * gr:NCMP * gr + NCMP],
                                  ACT.Silu).then_inc(sem("hid"), 1)
                    act.wait_ge(sem("cmp_t"), 1)
                    A(kcT[:].rearrange("p g n -> p (g n)"), ps[:, 4, 0:62], ACT.Copy).then_inc(sem("cmp_free"), 1)
            nxt(U_TAIL)
            table_for(ACT.Sigmoid)
            act.wait_ge(sem("tile"), G_A1 + 16)
            A(zg[0:24, :], ps[0:24, bank(15), :], ACT.Sigmoid).then_inc(sem("zg"), 1)
            freed(act, 13)
            freed(act, 14)
            norm_squares("ncq", 384)
            norm_hi("ncq")
            act.wait_ge(sem("gate_t"), 1)
            for h in range(HEADS):
                u, g = U_UQ + h // 2, G_UQ + h
                if h % 2 == 0:
                    nxt(u)
                copy_out(qm[0:64, h, :], ps[0:64, bank(g), :], g, last=False).then_inc(sem("qm"), 1)
                if h == 0:
                    norm_squares("nckv", 256)
                    norm_hi("nckv")
            nxt(U_UK)
            for i in range(4):
                g = G_UK + i
                if i == 0:
                    act.wait_ge(sem("nckv_lo"), since("nckv_lo", 2))
                copy_out(km[0:64, 2 * i, :], ps[0:64, bank(g), :], g, last=False)
                free(A(km[0:64, 2 * i + 1, :], ps[64:128, bank(g), :], ACT.Copy), g)
            nxt(U_UV)
            for t in range(TT):
                g = G_UV + t
                copy_out(vm[:, t, :], ps[:, bank(g), :], g)
            table_for(ACT.Exp)
            act.wait_ge(sem("cs"), 1)
            A(cp[:, :, 0:NCMP], cs[:, :, :], ACT.Exp, scale=DH ** -0.5).then_inc(sem("ce"), 1)
            act.wait_ge(sem("cp_t"), 1)
            A(cpt[:, 0:4, :].rearrange("p b n -> p (b n)"), ps[:, 4, :], ACT.Copy).then_inc(sem("cpt"), 1)
            act.wait_ge(sem("oc_t"), 1)
            A(onsa[:, 0, :], ps[:, 6, :], ACT.Copy)
            A(onsa[:, 1, :], ps[:, 7, :], ACT.Copy).then_inc(sem("oc_ev"), 1)
            attention("nsa")
            attention("mla")
            table_for(ACT.Sigmoid)
            for i in range(8):
                act.wait_ge(sem("ot_t"), i + 1)
                A(othi[:, i, :], ps[:, 4 + i % 2, :], ACT.Copy).then_inc(sem("ot_hi"), 1)
            for n in range(KD):
                for j in range(2):
                    u, g = U_Y + 3 * n + j, G_Y + 4 * n + j
                    nxt(u)
                    act.wait_ge(sem("tile"), g + 1)
                    if n >= 1:
                        freed(act, g - 2)
                    free(A(sg[:, j, :], ps[:, bank(g), :], ACT.Sigmoid), g)
                nxt(U_Y + 3 * n + 2)
                act.wait_ge(sem("y"), n + 1)
                A(yhi[:, n, :], ym[:, 2, :], ACT.Copy).then_inc(sem("y_hi"), 1)

            def residual_hi(u0, g0, nm):
                for k in range(KD):
                    split_hi(u0 + k + AHEAD)
                    freed(act, g0 + k)
                    norm_square(nm, k)
                norm_root(nm, D)
                norm_hi(nm)

            def hi_loop(u0, g0, n, evac):
                with loop(act, n // RING) as i:
                    for j in range(RING):
                        split_hi_turn(u0 + j + AHEAD, i, "tile", g0 + RING * i + j)
                        evac(i, j)
            residual_hi(U_OUT, G_OUT, "n2")

            done = 0
            for qq, part in enumerate(FC1_PARTS):
                if qq >= 1:
                    ssm_out(qq - 1)

                def relu(i, j):
                    g = G_FC1 + j
                    act.wait_ge(sem("tile"), G_FC1 + done + RING * i + j + 1)
                    act.wait_ge(sem("ff"), done + RING * i + j + 1)
                    free(A(rb[:, j % 2, :], ps[:, bank(g), :], ACT.Relu), g)
                hi_loop(U_FC1 + done, G_FC1 + done, part, relu)
                done += part
            act.wait_ge(sem("w1_out"), 128)
            act.wait_ge(sem("w2_out"), 128)
            act.wait_ge(sem("kk_out"), 64)

            def f_hi(nm, j, idx, counted):
                if counted:
                    act.wait_ge(sem(nm + "_used"), since(nm + "_used", idx - 1))
                A(fhi[:, j % 2, :], ff[:, idx, :] if isinstance(idx, int) else ff[:, bass.ds(idx, 1), :].rearrange("p a t -> p (a t)"),
                  ACT.Copy).then_inc(sem(nm + "_hi"), 1)

            def rows_hi(u0, n, nm):
                for j in range(2):
                    f_hi(nm, j, j, False)
                    split_hi(u0 + j + AHEAD)
                turns = (n - 4) // 4
                with loop(act, turns) as i:
                    for j in range(4):
                        f_hi(nm, j, 4 * i + 2 + j, True)
                        split_hi_turn(u0 + 2 + j + AHEAD, i, nm + "_used", 4 * i + 2 + j)
                for j in range(2 + 4 * turns, n):
                    f_hi(nm, j, j, True)
                    if u0 + j + AHEAD < U_END and j < n - 1:
                        split_hi(u0 + j + AHEAD)
            act.wait_ge(sem("ff"), NF1 + 2)
            rows_hi(U_FC2, NF1, "f1")
            for k in range(KD):
                act.wait_ge(sem("fc2_evac"), k + 1)
                A(sq3[:, k, :], xT[:, k, :], ACT.Square).then_inc(sem("n3_sq"), 1)
            table_for(ACT.Sqrt)
            act.wait_ge(sem("n3_ms"), 1)
            A(stat[:, 1, :], stat[:, 6, :], ACT.Sqrt, scale=1.0 / D, bias=eps[:, 1:2]).then_inc(sem("n3_rt"), 1)
            A(stat[:, 3, :], ps[:, 0, 0:4], ACT.Sqrt, scale=1.0 / D, bias=eps[:, 0:1]).then_inc(sem("xf_rt"), 1)
            split_hi(U_IN2 + AHEAD - 1)
            norm_hi("n3")
            for i in range(12):
                u, g = U_IN2 + i, G_IN2 + i
                nxt(u)
                if i < 4:
                    act.wait_ge(sem("tile"), g + 1)
                    free(A(uT[:, i, :, :].rearrange("p j c -> p c j"), ps[:, bank(g), :].rearrange("p (c j) -> p c j", j=SSM_L),
                           ACT.Copy), g)
                else:
                    copy_out((q2, k2)[(i - 4) // 4][:, i % 4, :], ps[:, bank(g), :], g)
                if i == 8:
                    act.wait_ge(sem("s_done"), 1)
                    for c in range(2):
                        for half in range(2):
                            A((sA, sB)[c][:, 8 * half:8 * half + 8, :].rearrange("p q c -> p (q c)"), ps[:, 2 + 2 * c + half, :],
                              ACT.Copy).then_inc(sem("s_ev"), 1)
            for i in range(4):
                nxt(U_V2 + i)
            act.wait_ge(sem("v2_t"), 4)
            for t in range(TT):
                A(v2[:, t, :], ps[:, 2 + t, :], ACT.Copy).then_inc(sem("v2_ev"), 1)
            for m in range(4):
                act.wait_ge(sem("ssm_y"), 1)
                A(yg[:, 16 * (m % 2) + m // 2:16 * (m % 2) + 16:2, :], ps[:, 2 + m, :].rearrange("p (q c) -> p q c", q=8),
                  ACT.Copy).then_inc(sem("yg_ev"), 1)
            table_for(ACT.Exp)
            attention("chk")
            table_for(ACT.Gelu_apprx_tanh)
            for m in range(4):
                act.wait_ge(sem("yk"), m + 1)
                A(ygel[:, m, :].rearrange("p (c j) -> p c j", j=SSM_L), yssm[:, m, :, :].rearrange("p j c -> p c j"),
                  ACT.Gelu_apprx_tanh).then_inc(sem("gel"), 1)
            for m in range(4):
                act.wait_ge(sem("gel"), m + 1)
                A(ghi[:, m, :], ygel[:, m, :], ACT.Copy).then_inc(sem("g_hi"), 1)
            act.wait_ge(sem("chk_o"), since("chk_o", HEADS))
            for t in range(TT):
                A(hb[:, t % 2, :], yatt[:, t, :], ACT.Square, accum_out=stat[:, 2, t:t + 1]).then_inc(sem("row_sq"), 1)
                act.wait_ge(sem("row_sq"), t + 1)
            table_for(ACT.Sqrt)
            act.wait_ge(sem("row_ms"), 1)
            A(stat[:, 4, :], stat[:, 3, :], ACT.Sqrt).then_inc(sem("row_rt"), 1)
            for i in range(4):
                g = G_GLU + i
                if i % 2 == 0:
                    nxt(U_GLU + i // 2)
                act.wait_ge(sem("tile"), g + 1)
                free(A(ysg[:, i, :], ps[:, bank(g), :], ACT.Sigmoid, bias=col("ssm_b_glu_2", i)), g)
                if i % 2 == 1:
                    for m in (i - 1, i):
                        act.wait_ge(sem("ya_hb"), m + 1)
                        A(hhi[:, 4 + m, :], hb[:, m % 2, :], ACT.Copy).then_inc(sem("ya_hi"), 1)
            norm_squares("nssm", 512, lambda k: act.wait_ge(sem("ysg"), k + 1))
            norm_hi("nssm")
            residual_hi(U_OUT2, G_OUT2, "n4")
            for i in range(8):
                act.wait_ge(sem("xn_t"), i + 1)
                A(xn[:, i // 2, 512 * (i % 2):512 * (i % 2) + 512], ps[:, 2 + i % 4, :], ACT.Copy).then_inc(sem("xn_ev"), 1)

            def silu(i, j):
                if j % 2 == 0:
                    g = G_GU + j
                    act.wait_ge(sem("tile"), G_GU + RING * i + j + 1)
                    freed(act, G_GU + j + 1 - RING, i)
                    free(A(rb[:, j // 2, :], ps[:, bank(g), :], ACT.Silu), g)
            table_for(ACT.Silu)
            hi_loop(U_GU, G_GU, 2 * NF2, silu)
            freed(act, G_GU + 2 * NF2 - 1)
            rows_hi(U_DN, NF2, "f2")
            for t in range(TT):
                act.wait_ge(sem("xo"), 2 * t + 2)
                A(ff[:, 2 * (t % 2):2 * (t % 2) + 2, :].rearrange("p a b -> p (a b)"), xn[:, t, :], ACT.Square,
                  accum_out=stat[:, 5, t:t + 1]).then_inc(sem("row_sq"), 1)
                act.wait_ge(sem("row_ms"), 1 + t + 1)
                A(stat[:, 6, t:t + 1], stat[:, 7, t:t + 1], ACT.Sqrt).then_inc(sem("row_rt"), 1)

        @block.vector
        def _(dve):
            chain = [0]

            def link(i):
                chain[0] += 1
                i.then_inc(sem("dve_chain"), 1)
                dve.wait_ge(sem("dve_chain"), chain[0])

            TTo, TS, STT, CP = dve.tensor_tensor, dve.tensor_scalar, dve.scalar_tensor_tensor, dve.tensor_copy

            def split_lo(u):
                dve.wait_ge(sem("w_hi"), u + 1)
                TTo(out=wlo[:, slot(u), :], in0=wraw[:, slot(u), :], in1=whi[:, slot(u), :].bitcast(F32),
                    op=ALU.subtract).then_inc(sem("w_lo"), 1)

            def nxt(u):
                if u + AHEAD < U_END:
                    split_lo(u + AHEAD)

            def norm_add(nm, k):
                buf = NORM[nm][2]
                if k == 0:
                    return
                dve.wait_ge(sem(nm + "_sq"), since(nm + "_sq", k + 1))
                if k >= 2:
                    dve.wait_ge(sem(nm + "_ac"), since(nm + "_ac", k))
                TTo(out=hb[:, 0, :], in0=buf[:, 0, :] if k == 1 else hb[:, 0, :], in1=buf[:, k % 3, :], op=ALU.add
                    ).then_inc(sem(nm + "_ac"), 2 if k == 1 else 1)

            def norm_adds(nm):
                for k in range(NORM[nm][1]):
                    norm_add(nm, k)

            def diagonal(rows):
                return TTo(out=diag.rearrange("p (t n) -> p t n", t=TT), in0=ident[:, :].unsqueeze(1).to_broadcast([P, TT, P]),
                           in1=rows.unsqueeze(2).to_broadcast([P, TT, P]), op=ALU.mult)

            def norm_inverse(nm):
                dve.wait_ge(sem(nm + "_rt"), since(nm + "_rt", 1))
                link(dve.reciprocal(stat[:, 0, :], stat[:, 1, :]))
                diagonal(stat[:, 0, :]).then_inc(sem(nm + "_dg"), 1)

            def norm_apply(nm):
                src, n, _ = NORM[nm]
                mul, add, hi, lo = AFTER[nm]
                dve.wait_ge(sem(nm + "_r"), since(nm + "_r", 1))
                for k in range(n + 1):
                    if k < n:
                        if k >= 2:
                            dve.wait_ge(sem(nm + "_lo"), since(nm + "_lo", k - 1))
                        STT(out=hb[:, k % 2, :], in0=src(k), scalar=mul(k), in1=ps[:, 7, :], op0=ALU.mult, op1=ALU.mult
                            ).then_inc(sem(nm + "_h"), 1)
                    if k >= 1:
                        dve.wait_ge(sem(nm + "_hi"), since(nm + "_hi", k))
                        if add is None:
                            e = TTo(out=lo[:, k - 1, :], in0=hb[:, (k - 1) % 2, :], in1=hi[:, k - 1, :].bitcast(F32), op=ALU.subtract)
                        else:
                            e = STT(out=lo[:, k - 1, :], in0=hb[:, (k - 1) % 2, :], scalar=add(k - 1), in1=hi[:, k - 1, :].bitcast(F32),
                                    op0=ALU.add, op1=ALU.subtract)
                        e.then_inc(sem(nm + "_lo"), 1)
                dve.wait_ge(sem(nm + "_lo"), since(nm + "_lo", n))

            def attention(nm):
                heads, _, tb = ATT[nm]
                N = 4 * len(heads)
                for s in range(N + 4):
                    if nm == "chk" and s == 28:
                        dve.wait_ge(sem("y_in"), 16 * 32)
                        for m in range(4):
                            STT(out=yssm[:, m].rearrange("p j c -> p (j c)"), in0=uT[:, m].rearrange("p j c -> p (j c)"),
                                scalar=col("ssm_d_2", m), in1=yssm[:, m].rearrange("p j c -> p (j c)"),
                                op0=ALU.mult, op1=ALU.add).then_inc(sem("yk"), 1)
                    if nm == "nsa" and s < 64:
                        part, k, half = s // 16, s // 2 % 8, s % 2
                        dve.wait_ge(sem(f"ada_in{s % 2}"), 16 * (2 + s // 2 + 1))
                        if k == 0:
                            if part:
                                dve.wait_ge(sem("ada2_t"), part)
                            e = TS(ada2[:, half, :], aring2[:, half, :], col("c", k), None, ALU.mult)
                        else:
                            dve.wait_ge(sem("ada2_used"), s - 1)
                            e = STT(out=ada2[:, half, :], in0=aring2[:, half, :], scalar=col("c", k), in1=ada2[:, half, :],
                                    op0=ALU.mult, op1=ALU.add)
                        e.then_inc(sem("ada2_used"), 1)
                    if s < N:
                        hd, b = heads[s // 4], s % 4
                        w = P * (b + 1)
                        if hd["rescale"] and b == 0:
                            link(TS(bias[:].rearrange("p h n -> p (h n)"), bias[:].rearrange("p h n -> p (h n)"), 1.0 / 16.0, None, ALU.mult))
                        dve.wait_ge(sem(nm + "_qk"), since(nm + "_qk", s + 1))
                        if s >= 4:
                            dve.wait_ge(sem(nm + "_p"), since(nm + "_p", s - 3))
                        dve.tensor_tensor_reduce(out=ps[:, score_bank(s), 0:w], in0=ps[:, score_bank(s), 0:w], in1=hd["bias"][:, T - w:T],
                                                 scale=-hd["scale"], scalar=3e38, op0=ALU.add, op1=ALU.min,
                                                 accum_out=smax[:, s % 4:s % 4 + 1]).then_inc(sem(nm + "_s"), 1)
                    r = s - 2
                    if 0 <= r < N and turned(nm, r)[0] == nm + "_ptd":
                        w = P * (r % 4 + 1)
                        dve.wait_ge(sem(nm + "_t"), since(nm + "_t", r + 1))
                        if r >= 4:
                            dve.wait_ge(sem(nm + "_pv"), since(nm + "_pv", r - 3))
                        CP(tb[:, r % 4, 0:w], ps[:, 4 + r % 2, 0:w]).then_inc(sem(nm + "_ptd"), 1)
                    r = s - 4
                    if r >= 0 and r % 4 == 3:
                        finish(nm, heads, r // 4)

            def finish(nm, heads, i):
                hd = heads[i]
                dve.wait_ge(sem(nm + "_p"), since(nm + "_p", 4 * i + 4))
                dve.wait_ge(sem(nm + "_pv"), since(nm + "_pv", 4 * i + 4))
                link(dve.reciprocal(rinv[:, :], rsum[:, i % 2, :]))
                if hd["gate"] is not None:
                    link(TTo(out=rinv[:, :], in0=rinv[:, :], in1=hd["gate"], op=ALU.mult))
                pso = ps[:, 6 + i % 2, 0:4 * DH].rearrange("p (b d) -> p b d", b=4)
                rb_ = rinv[:, :].unsqueeze(2).to_broadcast([P, 4, DH])
                dst = hd["o"][:, :, DH * hd["h"]:DH * hd["h"] + DH]
                if hd["gate"] is None:
                    e = TTo(out=dst, in0=pso, in1=rb_, op=ALU.mult)
                else:
                    t_ = hb[:, 0, 0:4 * DH].rearrange("p (b d) -> p b d", b=4)
                    link(TTo(out=t_, in0=pso, in1=rb_, op=ALU.mult))
                    e = TTo(out=dst, in0=dst, in1=t_, op=ALU.add)
                e.then_inc(sem(nm + "_o"), 1)
                dve.wait_ge(sem(nm + "_o"), since(nm + "_o", i + 1))

            dve.memset(ones[:], 1.0).then_inc(sem("ones_ok"), 1)
            dve.memset(eps[:, 0:1], EPS)
            dve.memset(eps[:, 1:2], EPS * EPS).then_inc(sem("ones_ok"), 1)
            dve.sem_inc(sem("ff"), 2)

            for k in range(1, KD, 2):
                dve.wait_ge(sem("xt_t"), k + 1)
                CP(xT[:, k, :], ps[:, 3, :]).then_inc(sem("xt_ev2"), 1)
            dve.wait_ge(sem("vec_t"), 1)
            CP(vcol[:, :], ps[:, 4, 0:NV + 32]).then_inc(sem("vec_ok"), 1)
            dve.wait_ge(sem("vec_ok"), 1)
            gf = vcol[:, VROWS["g_final"][0]:VROWS["g_final"][0] + KD]
            TTo(out=gsq[:], in0=gf, in1=gf, op=ALU.mult)
            TTo(out=gmix2[:], in0=gf, in1=vcol[:, VROWS["norm_mix_g_2"][0]:VROWS["norm_mix_g_2"][0] + KD], op=ALU.mult)
            for k in range(KD):
                dve.wait_ge(sem(f"ada_in{k % 4}"), 16 * (k // 4 + 1))
                if k == 0:
                    e = TS(ada1[:, :], aring[:, k % 4, 0:D], col("c", k), None, ALU.mult)
                else:
                    dve.wait_ge(sem("ada_used"), k)
                    e = STT(out=ada1[:, :], in0=aring[:, k % 4, 0:D], scalar=col("c", k), in1=ada1[:, :],
                            op0=ALU.mult, op1=ALU.add)
                e.then_inc(sem("ada_used"), 1)
                if k < 4:
                    norm_add("n1", 2 * k)
                    norm_add("n1", 2 * k + 1)
                if k == 5:
                    norm_inverse("n1")
            split_lo(0)
            split_lo(1)
            dve.wait_ge(sem("ada_t"), 1)
            dve.wait_ge(sem("ada_pe"), KD)
            link(TTo(out=modc[:, 0:8], in0=ps[:, 5, 0:8], in1=vcol[:, 0:8], op=ALU.add))
            link(TTo(out=modc[:, 8:16], in0=ps[:, 4, 0:8], in1=vcol[:, 8:16], op=ALU.add))
            STT(out=gain[:, 0, :], in0=modc[:, 8:16], scalar=1.0, in1=vcol[:, VROWS["g_mix"][0]:VROWS["g_mix"][0] + 8],
                op0=ALU.add, op1=ALU.mult).then_inc(sem("modc"), 1)
            dve.wait_ge(sem("modc"), 1)
            norm_apply("n1")
            split_lo(2)
            dve.wait_ge(sem("rel_in"), 16)
            link(TS(rel[0:8, 383:640], rel[0:8, 383:640], DH ** 0.5, None, ALU.mult))
            link(dve.memset(rel[0:8, 0:383], 0.0))
            TS(rel[0:8, 0:383], rel[0:8, 0:383], rel[0:8, 383:384], None, ALU.add).then_inc(sem("rel_ok"), 1)

            def parameters():
                dve.wait_ge(sem("par_t"), 1)
                CP(apar[:].rearrange("p a q -> p (a q)"), ps[:, 2, 0:112]).then_inc(sem("par_ev"), 1)
                for c in range(2):
                    for r in range(2):
                        e = CP(ctp[64 * r:64 * r + 64, c, :, :], ps[64 * r:64 * r + 64, (3, 6)[c], :].rearrange(
                            "p (q r h) -> p q r h", r=2, h=16)[:, :, r, :])
                e.then_inc(sem("par_ev"), 1)
                dve.wait_ge(sem("par_ev"), 1)
                CP(ssmc[:], apar[:, 4:7, :]).then_inc(sem("par_ev"), 1)

            def compress_in(w):
                dve.wait_ge(sem("x2"), 3 * (w + 1))
                freed(dve, G_A1 + w)
                for h in range(2):
                    src = x2[:, w, :, 16 * h:16 * h + 496].rearrange("p g (n b l) -> p g n b l", b=8, l=2)[:, :, :, :, 0]
                    for gr in range(2):
                        dst = flat[:, w, 8 * h:8 * h + 8, NCMP * gr:NCMP * gr + NCMP].rearrange("p b n -> p n b")
                        pe_ = vcol[:, NV + 16 * w + 8 * h:NV + 16 * w + 8 * h + 8].unsqueeze(1).to_broadcast([P, NCMP, 8])
                        TTo(out=dst, in0=src[:, gr], in1=pe_, op=ALU.add).then_inc(sem("flat_"), 1)
                dve.wait_ge(sem("flat_"), 4 * (w + 1))
                dve.sem_inc(sem("flat"), 1)

            for i in range(len(A1_COLS)):
                u, g, c = U_A1 + i, G_A1 + i, A1_COLS[i]
                nxt(u)
                if c in (C_KC, C_VC):
                    compress_in(i)
                elif c in (C_KS, C_KW):
                    br = 0 if c == C_KS else 1
                    dve.wait_ge(sem("tile"), g + 1)
                    for gr in range(2):
                        for half in range(2):
                            e = CP(kdup[64 * half:64 * half + 64, br, gr, :], ps[64 * gr:64 * gr + 64, bank(g), :])
                    free(e, g)
                if i == 4:
                    dve.memset(hidr[:, :, :, :, 31:32], 0.0).then_inc(sem("hidr"), 1)
                    dve.wait_ge(sem("hid"), 8)
                    for half in range(2):
                        for gr in range(2):
                            e = CP(hidr[:, half, gr, :, 0:NCMP], hid[:, 1, half, gr, 0:NCMP].unsqueeze(1).to_broadcast([P, 4, NCMP]))
                    e.then_inc(sem("hidr"), 1)
                    link(dve.memset(vblk[:], 0.0))
                    dve.wait_ge(sem("cmp_t"), 1)
                    for h in range(4):
                        e = CP(vblk[32 * h:32 * h + 32, :, h, :], ps[32 * h:32 * h + 32, 5, 0:2 * DH].rearrange("p (g d) -> p g d", g=2))
                    e.then_inc(sem("cmp_free"), 2)
            nxt(U_TAIL)
            dve.wait_ge(sem("rope_in"), 16)
            dve.wait_ge(sem("tile"), G_A1 + 16)
            TTo(out=krot[64:96, :], in0=ps[64:96, bank(15), :], in1=rope[64:96, :], op=ALU.mult).then_inc(sem("krot"), 1)
            TTo(out=hb[64:96, 1, :], in0=ps[96:128, bank(15), :], in1=rope[96:128, :], op=ALU.mult).then_inc(sem("krot"), 1)
            dve.wait_ge(sem("krot"), 2)
            TTo(out=krot[64:96, :], in0=krot[64:96, :], in1=hb[64:96, 1, :], op=ALU.add).then_inc(sem("krot"), 1)
            dve.wait_ge(sem("zg"), 1)
            dve.wait_ge(sem("krot"), 3)
            dve.sem_inc(sem(f"t_free{15 % 2}"), 1)
            norm_adds("ncq")
            norm_inverse("ncq")
            dve.wait_ge(sem("gate_t"), 1)
            CP(gates[:].rearrange("p t g -> p (t g)"), ps[:, 2, 0:96]).then_inc(sem("gates"), 1)
            norm_apply("ncq")
            for h in range(HEADS):
                u, g = U_UQ + h // 2, G_UQ + h
                if h % 2 == 0:
                    nxt(u)
                if h == 0:
                    norm_adds("nckv")
                    norm_inverse("nckv")
                    norm_apply("nckv")
                dve.wait_ge(sem("tile"), g + 1)
                link(TTo(out=hb[64:96, 0, :], in0=ps[64:96, bank(g), :], in1=rope[64:96, :], op=ALU.mult))
                link(TTo(out=hb[64:96, 1, :], in0=ps[96:128, bank(g), :], in1=rope[96:128, :], op=ALU.mult))
                dve.wait_ge(sem("qm"), h + 1)
                free(TTo(out=qm[64:96, h, :], in0=hb[64:96, 0, :], in1=hb[64:96, 1, :], op=ALU.add), g)
                freed(dve, g)
            nxt(U_UK)
            nxt(U_UV)
            freed(dve, G_Y - 2)
            freed(dve, G_Y - 1)
            dve.sem_inc(sem("ukv_done"), 1)
            dve.wait_ge(sem("cs_t"), 1)
            dve.wait_ge(sem("cbias_in"), 16)
            for half in range(2):
                own = [x[:].rearrange("p (i r) n -> p i r n", r=2)[:, :, half, :] for x in (cs, cbias)]
                link(TTo(out=own[0], in0=ps[:, 2 + half, :].rearrange("p (i n) -> p i n", n=32)[:, :, 0:NCMP],
                         in1=own[1], op=ALU.add))
            link(dve.tensor_reduce(out=cst[:, 0, :], in_=cs[:], op=ALU.max, axis=AX.X))
            link(TS(cst[:, 0, :], cst[:, 0, :], -1e25, None, ALU.max))
            link(dve.memset(cp[:, :, NCMP:32], 0.0))
            TTo(out=cs[:], in0=cs[:], in1=cst[:, 0, :].unsqueeze(2).to_broadcast([P, 32, NCMP]), op=ALU.subtract).then_inc(sem("cs"), 1)
            dve.wait_ge(sem("ce"), 1)
            link(dve.tensor_reduce(out=cst[:, 1, :], in_=cp[:, :, 0:NCMP], op=ALU.add, axis=AX.X))
            link(TS(cst[:, 1, :], cst[:, 1, :], 1e-30, None, ALU.max))
            link(dve.reciprocal(cst[:, 2, :], cst[:, 1, :]))
            link(TTo(out=cst[:, 3, :].rearrange("p (b h) -> p b h", b=TT), in0=cst[:, 2, :].rearrange("p (b h) -> p b h", b=TT),
                     in1=gates[:, :, 0:8], op=ALU.mult))
            TTo(out=cp[:, :, 0:NCMP], in0=cp[:, :, 0:NCMP], in1=cst[:, 3, :].unsqueeze(2).to_broadcast([P, 32, NCMP]),
                op=ALU.mult).then_inc(sem("cp"), 1)
            dve.wait_ge(sem("cp_t"), 1)
            CP(cpt[:, 4:8, :].rearrange("p b n -> p (b n)"), ps[:, 5, :]).then_inc(sem("cpt"), 1)
            dve.wait_ge(sem("oc_t"), 1)
            CP(onsa[:, 2, :], ps[:, 2, :])
            CP(onsa[:, 3, :], ps[:, 3, :]).then_inc(sem("oc_ev"), 1)
            dve.wait_ge(sem("oc_ev"), 2)
            dve.wait_ge(sem("bias_in"), 16)
            attention("nsa")
            dve.wait_ge(sem("ada2_t"), 4)
            link(TTo(out=modc[:, 16:48], in0=ps[:, 0, 0:32], in1=vcol[:, 16:48], op=ALU.add))
            STT(out=gain[:, 1, :], in0=modc[:, 32:40], scalar=1.0, in1=vcol[:, VROWS["g_mlp"][0]:VROWS["g_mlp"][0] + 8],
                op0=ALU.add, op1=ALU.mult).then_inc(sem("modc"), 1)
            dve.wait_ge(sem("cmask_in"), 16)
            attention("mla")
            for i in range(8):
                dve.wait_ge(sem("ot_hi"), i + 1)
                TTo(out=otlo[:, i, :], in0=ps[:, 4 + i % 2, :], in1=othi[:, i, :].bitcast(F32), op=ALU.subtract).then_inc(sem("ot_lo"), 1)
            for n in range(KD):
                u = U_Y + 3 * n
                if n == 1:
                    dve.wait_ge(sem("lam_sq"), 1)
                    dve.reciprocal(pv[0:16, 17, :], pv[0:16, 17, :]).then_inc(sem("lam_inv"), 1)
                if n == 7:
                    parameters()
                for j in range(3):
                    nxt(u + j)
                for j in range(2):
                    g = G_Y + 4 * n + 2 + j
                    dve.wait_ge(sem("tile"), g + 1)
                    free(TTo(out=ym[:, j, :], in0=ps[:, bank(g), :], in1=sg[:, j, :], op=ALU.mult), g)
                    freed(dve, g)
                if n >= 1:
                    dve.wait_ge(sem("y_lo"), n)
                TTo(out=ym[:, 2, :], in0=ym[:, 0, :], in1=ym[:, 1, :], op=ALU.add).then_inc(sem("y"), 1)
                dve.wait_ge(sem("y_hi"), n + 1)
                TTo(out=ylo[:, n, :], in0=ym[:, 2, :], in1=yhi[:, n, :].bitcast(F32), op=ALU.subtract).then_inc(sem("y_lo"), 1)

            def lo_loop(u0, n, evac):
                with loop(dve, n // RING) as i:
                    for j in range(RING):
                        dve.wait_ge(sem("w_hi"), u0 + RING * i + j + AHEAD + 1)
                        s = slot(u0 + j + AHEAD)
                        TTo(out=wlo[:, s, :], in0=wraw[:, s, :], in1=whi[:, s, :].bitcast(F32), op=ALU.subtract).then_inc(sem("w_lo"), 1)
                        evac(i, j)

            def at1(t, idx):
                return t[:, bass.ds(idx, 1), :].rearrange("p a t -> p (a t)")

            def residual_lo(u0, g0, nm, scale):
                for k in range(KD):
                    split_lo(u0 + k + AHEAD)
                    g = g0 + k
                    dve.wait_ge(sem("tile"), g + 1)
                    if scale is None:
                        free(TTo(out=xT[:, k, :], in0=xT[:, k, :], in1=ps[:, bank(g), :], op=ALU.add), g)
                    else:
                        free(STT(out=xT[:, k, :], in0=ps[:, bank(g), :], scalar=mod(scale, k), in1=xT[:, k, :],
                                 op0=ALU.mult, op1=ALU.add), g)
                    if k >= 1:
                        norm_add(nm, k - 1)
                norm_add(nm, KD - 1)
                norm_inverse(nm)
                norm_apply(nm)
            residual_lo(U_OUT, G_OUT, "n2", 2)

            def square(i, j):
                freed(dve, G_FC1 + j, i)
                TTo(out=at1(ff, RING * i + j), in0=rb[:, j % 2, :], in1=rb[:, j % 2, :], op=ALU.mult).then_inc(sem("ff"), 1)
            lo_loop(U_FC1, NF1, square)

            def f_lo(nm, j, idx):
                dve.wait_ge(sem(nm + "_hi"), since(nm + "_hi", idx + 1))
                TTo(out=flo[:, j % 2, :], in0=ff[:, idx, :] if isinstance(idx, int) else at1(ff, idx),
                    in1=fhi[:, j % 2, :].bitcast(F32), op=ALU.subtract).then_inc(sem(nm + "_lo"), 1)

            def rows_lo(u0, n, nm):
                for j in range(2):
                    f_lo(nm, j, j)
                    split_lo(u0 + j + AHEAD)
                turns = (n - 4) // 4
                with loop(dve, turns) as i:
                    for j in range(4):
                        f_lo(nm, j, 4 * i + 2 + j)
                        dve.wait_ge(sem("w_hi"), u0 + 2 + RING * i + j + AHEAD + 1)
                        s = slot(u0 + 2 + j + AHEAD)
                        TTo(out=wlo[:, s, :], in0=wraw[:, s, :], in1=whi[:, s, :].bitcast(F32), op=ALU.subtract).then_inc(sem("w_lo"), 1)
                for j in range(2 + 4 * turns, n):
                    f_lo(nm, j, j)
                    if u0 + j + AHEAD < U_END and j < n - 1:
                        split_lo(u0 + j + AHEAD)
            rows_lo(U_FC2, NF1, "f1")
            def add3(k):
                dve.wait_ge(sem("n3_sq"), since("n3_sq", k + 1))
                if k == 0:
                    e = TS(hb[:, 0, :], sq3[:, 0, :], gsq[:, 0:1], None, ALU.mult)
                else:
                    dve.wait_ge(sem("n3_ac"), since("n3_ac", k))
                    e = STT(out=hb[:, 0, :], in0=sq3[:, k, :], scalar=gsq[:, k:k + 1], in1=hb[:, 0, :], op0=ALU.mult, op1=ALU.add)
                e.then_inc(sem("n3_ac"), 1)
            for n in range(KD):
                dve.wait_ge(sem("f1_bank"), n + 1)
                STT(out=xT[:, n, :], in0=ps[:, n, :], scalar=mod(5, n), in1=xT[:, n, :], op0=ALU.mult, op1=ALU.add).then_inc(sem("fc2_evac"), 1)
                if n >= 1:
                    add3(n - 1)
            add3(KD - 1)
            dve.wait_ge(sem("n3_st"), since("n3_st", 1))
            dve.wait_ge(sem("xf_st"), 1)
            link(CP(stat[:, 5, :], ps[:, 0, 0:4]))
            STT(out=stat[:, 6, :], in0=stat[:, 5, :], scalar=EPS, in1=ps[:, 6, 0:4], op0=ALU.mult, op1=ALU.add).then_inc(sem("n3_ms"), 1)
            norm_inverse("n3")
            dve.wait_ge(sem("xf_rt"), 1)
            link(dve.reciprocal(stat[:, 4, :], stat[:, 3, :]))
            TTo(out=hb[:, 0, :].rearrange("p (t n) -> p t n", t=TT), in0=ident[:, :].unsqueeze(1).to_broadcast([P, TT, P]),
                in1=stat[:, 4, :].unsqueeze(2).to_broadcast([P, TT, P]), op=ALU.mult).then_inc(sem("xf_dg"), 1)
            dve.wait_ge(sem("xf_r"), 1)
            norm_apply("n3")
            split_lo(U_IN2 + AHEAD - 1)

            def cmul(ore, oim, xre, xim, yre, yim, t1, t2):
                link(TTo(out=t1, in0=xre, in1=yre, op=ALU.mult))
                link(TTo(out=t2, in0=xim, in1=yim, op=ALU.mult))
                link(TTo(out=ore, in0=t1, in1=t2, op=ALU.subtract))
                link(TTo(out=t1, in0=xre, in1=yim, op=ALU.mult))
                link(TTo(out=t2, in0=xim, in1=yre, op=ALU.mult))
                link(TTo(out=oim, in0=t1, in1=t2, op=ALU.add))

            def double(s, c1, t):
                link(STT(out=t, in0=c1, scalar=1.0, in1=s, op0=ALU.add, op1=ALU.mult))
                link(STT(out=c1, in0=s, scalar=-2.0, in1=s, op0=ALU.mult, op1=ALU.mult))
                link(TS(s, t, 2.0, None, ALU.mult))

            def turns_table():
                c1, s1, t = twc[:, 0, :], twc[:, 1, :], twc[:, 2, :]
                link(CP(c1, ssmc[:, 1, :]))
                link(CP(s1, ssmc[:, 2, :]))
                link(dve.memset(twr[:, :, 0:1], 1.0))
                link(dve.memset(twi[:, :, 0:1], 0.0))
                n = 1
                while n < SSM_C:
                    cc = twc[:, 3, :]
                    link(TS(cc, c1, 1.0, None, ALU.add))
                    t1, t2 = (x[:].rearrange("p q c -> p (q c)")[:, 0:16 * n].rearrange("p (q c) -> p q c", c=n) for x in (tA, tB))
                    cmul(twr[:, :, n:2 * n], twi[:, :, n:2 * n], twr[:, :, 0:n], twi[:, :, 0:n],
                         cc.unsqueeze(2).to_broadcast([P, SSM_Q, n]), s1.unsqueeze(2).to_broadcast([P, SSM_Q, n]), t1, t2)
                    n *= 2
                    if n < SSM_C:
                        double(s1, c1, t)

            W = slice(1, SSM_C)
            Y_ = slice(0, SSM_C - 1)

            def turn_back():
                link(TTo(out=tA[:, :, W], in0=sA[:, :, Y_], in1=twr[:, :, W], op=ALU.mult))
                link(TTo(out=tB[:, :, W], in0=sB[:, :, Y_], in1=twi[:, :, W], op=ALU.mult))
                link(dve.memset(vA[:, :, 0:1], 0.0))
                link(TTo(out=vA[:, :, W], in0=tA[:, :, W], in1=tB[:, :, W], op=ALU.add))
                link(TTo(out=tA[:, :, W], in0=sB[:, :, Y_], in1=twr[:, :, W], op=ALU.mult))
                link(TTo(out=tB[:, :, W], in0=sA[:, :, Y_], in1=twi[:, :, W], op=ALU.mult))
                link(dve.memset(vB[:, :, 0:1], 0.0))
                link(TTo(out=vB[:, :, W], in0=tA[:, :, W], in1=tB[:, :, W], op=ALU.subtract))

            def scan():
                link(CP(sA[:], ssmc[:, 0, :].unsqueeze(2).to_broadcast([P, SSM_Q, SSM_C])))
                link(dve.memset(sA[:, :, 0:1], 0.0))
                fl = lambda x: x[:].rearrange("p q c -> p (q c)")
                link(dve.tensor_tensor_scan(fl(tA), fl(sA), fl(vA), 0.0, ALU.mult, ALU.add))
                link(dve.tensor_tensor_scan(fl(tB), fl(sA), fl(vB), 0.0, ALU.mult, ALU.add))

            def turn_forth():
                link(TTo(out=vA[:], in0=twr[:], in1=tA[:], op=ALU.mult))
                link(TTo(out=vB[:], in0=twi[:], in1=tB[:], op=ALU.mult))
                link(TTo(out=sB[:], in0=vA[:], in1=vB[:], op=ALU.subtract))
                link(TTo(out=vA[:], in0=twr[:], in1=tB[:], op=ALU.mult))
                link(TTo(out=vB[:], in0=twi[:], in1=tA[:], op=ALU.mult))
                TTo(out=sA[:], in0=vA[:], in1=vB[:], op=ALU.add).then_inc(sem("xst"), 2)

            for i in range(12):
                u, g = U_IN2 + i, G_IN2 + i
                nxt(u)
                if i < KD:
                    STT(out=xT[:, i, :], in0=xT[:, i, :], scalar=col("g_final", i), in1=ps[:, 6, :], op0=ALU.mult, op1=ALU.mult)
                if i == 4:
                    turns_table()
                if i == 9:
                    dve.wait_ge(sem("s_ev"), 4)
                    turn_back()
                if i == 10:
                    scan()
                if i == 11:
                    turn_forth()
            for i in range(4):
                nxt(U_V2 + i)
            dve.wait_ge(sem("bias2_ok"), 1)
            attention("chk")
            for m in range(4):
                dve.wait_ge(sem("g_hi"), m + 1)
                TTo(out=glo[:, m, :], in0=ygel[:, m, :], in1=ghi[:, m, :].bitcast(F32), op=ALU.subtract).then_inc(sem("g_lo"), 1)
            dve.wait_ge(sem("row_sq"), 4)
            TS(stat[:, 3, :], stat[:, 2, :], 1.0 / 512, EPS, ALU.mult, ALU.add).then_inc(sem("row_ms"), 1)
            dve.wait_ge(sem("row_rt"), 1)
            link(dve.reciprocal(stat[:, 3, :], stat[:, 4, :]))
            for t in range(TT):
                TS(yatt[:, t, :], yatt[:, t, :], stat[:, 3, t:t + 1], None, ALU.mult).then_inc(sem("ya_n"), 1)
            for i in range(4):
                g = G_GLU + i
                if i % 2 == 0:
                    nxt(U_GLU + i // 2)
                freed(dve, g)
                TTo(out=ysg[:, i, :], in0=ysg[:, i, :], in1=ygel[:, i, :], op=ALU.mult).then_inc(sem("ysg"), 1)
                if i % 2 == 1:
                    for m in (i - 1, i):
                        dve.wait_ge(sem("ya_t"), m + 1)
                        if m >= 2:
                            dve.wait_ge(sem("ya_lo"), m - 1)
                        TS(hb[:, m % 2, :], ps[:, 4 + m % 2, :], col("norm_att_out_g_2", m), None, ALU.mult).then_inc(sem("ya_hb"), 1)
                        dve.wait_ge(sem("ya_hi"), m + 1)
                        TTo(out=hlo[:, 4 + m, :], in0=hb[:, m % 2, :], in1=hhi[:, 4 + m, :].bitcast(F32), op=ALU.subtract).then_inc(sem("ya_lo"), 1)
            dve.wait_ge(sem("ya_lo"), 4)
            norm_adds("nssm")
            norm_inverse("nssm")
            norm_apply("nssm")
            residual_lo(U_OUT2, G_OUT2, "n4", None)
            dve.sem_inc(sem("fc2b_free"), 1)

            def gate_up(i, j):
                if j % 2 == 1:
                    g = G_GU + j
                    dve.wait_ge(sem("tile"), G_GU + RING * i + j + 1)
                    freed(dve, g - 1, i)
                    free(TTo(out=at1(ff, 2 * i + j // 2), in0=rb[:, j // 2, :], in1=ps[:, bank(g), :], op=ALU.mult), g)
            lo_loop(U_GU, 2 * NF2, gate_up)
            rows_lo(U_DN, NF2, "f2")
            dve.wait_ge(sem("xn_ev"), 8)
            dve.wait_ge(sem("gfin_in"), 16)
            for t in range(TT):
                for half in range(2):
                    c = slice(512 * half, 512 * half + 512)
                    dve.wait_ge(sem("f2_bank"), 2 * t + half + 1)
                    TTo(out=xn[:, t, c], in0=xn[:, t, c], in1=ps[:, 2 * t + half, :], op=ALU.add).then_inc(sem("xo"), 1)
                dve.wait_ge(sem("row_sq"), 4 + t + 1)
                TS(stat[:, 7, t:t + 1], stat[:, 5, t:t + 1], 1.0 / D, EPS, ALU.mult, ALU.add).then_inc(sem("row_ms"), 1)
                dve.wait_ge(sem("row_rt"), 1 + t + 1)
                link(dve.reciprocal(stat[:, 4, t:t + 1], stat[:, 6, t:t + 1]))
                STT(out=xn[:, t, :], in0=xn[:, t, :], scalar=stat[:, 4, t:t + 1], in1=gfin[:, :], op0=ALU.mult, op1=ALU.mult).then_inc(sem("o_ready"), 1)


_INS = ["x", "c", "w_ada", "b_ada", "g_mix", "w_in", "pe_ck", "w_ck1", "w_ck2", "pe_cv", "w_cv1", "w_cv2", "g_cq", "w_uq",
        "g_ckv", "w_uk", "w_uv", "w_o_nsa", "w_o_mla", "w_out", "g_mlp", "w_fc1", "w_fc2", "g_final", "norm_mix_g_2",
        "w_in_2", "ssm_lam_re_2", "ssm_lam_im_2", "ssm_log_dt_2", "ssm_b_re_2", "ssm_b_im_2", "ssm_c_re_2",
        "ssm_c_im_2", "ssm_d_2", "ssm_w_glu_2", "ssm_b_glu_2", "attn_rel_bias_2", "norm_ssm_out_g_2",
        "norm_att_out_g_2", "w_out_2", "norm_ffn_g_2", "w_gate_2", "w_up_2", "w_down_2", "norm_final_g_2"]


def constants():
    f = np.float32
    p = np.arange(P)[:, None]
    j = np.arange(T)[None, :]
    dist = p - (j - (T - P))
    seen = dist >= 0
    alibi = np.stack([np.where(seen, -(8.0 * 2.0 ** -(h + 1)) * dist, NEG) for h in range(4)], axis=1)
    causal = np.where(seen, 0.0, NEG)
    block, head, n = np.meshgrid(np.arange(TT), np.arange(HEADS), np.arange(NCMP), indexing="ij")
    d = (P * block + 0)[None] + p[:, :, None, None] - (16 * n + 31)[None]
    cmp_bias = np.where(d >= 0, -(8.0 * 2.0 ** -(head + 1.0))[None] * d, NEG).reshape(P, 32, NCMP)
    ang = np.arange(T, dtype=f)[None, :] * (f(10000.0) ** (-np.arange(16, dtype=f) / f(16)))[:, None]
    cos, sin = np.cos(ang.astype(np.float64)), np.sin(ang.astype(np.float64))
    rope = np.zeros((P, T))
    rope[64:96] = np.concatenate([cos, cos])
    rope[96:128] = np.concatenate([-sin, sin])
    return {"identity": np.eye(P).astype(f), "alibi": alibi.astype(f), "causal": causal.astype(f),
            "cmp_bias": cmp_bias.astype(f), "rope_table": rope.astype(f)}


def kernel(**inputs):
    import concourse.bacc as _bacc
    from concourse.bass_utils import run_bass_kernel_spmd as _run

    nc = _bacc.Bacc("TRN2", target_bir_lowering=False, num_devices=1)
    arrays, aps = {}, {}
    given = {name: np.ascontiguousarray(inputs[name]) for name in _INS}
    given.update(constants())
    for name, v in given.items():
        arrays[f"in_{name}"] = v
        aps[name] = nc.dram_tensor(f"in_{name}", v.shape, mybir.dt.from_np(v.dtype), kind="ExternalInput").ap()
    scr = {"rel": [8, 640], "relp": [P, 8, 640], "w1": [2, P, SSM_Q, P], "w2": [2, P, SSM_Q, P], "kk": [32, SSM_Q, P],
           "u": [4, P, SSM_L, SSM_C], "y": [P, 32 * SSM_C]}
    scr = {k: nc.dram_tensor(f"scratch_{k}", v, F32, kind="Internal").ap() for k, v in scr.items()}
    out = nc.dram_tensor("out_0", [1, T, D], F32, kind="ExternalOutput").ap()
    program(nc, aps, out, scr)
    r = _run(nc, [arrays], core_ids=[0])
    return r.results[0]["out_0"]
```
